# Optimizing a Trainium2 kernel written in Bass

```python
import jax, jax.numpy as jnp
from jax import lax
import numpy as np

D_MODEL = 1024
BATCH = 1
SEQ = 512
DEPTH = 1
DEC_BATCH = 8
DEC_SEQ = 4
PAST_LEN = 2048
PAGE_SIZE = 128

HEAD_DIM = 64
RWKV_HEADS = D_MODEL // (2 * HEAD_DIM)
C_A = RWKV_HEADS * HEAD_DIM
R_DECAY = 32
R_ICLR = 32
R_GATE = 96
RW_IN = 3 * C_A + R_DECAY + R_ICLR + R_GATE
NSA_HEADS = D_MODEL // (2 * HEAD_DIM)
NSA_KV_HEADS = 2
NSA_GROUP = NSA_HEADS // NSA_KV_HEADS
C_B = NSA_HEADS * HEAD_DIM
KV_W = 2 * NSA_KV_HEADS * HEAD_DIM
CMP_LEN = 32
CMP_STRIDE = 16
CMP_RATIO = CMP_LEN // CMP_STRIDE
CMP_HIDDEN = HEAD_DIM
SEL_BLOCK = 64
N_SEL = 16
WINDOW = 512
Q_BLOCK = 64
OFF_Q = RW_IN
OFF_KVC = OFF_Q + C_B
OFF_KVS = OFF_KVC + KV_W
OFF_KVW = OFF_KVS + KV_W
OFF_NG = OFF_KVW + KV_W
OFF_MG = OFF_NG + 3 * NSA_HEADS
N_IN = OFF_MG + 2 * D_MODEL
N_GROUPS = 4
EXPERTS_PER_GROUP = 8
N_EXPERTS = N_GROUPS * EXPERTS_PER_GROUP
TOP_K = 2
D_EXPERT = D_MODEL // 2
MOE_BLOCK = 128
RMS_EPS = 1e-6
GN_EPS = 64e-5
NEG_INF = -1e30
FORCE_SCORE = 1e6

kernel_name = 'hybrid_rwkv7_nsa_hmoe_step'

F32 = jnp.float32

def rms_norm(x, g):
    xf = x.astype(F32)
    y = xf * lax.rsqrt(jnp.mean(xf * xf, axis=-1, keepdims=True) + RMS_EPS)
    return (y * g.astype(F32)).astype(x.dtype)

def masked_softmax(s, mask):
    s = jnp.where(mask, s, NEG_INF)
    e = jnp.where(mask, jnp.exp(s - jnp.max(s, axis=-1, keepdims=True)), 0.0)
    return e / jnp.maximum(jnp.sum(e, axis=-1, keepdims=True), 1e-30)

def wkv_scan(r, w, k, v, a, b, s0):
    def step(s, inp):
        r_t, w_t, k_t, v_t, a_t, b_t = inp
        sa = jnp.einsum('bhij,bhj->bhi', s, a_t)
        s = s * w_t[:, :, None, :] + sa[..., None] * b_t[:, :, None, :] + v_t[..., None] * k_t[:, :, None, :]
        return s, jnp.einsum('bhij,bhj->bhi', s, r_t)
    xs = tuple(jnp.moveaxis(t, 1, 0) for t in (r, w, k, v, a, b))
    s_fin, ys = lax.scan(step, s0, xs)
    return jnp.moveaxis(ys, 0, 1), s_fin

def rwkv_branch(z_a, shift_prev, wkv_prev, mu_shift, w0, w_decay_up, a0, w_iclr_up, w_gate_up,
                k_k, k_a, r_k, ln_x_w, ln_x_b):
    B, T, _ = z_a.shape
    zf = z_a.astype(F32)
    z_prev = jnp.concatenate([shift_prev.astype(F32)[:, None], zf[:, :-1]], axis=1)
    zm = zf + (z_prev - zf) * mu_shift.astype(F32)
    r, k, v, w_lo, a_lo, g_lo = jnp.split(
        zm, [C_A, 2 * C_A, 3 * C_A, 3 * C_A + R_DECAY, 3 * C_A + R_DECAY + R_ICLR], axis=-1)
    w_log = -jax.nn.softplus(-(w0.astype(F32) + jnp.tanh(w_lo) @ w_decay_up.astype(F32))) - 0.5
    decay = jnp.exp(-jnp.exp(w_log))
    a = jax.nn.sigmoid(a0.astype(F32) + a_lo @ w_iclr_up.astype(F32))
    g = jax.nn.sigmoid(g_lo) @ w_gate_up.astype(F32)
    heads = lambda t: t.reshape(B, T, RWKV_HEADS, HEAD_DIM)
    kk = heads(k * k_k.astype(F32))
    kk = kk / jnp.maximum(jnp.sqrt(jnp.sum(kk * kk, axis=-1, keepdims=True)), 1e-12)
    k = k * (1.0 + (a - 1.0) * k_a.astype(F32))
    r_h, k_h, v_h, a_h = heads(r), heads(k), heads(v), heads(a)
    y, wkv_new = wkv_scan(r_h, heads(decay), k_h, v_h, -kk, kk * a_h, wkv_prev.astype(F32))
    mean = jnp.mean(y, axis=-1, keepdims=True)
    var = jnp.mean(jnp.square(y - mean), axis=-1, keepdims=True)
    y = ((y - mean) * lax.rsqrt(var + GN_EPS)).reshape(B, T, C_A) * ln_x_w.astype(F32) + ln_x_b.astype(F32)
    bonus = jnp.sum(r_h * k_h * r_k.astype(F32), axis=-1, keepdims=True) * v_h
    y = (y + bonus.reshape(B, T, C_A)) * g
    return y, wkv_new.astype(wkv_prev.dtype), z_a[:, -1]

def nsa_inputs(z, q_norm, ks_norm, kw_norm):
    B, T, _ = z.shape
    kv_shape = (B, T, 2, NSA_KV_HEADS, HEAD_DIM)
    q = rms_norm(z[..., OFF_Q:OFF_KVC].reshape(B, T, NSA_HEADS, HEAD_DIM), q_norm)
    kv_c = z[..., OFF_KVC:OFF_KVS].reshape(kv_shape)
    kv_s = z[..., OFF_KVS:OFF_KVW].reshape(kv_shape)
    kv_w = z[..., OFF_KVW:OFF_NG].reshape(kv_shape)
    kv_s = jnp.stack([rms_norm(kv_s[:, :, 0], ks_norm), kv_s[:, :, 1]], axis=2)
    kv_w = jnp.stack([rms_norm(kv_w[:, :, 0], kw_norm), kv_w[:, :, 1]], axis=2)
    gates = jax.nn.sigmoid(z[..., OFF_NG:OFF_MG].astype(F32)).reshape(B, T, 3, NSA_HEADS)
    return q, kv_c, kv_s, kv_w, gates

def compress(rows, pe, w1, b1, w2):
    B, T = rows.shape[:2]
    nc = (T - CMP_LEN) // CMP_STRIDE + 1
    ch = rows[:, :(nc + CMP_RATIO - 1) * CMP_STRIDE].reshape(
        B, nc + CMP_RATIO - 1, CMP_STRIDE, NSA_KV_HEADS, HEAD_DIM)
    blocks = jnp.concatenate([ch[:, r:r + nc] for r in range(CMP_RATIO)], axis=2)
    hid = jax.nn.silu(jnp.einsum('bnlgd,ldf->bngf', blocks + pe[:, None, :], w1) + b1)
    return jnp.einsum('bngf,fd->bngd', hid, w2)

def compress_kv(kv_rows, kc_norm, pe_k, w1_k, b1_k, w2_k, pe_v, w1_v, b1_v, w2_v):
    kc = rms_norm(compress(kv_rows[:, :, 0], pe_k, w1_k, b1_k, w2_k), kc_norm)
    vc = compress(kv_rows[:, :, 1], pe_v, w1_v, b1_v, w2_v)
    return kc, vc

def nsa_core(q, q_pos, kc, vc, n_blocks, gather_sel, kw, vw, kw_pos, gates):
    B, Tq = q.shape[:2]
    nc = kc.shape[1]
    qg = q.astype(F32).reshape(B, Tq, NSA_KV_HEADS, NSA_GROUP, HEAD_DIM) * (HEAD_DIM ** -0.5)
    t = q_pos[:, None]
    c_idx = jnp.arange(nc)
    s_c = jnp.einsum('btgmd,bngd->btgmn', qg, kc.astype(F32))
    p_c = masked_softmax(s_c, (c_idx * CMP_STRIDE + CMP_LEN - 1 <= t)[None, :, None, None, :])
    o_c = jnp.einsum('btgmn,bngd->btgmd', p_c, vc.astype(F32))
    j = jnp.arange(n_blocks)
    c0 = c_idx[:, None] * CMP_STRIDE
    overlap = ((c0 < (j[None, :] + 1) * SEL_BLOCK) & (c0 + CMP_LEN > j[None, :] * SEL_BLOCK)).astype(F32)
    importance = jnp.einsum('btgmn,nj->btgj', p_c, overlap)
    cur = t // SEL_BLOCK
    valid = (j[None, :] * SEL_BLOCK <= t)[None, :, None, :]
    forced = ((j[None, :] == 0) | (j[None, :] == cur) | (j[None, :] == cur - 1))[None, :, None, :]
    score = jnp.where(valid, jnp.where(forced, FORCE_SCORE, importance), NEG_INF)
    _, idx = lax.top_k(score, min(N_SEL, n_blocks))
    k_g, v_g, pos_g = gather_sel(idx)
    s_s = jnp.einsum('btgmd,btgkd->btgmk', qg, k_g.astype(F32))
    p_s = masked_softmax(s_s, (pos_g <= q_pos[None, :, None, None])[:, :, :, None, :])
    o_s = jnp.einsum('btgmk,btgkd->btgmd', p_s, v_g.astype(F32))
    s_w = jnp.einsum('btgmd,bkgd->btgmk', qg, kw.astype(F32))
    kp = kw_pos[None, :]
    mask_w = (kp <= t) & (kp > t - WINDOW) & (kp >= 0)
    p_w = masked_softmax(s_w, mask_w[None, :, None, None, :])
    o_w = jnp.einsum('btgmk,bkgd->btgmd', p_w, vw.astype(F32))
    g = gates.reshape(B, Tq, 3, NSA_KV_HEADS, NSA_GROUP)[..., None]
    o = g[:, :, 0] * o_c + g[:, :, 1] * o_s + g[:, :, 2] * o_w
    return o.reshape(B, Tq, C_B)

def make_prompt_gather(kv_s):
    B = kv_s.shape[0]
    def gather(idx):
        pos = idx[..., None] * SEL_BLOCK + jnp.arange(SEL_BLOCK)
        bi = jnp.arange(B)[:, None, None, None, None]
        gi = jnp.arange(NSA_KV_HEADS)[None, None, :, None, None]
        k = kv_s[bi, pos, 0, gi]
        v = kv_s[bi, pos, 1, gi]
        flat = pos.shape[:3] + (-1,)
        return k.reshape(flat + (HEAD_DIM,)), v.reshape(flat + (HEAD_DIM,)), pos.reshape(flat)
    return gather

def make_paged_gather(pool, page_table, new_kv):
    DB, DS = new_kv.shape[:2]
    def gather(idx):
        pos = idx[..., None] * SEL_BLOCK + jnp.arange(SEL_BLOCK)
        bi = jnp.arange(DB)[:, None, None, None, None]
        gi = jnp.arange(NSA_KV_HEADS)[None, None, :, None, None]
        pc = jnp.minimum(pos, PAST_LEN - 1)
        page = page_table[bi, pc // PAGE_SIZE]
        off = pc % PAGE_SIZE
        npos = jnp.clip(pos - PAST_LEN, 0, DS - 1)
        past = (pos < PAST_LEN)[..., None]
        k = jnp.where(past, pool[page, off, 0, gi], new_kv[bi, npos, 0, gi])
        v = jnp.where(past, pool[page, off, 1, gi], new_kv[bi, npos, 1, gi])
        flat = pos.shape[:3] + (-1,)
        return k.reshape(flat + (HEAD_DIM,)), v.reshape(flat + (HEAD_DIM,)), pos.reshape(flat)
    return gather

def nsa_prompt(q, kc, vc, kv_s, kv_w, gates):
    B, T = q.shape[:2]
    n_blocks = T // SEL_BLOCK
    gather = make_prompt_gather(kv_s)
    kw_pad = jnp.pad(kv_w, ((0, 0), (WINDOW, 0), (0, 0), (0, 0), (0, 0)))
    def block(i):
        s0 = i * Q_BLOCK
        qb = lax.dynamic_slice_in_dim(q, s0, Q_BLOCK, axis=1)
        gb = lax.dynamic_slice_in_dim(gates, s0, Q_BLOCK, axis=1)
        wb = lax.dynamic_slice_in_dim(kw_pad, s0, WINDOW + Q_BLOCK, axis=1)
        q_pos = s0 + jnp.arange(Q_BLOCK)
        kw_pos = s0 - WINDOW + jnp.arange(WINDOW + Q_BLOCK)
        return nsa_core(qb, q_pos, kc, vc, n_blocks, gather, wb[:, :, 0], wb[:, :, 1], kw_pos, gb)
    o = lax.map(block, jnp.arange(T // Q_BLOCK))
    return o.transpose(1, 0, 2, 3).reshape(B, T, C_B)

def hier_moe(h, w_route_group, b_route_group, w_route_expert, b_route_expert, w_exp_gate, w_exp_up, w_exp_down):
    T = h.shape[0]
    g_logit = (h @ w_route_group).astype(F32) + b_route_group.astype(F32)
    g_sel = jnp.argmax(g_logit, axis=-1)
    g_w = jnp.take_along_axis(jax.nn.softmax(g_logit, axis=-1), g_sel[:, None], axis=1)
    e_logit = ((h @ w_route_expert).astype(F32) + b_route_expert.astype(F32)).reshape(T, N_GROUPS, EXPERTS_PER_GROUP)
    e_logit = jnp.take_along_axis(e_logit, g_sel[:, None, None], axis=1)[:, 0]
    top_v, top_i = lax.top_k(e_logit, TOP_K)
    wts = (jax.nn.softmax(top_v, axis=-1) * g_w).reshape(-1)
    expert = (g_sel[:, None] * EXPERTS_PER_GROUP + top_i).reshape(-1)
    tok = jnp.repeat(jnp.arange(T), TOP_K)
    n_slots = T * TOP_K
    order = jnp.argsort(expert)
    e_s, tok_s, w_s = expert[order], tok[order], wts[order]
    counts = jnp.bincount(expert, length=N_EXPERTS)
    padded = (counts + MOE_BLOCK - 1) // MOE_BLOCK * MOE_BLOCK
    p_end = jnp.cumsum(padded)
    dest = (p_end - padded)[e_s] + jnp.arange(n_slots) - (jnp.cumsum(counts) - counts)[e_s]
    n_blk = -(-n_slots // MOE_BLOCK) + N_EXPERTS
    xbuf = jnp.zeros((n_blk * MOE_BLOCK, D_MODEL), h.dtype).at[dest].set(h[tok_s])
    blk_e = jnp.minimum(jnp.searchsorted(p_end, jnp.arange(n_blk) * MOE_BLOCK, side='right'), N_EXPERTS - 1)
    def expert_block(args):
        xb, e = args
        return (jax.nn.silu(xb @ w_exp_gate[e]) * (xb @ w_exp_up[e])) @ w_exp_down[e]
    ybuf = lax.map(expert_block, (xbuf.reshape(n_blk, MOE_BLOCK, D_MODEL), blk_e)).reshape(n_blk * MOE_BLOCK, D_MODEL)
    out = jnp.zeros((T, D_MODEL), F32).at[tok_s].add(ybuf[dest].astype(F32) * w_s[:, None])
    return out.astype(h.dtype)

def merge_and_channel_mix(x, z, o_a, o_b, w_branch_a, w_branch_b, w_out, norm2, w_route_group, b_route_group,
                          w_route_expert, b_route_expert, w_exp_gate, w_exp_up, w_exp_down):
    dt = x.dtype
    B, T, _ = x.shape
    gate_a = jax.nn.sigmoid(z[..., OFF_MG:OFF_MG + D_MODEL].astype(F32))
    gate_b = jax.nn.sigmoid(z[..., OFF_MG + D_MODEL:OFF_MG + 2 * D_MODEL].astype(F32))
    merged = gate_a * (o_a.astype(dt) @ w_branch_a).astype(F32) + gate_b * (o_b.astype(dt) @ w_branch_b).astype(F32)
    x1 = x + (merged.astype(dt) @ w_out).astype(dt)
    h = rms_norm(x1, norm2).reshape(B * T, D_MODEL)
    y = hier_moe(h, w_route_group, b_route_group, w_route_expert, b_route_expert, w_exp_gate, w_exp_up, w_exp_down)
    return x1 + y.reshape(B, T, D_MODEL)

def decoder_layer(x_prompt, x_sample, cache_cmp_kv, cache_slc_kv, cache_win_kv, state_wkv, state_shift, page_table, p):
    (norm1, w_in, mu_shift, w0, w_decay_up, a0, w_iclr_up, w_gate_up, k_k, k_a, r_k, ln_x_w, ln_x_b,
     q_norm, kc_norm, ks_norm, kw_norm, cmp_pe_k, cmp_w1_k, cmp_b1_k, cmp_w2_k, cmp_pe_v, cmp_w1_v, cmp_b1_v,
     cmp_w2_v, w_branch_a, w_branch_b, w_out, norm2, w_route_group, b_route_group, w_route_expert,
     b_route_expert, w_exp_gate, w_exp_up, w_exp_down) = p
    rwkv_p = (mu_shift, w0, w_decay_up, a0, w_iclr_up, w_gate_up, k_k, k_a, r_k, ln_x_w, ln_x_b)
    cmp_p = (kc_norm, cmp_pe_k, cmp_w1_k, cmp_b1_k, cmp_w2_k, cmp_pe_v, cmp_w1_v, cmp_b1_v, cmp_w2_v)
    merge_p = (w_branch_a, w_branch_b, w_out, norm2, w_route_group, b_route_group, w_route_expert,
               b_route_expert, w_exp_gate, w_exp_up, w_exp_down)

    Bp, Tp, _ = x_prompt.shape
    zp = rms_norm(x_prompt, norm1) @ w_in
    oa_p, wkv_p, shift_p = rwkv_branch(
        zp[..., :RW_IN], jnp.zeros((Bp, RW_IN), zp.dtype),
        jnp.zeros((Bp, RWKV_HEADS, HEAD_DIM, HEAD_DIM), state_wkv.dtype), *rwkv_p)
    q_p, kvc_p, kvs_p, kvw_p, gates_p = nsa_inputs(zp, q_norm, ks_norm, kw_norm)
    kc_p, vc_p = compress_kv(kvc_p, *cmp_p)
    ob_p = nsa_prompt(q_p, kc_p, vc_p, kvs_p, kvw_p, gates_p)
    y_p = merge_and_channel_mix(x_prompt, zp, oa_p, ob_p, *merge_p)
    win_p = kvw_p[:, Tp - min(WINDOW, Tp):]

    Bs, Ts, _ = x_sample.shape
    zs = rms_norm(x_sample, norm1) @ w_in
    oa_s, wkv_s, shift_s = rwkv_branch(zs[..., :RW_IN], state_shift, state_wkv, *rwkv_p)
    q_s, kvc_s, kvs_s, kvw_s, gates_s = nsa_inputs(zs, q_norm, ks_norm, kw_norm)
    past_c = cache_cmp_kv[page_table].reshape((Bs, PAST_LEN, 2, NSA_KV_HEADS, HEAD_DIM))
    kc_s, vc_s = compress_kv(jnp.concatenate([past_c.astype(kvc_s.dtype), kvc_s], axis=1), *cmp_p)
    n_buf = cache_win_kv.shape[1]
    win_all = jnp.concatenate([cache_win_kv.astype(kvw_s.dtype), kvw_s], axis=1)
    q_pos = PAST_LEN + jnp.arange(Ts)
    kw_pos = PAST_LEN - n_buf + jnp.arange(n_buf + Ts)
    ob_s = nsa_core(q_s, q_pos, kc_s, vc_s, -(-(PAST_LEN + Ts) // SEL_BLOCK),
                    make_paged_gather(cache_slc_kv, page_table, kvs_s),
                    win_all[:, :, 0], win_all[:, :, 1], kw_pos, gates_s)
    y_s = merge_and_channel_mix(x_sample, zs, oa_s, ob_s, *merge_p)
    keep = min(WINDOW, n_buf + Ts)
    win_s = win_all[:, n_buf + Ts - keep:]
    return y_p, y_s, (kvc_p, kvs_p, win_p, wkv_p, shift_p, kvc_s, kvs_s, win_s, wkv_s, shift_s)

def setup_inputs(seed: int = 0) -> dict:
    key = jax.random.key(seed)
    keys = iter(jax.random.split(key, 64))
    nrm = lambda shape, scale: jax.random.normal(next(keys), shape, F32) * scale
    uni = lambda shape, lo, hi: jax.random.uniform(next(keys), shape, F32, lo, hi)
    L = DEPTH
    n_pages = PAST_LEN // PAGE_SIZE
    n_used = DEC_BATCH * n_pages
    n_pool = (n_used * 5) // 4
    return {
        'x_prompt': nrm((BATCH, SEQ, D_MODEL), 1.0),
        'x_sample': nrm((DEC_BATCH, DEC_SEQ, D_MODEL), 1.0),
        'cache_cmp_kv': nrm((L, n_pool, PAGE_SIZE, 2, NSA_KV_HEADS, HEAD_DIM), 1.0),
        'cache_slc_kv': nrm((L, n_pool, PAGE_SIZE, 2, NSA_KV_HEADS, HEAD_DIM), 1.0),
        'cache_win_kv': nrm((L, DEC_BATCH, min(WINDOW, PAST_LEN), 2, NSA_KV_HEADS, HEAD_DIM), 1.0),
        'state_wkv': nrm((L, DEC_BATCH, RWKV_HEADS, HEAD_DIM, HEAD_DIM), 0.5),
        'state_shift': nrm((L, DEC_BATCH, RW_IN), 1.0),
        'page_table': jax.random.permutation(next(keys), n_pool)[:n_used].reshape(DEC_BATCH, n_pages).astype(jnp.int32),
        'norm1': 1.0 + nrm((L, D_MODEL), 0.02),
        'w_in': nrm((L, D_MODEL, N_IN), D_MODEL ** -0.5),
        'mu_shift': uni((L, RW_IN), 0.0, 1.0),
        'w0': uni((L, C_A), -6.0, -0.5),
        'w_decay_up': nrm((L, R_DECAY, C_A), 0.5 * R_DECAY ** -0.5),
        'a0': nrm((L, C_A), 0.1),
        'w_iclr_up': nrm((L, R_ICLR, C_A), R_ICLR ** -0.5),
        'w_gate_up': nrm((L, R_GATE, C_A), R_GATE ** -0.5),
        'k_k': 0.85 + nrm((L, C_A), 0.05),
        'k_a': 1.0 + nrm((L, C_A), 0.05),
        'r_k': nrm((L, RWKV_HEADS, HEAD_DIM), 0.1),
        'ln_x_w': 1.0 + nrm((L, C_A), 0.02),
        'ln_x_b': nrm((L, C_A), 0.02),
        'q_norm': 1.0 + nrm((L, HEAD_DIM), 0.02),
        'kc_norm': 1.0 + nrm((L, HEAD_DIM), 0.02),
        'ks_norm': 1.0 + nrm((L, HEAD_DIM), 0.02),
        'kw_norm': 1.0 + nrm((L, HEAD_DIM), 0.02),
        'cmp_pe_k': nrm((L, CMP_LEN, HEAD_DIM), 0.1),
        'cmp_w1_k': nrm((L, CMP_LEN, HEAD_DIM, CMP_HIDDEN), (CMP_LEN * HEAD_DIM) ** -0.5),
        'cmp_b1_k': nrm((L, CMP_HIDDEN), 0.02),
        'cmp_w2_k': nrm((L, CMP_HIDDEN, HEAD_DIM), CMP_HIDDEN ** -0.5),
        'cmp_pe_v': nrm((L, CMP_LEN, HEAD_DIM), 0.1),
        'cmp_w1_v': nrm((L, CMP_LEN, HEAD_DIM, CMP_HIDDEN), (CMP_LEN * HEAD_DIM) ** -0.5),
        'cmp_b1_v': nrm((L, CMP_HIDDEN), 0.02),
        'cmp_w2_v': nrm((L, CMP_HIDDEN, HEAD_DIM), CMP_HIDDEN ** -0.5),
        'w_branch_a': nrm((L, C_A, D_MODEL), C_A ** -0.5),
        'w_branch_b': nrm((L, C_B, D_MODEL), C_B ** -0.5),
        'w_out': nrm((L, D_MODEL, D_MODEL), D_MODEL ** -0.5),
        'norm2': 1.0 + nrm((L, D_MODEL), 0.02),
        'w_route_group': nrm((L, D_MODEL, N_GROUPS), D_MODEL ** -0.5),
        'b_route_group': nrm((L, N_GROUPS), 0.01),
        'w_route_expert': nrm((L, D_MODEL, N_EXPERTS), D_MODEL ** -0.5),
        'b_route_expert': nrm((L, N_EXPERTS), 0.01),
        'w_exp_gate': nrm((L, N_EXPERTS, D_MODEL, D_EXPERT), D_MODEL ** -0.5),
        'w_exp_up': nrm((L, N_EXPERTS, D_MODEL, D_EXPERT), D_MODEL ** -0.5),
        'w_exp_down': nrm((L, N_EXPERTS, D_EXPERT, D_MODEL), D_EXPERT ** -0.5),
    }

def reference(x_prompt, x_sample, cache_cmp_kv, cache_slc_kv, cache_win_kv, state_wkv, state_shift, page_table,
              norm1, w_in, mu_shift, w0, w_decay_up, a0, w_iclr_up, w_gate_up, k_k, k_a, r_k, ln_x_w, ln_x_b,
              q_norm, kc_norm, ks_norm, kw_norm, cmp_pe_k, cmp_w1_k, cmp_b1_k, cmp_w2_k, cmp_pe_v, cmp_w1_v,
              cmp_b1_v, cmp_w2_v, w_branch_a, w_branch_b, w_out, norm2, w_route_group, b_route_group,
              w_route_expert, b_route_expert, w_exp_gate, w_exp_up, w_exp_down):
    layer_weights = (norm1, w_in, mu_shift, w0, w_decay_up, a0, w_iclr_up, w_gate_up, k_k, k_a, r_k, ln_x_w,
                     ln_x_b, q_norm, kc_norm, ks_norm, kw_norm, cmp_pe_k, cmp_w1_k, cmp_b1_k, cmp_w2_k, cmp_pe_v,
                     cmp_w1_v, cmp_b1_v, cmp_w2_v, w_branch_a, w_branch_b, w_out, norm2, w_route_group,
                     b_route_group, w_route_expert, b_route_expert, w_exp_gate, w_exp_up, w_exp_down)
    xp, xs = x_prompt, x_sample
    per_layer = []
    for l in range(DEPTH):
        xp, xs, st = decoder_layer(xp, xs, cache_cmp_kv[l], cache_slc_kv[l], cache_win_kv[l], state_wkv[l],
                                   state_shift[l], page_table, tuple(w[l] for w in layer_weights))
        per_layer.append(st)
    s = [jnp.stack([st[i] for st in per_layer]) for i in range(10)]
    return (xp, xs, s[0], s[1], s[2], s[3], s[4], s[5], s[6], s[7], s[8], s[9])


_drawn_inputs = setup_inputs


def setup_inputs(seed=0):
    import zlib

    import numpy as np

    out = dict(_drawn_inputs(seed))
    spreads = {}
    factors = {'ln_x_b': 3.314,
     'q_norm': 8.0,
     'kc_norm': 8.0,
     'ks_norm': 4.149,
     'kw_norm': 3.742,
     'cmp_pe_k': 4.454,
     'cmp_b1_k': 8.0,
     'cmp_b1_v': 3.357,
     'b_route_group': 7.037,
     'b_route_expert': 4.73}
    for name, (base, spread) in spreads.items():
        noise = np.random.default_rng([zlib.crc32(name.encode()), seed]).standard_normal(out[name].shape)
        drawn = base * np.exp(spread * noise) if base else spread * noise
        out[name] = __import__('jax').numpy.asarray(drawn.astype(out[name].dtype))
    for name, factor in factors.items():
        out[name] = (out[name] * factor).astype(out[name].dtype)
    return out
```

```python
from contextlib import ExitStack

import concourse.bass as bass
from concourse import mybir
import numpy as np

F32 = mybir.dt.float32
I32 = mybir.dt.int32
U32 = mybir.dt.uint32
ALU = mybir.AluOpType
ACT = mybir.ActivationFunctionType
AX_X = mybir.AxisListType.X

P = 128
D = 1024
KC = D // P
TPR, NB, TS = 512, 8, 4
TSM = NB * TS
T = TPR + TSM
HD = 64
RW_IN = 1696
CH = 64
NCH = TPR // CH + 1
TP = NCH * CH
LV = 5
PAGE, NPAGES, PAST = 128, 16, 2048
NKC_P = (TPR - 32) // 16 + 1
NKC_S = (PAST + TS - 32) // 16 + 1
NSB = -(-(PAST + TS) // HD)
HR = 128
NE, CAP = 32, 128
NOV = 2 * T // CAP
NBLK = NE + NOV
NEG = -1e30
RMS_EPS, GN_EPS = 1e-6, 64e-5
DECAY = -float(np.exp(-0.5))



def shape_constants():
    c = {}
    p = np.arange(P)
    c["ident"] = np.eye(P)
    c["blockones"] = (p[:, None] // HD == p[None, :] // HD)
    c["ones"] = np.ones((P, P))
    c["tri"] = np.where(p[None, :] <= p[:, None], 0.0, NEG)
    s, t = p[:, None] % CH, np.arange(CH)[None, :]
    for name, same in (("p", np.ones((P, CH), bool)), ("s", s // TS == t // TS)):
        c["gram_" + name] = np.concatenate([(s < t) & same, (s <= t) & same], 1)
        c["lvl0_" + name] = np.concatenate([(t < s) & (t // 2 == s // 2) & same, (s < t) & (t // 2 == s // 2) & same], 1)
    c["eye2"] = (s == t)
    lv = []
    for l in range(1, LV + 1):
        b = 2 ** l
        lv.append((s // (2 * b) == t // (2 * b)) & (s // b % 2 == 0) & (t // b % 2 == 1))
    c["levels"] = np.concatenate(lv, 1)
    tok = np.arange(T)
    start = np.where(tok < TPR, tok % CH == 0, tok % TS == 0)
    c["restart"] = np.repeat((~start)[None, :], P, 0)
    c["seq"] = ((p % CH)[:, None] // TS == np.arange(NB)[None, :])
    q = np.arange(4)[None, :, None] * P + p[:, None, None]
    c["cmpneg_p"] = np.where(np.arange(NKC_P)[None, None, :] * 16 + 31 <= q, 0.0, NEG).reshape(P, -1)
    c["cmp_p"] = (np.arange(NKC_P)[None, None, :] * 16 + 31 <= q).reshape(P, -1)
    b4, g, m, st = p // 32, p // 16 % 2, p // 4 % 4, p % 4
    nb = np.arange(TSM)
    new = [(nb[None, :] // TS == (4 * h + b4)[:, None]) & (nb[None, :] % TS <= st[:, None]) for h in range(2)]
    c["new_s"] = np.concatenate([np.where(x, 0.0, NEG) for x in new], 1)
    c["win_old"] = np.where(np.arange(TS)[None, :] > st[:, None], 0.0, NEG)
    c["sumheads"] = (b4[:, None] == b4[None, :]) & (g[:, None] == g[None, :]) & (st[:, None] == st[None, :])
    n = np.arange(P)[:, None] * 16
    j = np.arange(NSB)[None, :]
    c["overlap"] = (n < (j + 1) * HD) & (n + 32 > j * HD) & (p[:, None] < NKC_S)
    c["grp"] = np.stack([g == 0, g == 1], 1)
    c["rowtok"] = np.concatenate([(p[:, None] < TSM) & (p[:, None] // TS == 4 * h + b4[None, :]) & (p[:, None] % TS == st[None, :]) for h in range(2)], 1)
    c["rowhead"] = np.tile(np.arange(8)[None, :] == (g * 4 + m)[:, None], (1, 3))
    c["before"] = p[:, None] < p[None, :]
    c["iota_e"] = np.repeat(np.arange(NE)[None, :], P, 0)
    c["egroup"] = np.repeat((np.arange(NE) // 8)[None, :], P, 0)
    c["iota_o"] = np.repeat(np.arange(NOV)[None, :], P, 0)
    c["slotval"] = np.concatenate([(2 * (i * P + p) + k)[:, None] for i in range(5) for k in range(2)], 1)
    out, at, cols = {}, 0, []
    for k, v in c.items():
        v = np.asarray(v, np.float32)
        out[k] = (at, v.shape[1])
        cols.append(v)
        at += v.shape[1]
    return out, np.concatenate(cols, 1)


CONST_AT, CONSTS = shape_constants()
PAR_AT = {}
_at = 0
for _n, _w in (("mu", 14), ("w0", 4), ("a0", 4), ("k_k", 4), ("k_a", 4), ("r_k", 4), ("ln_w", 4), ("ln_b", 4),
               ("norm1", KC), ("b1k", 1), ("b1v", 1), ("norm2", KC)):
    PAR_AT[_n] = (_at, _w)
    _at += _w
NPAR = _at


class Chain:

    def __init__(self, eng, sem):
        self.eng, self.sem, self.n = eng, sem, 0

    def __call__(self, ins):
        self.n += 1
        ins.then_inc(self.sem, 1)
        self.eng.wait_ge(self.sem, self.n)


def project_inputs(nc, io, PS, sem, cst, z):
    with ExitStack() as ctx:
        def t(name, shape, dt=F32):
            return ctx.enter_context(nc.sbuf_tensor(name, shape, dt))

        par = io["par_sb"]
        xT = t("p1_xT", [P, KC, T])
        sq = t("p1_sq", [P, KC, T])
        rstd = t("p1_rstd", [P, T])
        hT = t("p1_hT", [P, KC, T])
        NW = 3
        w = t("p1_w", [P, NW, KC, 512])
        NEV = 3
        ev = t("p1_ev", [P, NEV, 512])
        sqh = t("p1_sqh", [P, 512])
        ssh = t("p1_ssh", [P, 8])
        gains = t("p1_gains", [P, 3, HD])
        gate = t("p1_gate", [P, NEV, 24])

        slabs = [("T", 512), ("T", 512), ("T", 512), ("T", 160), ("q", 512), ("kvcs", 512), ("kvwg", 280)]
        units = []
        for s, (kind, width) in enumerate(slabs):
            if kind == "T" and width == 512:
                units += [(s, "T", 128 * j, 128, 4 * s + j) for j in range(4)]
            elif kind == "T":
                units += [(s, "T", 0, 64, 12), (s, "T", 64, 96, 13)]
            else:
                units += [(s, kind, i, min(P, T - i * P), width) for i in range(5)]
        tok_units = [u for u in units if u[1] != "T"]
        nT = len(units) - len(tok_units)
        last_of_slab = [max(i for i, u in enumerate(units) if u[0] == s) for s in range(len(slabs))]

        const_in, x_in = sem("p1_const_in"), sem("p1_x_in")
        w_ready = [sem(f"p1_w_ready{i}") for i in range(NW)]
        squared, sumsq, h_ready = sem("p1_squared"), sem("p1_sumsq"), sem("p1_h_ready")
        mm_done, evac_act, evac_dve = sem("p1_mm_done"), sem("p1_evac_act"), sem("p1_evac_dve")
        normed, stored = sem("p1_normed"), [sem(f"p1_stored{i}") for i in range(NEV)]
        h_stored = sem("p1_h_stored")
        root_in, root_out = sem("p1_root_in"), sem("p1_root_out")
        dchain, zeroed, gated = sem("p1_dchain"), sem("p1_zeroed"), sem("p1_gated")

        def unit_psum(i):
            u = units[i]
            if u[1] == "T":
                return PS[0:u[3], (i % 2) * 1024:(i % 2) * 1024 + T]
            k = i - nT
            return PS[0:u[3], 2048 + (k % 2) * 512:2048 + (k % 2) * 512 + u[4]]

        with nc.Block() as block:
            @block.sync
            def _(sp):
                sp.dma_start(xT[:], io["xT"]).then_inc(x_in, 16)
                sp.dma_start(cst[:], io["consts"]).then_inc(const_in, 16)
                sp.dma_start(par[:], io["par"]).then_inc(const_in, 16)
                sp.dma_start(gains[:], io["gains"]).then_inc(const_in, 16)
                for s in range(len(slabs)):
                    if s == 3:
                        sp.wait_ge(h_ready, KC)
                        sp.dma_start(io["h_dram"], hT[:]).then_inc(h_stored, 16)
                    if s >= NW:
                        sp.wait_ge(mm_done, last_of_slab[s - NW] + 1)
                    wd = slabs[s][1]
                    sp.dma_start(w[:, s % NW, :, 0:wd], io["w_in"][s]).then_inc(w_ready[s % NW], 16)
                sp.wait_ge(h_stored, 16)

            @block.gpsimd
            def _(pool):
                nc.gpsimd.memset(z[:, 12:14, :], 0.0).then_inc(zeroed, 1)
                n_st = [0] * NEV
                for k, (s, kind, i, rows, width) in enumerate(tok_units):
                    e = k % NEV
                    pool.wait_ge(normed, k + 1)
                    r = slice(i * P, i * P + rows)
                    if kind == "q":
                        pool.dma_start(io["q_dram"][r, :], ev[0:rows, e, :]).then_inc(stored[e], 16)
                    elif kind == "kvcs":
                        pool.dma_start(io["kvc"][r, :], ev[0:rows, e, 0:256]).then_inc(stored[e], 16)
                        pool.dma_start(io["kvs"][r, :], ev[0:rows, e, 256:512]).then_inc(stored[e], 16)
                    else:
                        pool.dma_start(io["kvw"][r, :], ev[0:rows, e, 0:256]).then_inc(stored[e], 16)
                        pool.wait_ge(gated, i + 1)
                        pool.dma_start(io["gate_dram"][r, :], gate[0:rows, e, :]).then_inc(stored[e], 16)
                    n_st[e] += 16 if kind == "q" else 32
                for e in range(NEV):
                    pool.wait_ge(stored[e], n_st[e])

            def stores_before(k):
                return sum(16 if tok_units[j][1] == "q" else 32 for j in range(k % NEV, k, NEV))

            @block.tensor
            def _(pe):
                pe.wait_ge(const_in, 48)
                for c in range(KC):
                    pe.wait_ge(squared, c + 1)
                    o = slice(c * 128, c * 128 + 128)
                    nc.tensor.matmul(PS[:, 3072:3584], cst["ones"], sq[:, c, 0:512], start=(c == 0), stop=(c == KC - 1))
                    last = nc.tensor.matmul(PS[:, 3584:3584 + TSM], cst["ones"], sq[:, c, 512:T],
                                            start=(c == 0), stop=(c == KC - 1))
                last.then_inc(sumsq, 1)
                pe.wait_ge(h_ready, KC)
                for i, (s, kind, a, m, b) in enumerate(units):
                    if i == 0 or units[i - 1][0] != s:
                        pe.wait_ge(w_ready[s % NW], 16 * (s // NW + 1))
                    out = unit_psum(i)
                    if kind == "T":
                        if i >= 2:
                            pe.wait_ge(evac_act if i % 2 == 0 else evac_dve, i // 2)
                        for n in (slice(0, 512), slice(512, T)):
                            for c in range(KC):
                                last = nc.tensor.matmul(out[:, n], w[:, s % NW, c, a:a + m], hT[:, c, n],
                                                        start=(c == 0), stop=(c == KC - 1))
                    else:
                        k = i - nT
                        if k >= 2:
                            pe.wait_ge(evac_act, nT // 2 + k - 1)
                        for c in range(KC):
                            last = nc.tensor.matmul(out, hT[:, c, a * P:a * P + m], w[:, s % NW, c, 0:b],
                                                    start=(c == 0), stop=(c == KC - 1))
                    last.then_inc(mm_done, 1)

            @block.scalar
            def _(act):
                act.wait_ge(x_in, 16)
                for c in range(KC):
                    nc.scalar.activation(sq[:, c, :], xT[:, c, :], ACT.Square).then_inc(squared, 1)
                act.wait_ge(root_in, 1)
                nc.scalar.activation(rstd[:], rstd[:], ACT.Sqrt).then_inc(root_out, 1)

                def root(k):
                    m, nh = tok_units[k][3], 8 if tok_units[k][1] == "q" else 2
                    act.wait_ge(root_in, k + 2)
                    nc.scalar.activation(ssh[0:m, 0:nh], ssh[0:m, 0:nh], ACT.Sqrt).then_inc(root_out, 1)

                act.wait_ge(zeroed, 1)
                for i, (s, kind, a, m, b) in enumerate(units):
                    if kind == "T":
                        if i % 2 == 0:
                            act.wait_ge(mm_done, i + 1)
                            nc.scalar.activation(z[0:m, b, 0:T], unit_psum(i), ACT.Copy).then_inc(evac_act, 1)
                        continue
                    k = i - nT
                    act.wait_ge(mm_done, i + 1)
                    if k >= NEV:
                        act.wait_ge(stored[k % NEV], stores_before(k))
                    if kind == "kvwg":
                        nc.scalar.activation(gate[0:m, k % NEV, :], unit_psum(i)[:, 256:280], ACT.Sigmoid).then_inc(gated, 1)
                        nc.scalar.activation(ev[0:m, k % NEV, 0:256], unit_psum(i)[:, 0:256], ACT.Copy).then_inc(evac_act, 1)
                    else:
                        nc.scalar.activation(ev[0:m, k % NEV, :], unit_psum(i), ACT.Copy).then_inc(evac_act, 1)
                    if k:
                        root(k - 1)
                root(len(tok_units) - 1)

            @block.vector
            def _(dve):
                link = Chain(dve, dchain)
                dve.wait_ge(sumsq, 1)
                link(nc.vector.tensor_scalar(rstd[:], PS[:, 3072:3072 + T], 1.0 / D, RMS_EPS, ALU.mult, ALU.add))
                dve.sem_inc(root_in, 1)
                dve.wait_ge(root_out, 1)
                link(nc.vector.reciprocal(rstd[:], rstd[:]))
                dve.wait_ge(x_in, 16)
                dve.wait_ge(const_in, 48)
                for c in range(KC):
                    nc.vector.scalar_tensor_tensor(out=hT[:, c, :], in0=xT[:, c, :], scalar=io["P"]("norm1", c),
                                                   in1=rstd[:], op0=ALU.mult, op1=ALU.mult).then_inc(h_ready, 1)
                dve.wait_ge(zeroed, 1)
                for i, (s, kind, a, m, b) in enumerate(units):
                    if kind == "T" and i % 2 == 1:
                        dve.wait_ge(mm_done, i + 1)
                        nc.vector.tensor_copy(z[0:m, b, 0:T], unit_psum(i)).then_inc(evac_dve, 1)
                for k, (s, kind, i, m, width) in enumerate(tok_units):
                    nh, lo, g = {"q": (8, 0, 0), "kvcs": (2, 256, 1), "kvwg": (2, 0, 2)}[kind]
                    dve.wait_ge(evac_act, nT // 2 + k + 1)
                    v = ev[0:m, k % NEV, lo:lo + nh * HD].rearrange("p (h d) -> p h d", d=HD)
                    s_ = sqh[0:m, 0:nh * HD].rearrange("p (h d) -> p h d", d=HD)
                    link(nc.vector.tensor_tensor(s_, v, v, ALU.mult))
                    link(nc.vector.reduce_sum(ssh[0:m, 0:nh], s_, AX_X))
                    link(nc.vector.tensor_scalar(ssh[0:m, 0:nh], ssh[0:m, 0:nh], 1.0 / HD, RMS_EPS, ALU.mult, ALU.add))
                    dve.sem_inc(root_in, 1)
                    dve.wait_ge(root_out, k + 2)
                    link(nc.vector.reciprocal(ssh[0:m, 0:nh], ssh[0:m, 0:nh]))
                    link(nc.vector.tensor_tensor(v, v, ssh[0:m, 0:nh].unsqueeze(2).to_broadcast([m, nh, HD]), ALU.mult))
                    nc.vector.tensor_tensor(v, v, gains[0:m, g, :].unsqueeze(1).to_broadcast([m, nh, HD]),
                                            ALU.mult).then_inc(normed, 1)


def rwkv(nc, io, PS, sem, cst, z):
    Pm = io["P"]
    with ExitStack() as ctx:
        def t(name, shape, dt=F32):
            return ctx.enter_context(nc.sbuf_tensor(name, shape, dt))

        zm = t("r_zm", [P, 14, TP])
        r_, k_, v_ = zm[:, 0:4, :], zm[:, 4:8, :], zm[:, 8:12, :]
        sp2 = t("r_sp2", [P, 4, TP])
        lw, a_, L, kk = z[:, 0:4, :], z[:, 4:8, :], z[:, 8:12, :], sp2[:, :, :]
        g_ = t("r_g", [P, 4, TP])
        kka = t("r_kka", [P, 4, TP])
        AR = t("r_AR", [P, 4, 2, TP])
        BK = t("r_BK", [P, 4, 2, TP])
        BD = t("r_BD", [P, 4, TP])
        KD = t("r_KD", [P, 4, TP])
        E3 = t("r_E3", [P, 4, TP])
        tw, sg = E3[0:32, 0, 0:T], E3[0:96, 1, 0:T]
        wup = t("r_wup", [64, 512])
        wgu = t("r_wgu", [96, 512])
        shift = t("r_shift", [P, 14, NB])
        wc = t("r_wc", [P, 4, NCH - 1 + NB])
        tok = t("r_tok", [P, 3, 4, CH])
        G = t("r_G", [P, 2, 4, 2, CH])
        NT = t("r_NT", [P, 4, LV, CH])
        TB = t("r_TB", [P, 4, 2, CH])
        X = t("r_X", [P, 4, CH])
        U0 = t("r_U0", [P, 4, CH])
        U = t("r_U", [P, 4, CH])
        S = t("r_S", [P, 4, HD])
        Yt = io["Yt"] = t("r_Y", [P, NCH, 4, HD])
        S0 = E3[:, :, 0:512].rearrange("p a (b i) -> p a b i", b=NB)
        SAT = t("r_SAT", [P, 4, 2, CH])
        expd = t("r_exp", [P, 2, NB, HD])
        st1, st2 = t("r_st1", [P, NCH * 4]), t("r_st2", [P, NCH * 4])

        par_in, lora_w, s0_in = sem("r_par_in"), sem("r_lora_w"), sem("r_s0_in")
        mixed, lora_in, lora_mm = sem("r_mixed"), sem("r_lora_in"), sem("r_lora_mm")
        lora_out, kk2_ready, kk_mm, kk_used = sem("r_lora_out"), sem("r_kk2"), sem("r_kkmm"), sem("r_kkused")
        L_ready, exps, ops_ready, e3_free = sem("r_L"), sem("r_exps"), sem("r_ops"), sem("r_e3free")
        bonus_in, bonus_mm, bonus_out = sem("r_bonus_in"), sem("r_bonus_mm"), sem("r_bonus_out")
        gram, gram_out, tok_out = sem("r_gram"), sem("r_gram_out"), sem("r_tok_out")
        x_mm, x_out, t_mm, t_out = sem("r_x_mm"), sem("r_x_out"), sem("r_t_mm"), sem("r_t_out")
        u0_mm, u0_out, u_mm, u_out = sem("r_u0_mm"), sem("r_u0_out"), sem("r_u_mm"), sem("r_u_out")
        y_mm, y_out, s_mm, s_out = sem("r_y_mm"), sem("r_y_out"), sem("r_s_mm"), sem("r_s_out")
        sat_mm, sat_out, exp_out, sf_mm, sf_out = (sem("r_sat_mm"), sem("r_sat_out"), sem("r_exp_out"), sem("r_sf_mm"),
                                                   sem("r_sf_out"))
        gn_ready, back_mm, back_out, oa_ready, out_dma = (sem("r_gn"), sem("r_back_mm"), sem("r_back_out"),
                                                          sem("r_oa"), sem("r_out_dma"))
        shift_dma = sem("r_shift_dma")
        root_in, root_out = sem("r_root_in"), sem("r_root_out")
        lastz = t("r_lastz", [P, 14, 1 + NB])
        last_rows = sem("r_last_rows")
        dchain, achain, s_init = sem("r_dchain"), sem("r_achain"), sem("r_s_init")

        def wide(k):
            return PS[:, (k % 4) * 1024:(k % 4) * 1024 + T]

        def mmT(k, m, lhsT, rhs):
            nc.tensor.matmul(wide(k)[0:m, 0:512], lhsT, rhs[:, 0:512], start=True, stop=True)
            return nc.tensor.matmul(wide(k)[0:m, 512:T], lhsT, rhs[:, 512:T], start=True, stop=True)

        halves = (slice(0, 64), slice(64, 128))
        psG = PS[:, 0:1024].rearrange("p (k a b s) -> p k a b s", k=2, a=4, b=2)
        psN = PS[:, 1024:1280].rearrange("p (a s) -> p a s", a=4)
        psX = PS[:, 1280:1536].rearrange("p (a s) -> p a s", a=4)
        psTok = PS[:, 1536:2304].rearrange("p (k a s) -> p k a s", k=3, a=4)
        psU0 = PS[:, 2304:2560].rearrange("p (a s) -> p a s", a=4)
        psT = PS[:, 2560:3072].rearrange("p (a b s) -> p a b s", a=4, b=2)
        psU = PS[:, 3072:3328].rearrange("p (a s) -> p a s", a=4)
        psY = PS[:, 3328:3584].rearrange("p (a s) -> p a s", a=4)
        psS = PS[:, 3584:3840].rearrange("p (a s) -> p a s", a=4)
        psSAT = PS[:, 0:512].rearrange("p (a b s) -> p a b s", a=4, b=2)

        with nc.Block() as block:
            @block.sync
            def _(sp):
                sp.dma_start(wup[:], io["w_lora_up"]).then_inc(lora_w, 16)
                sp.dma_start(wgu[:], io["w_gate_up"]).then_inc(lora_w, 16)
                sp.dma_start(shift[:], io["shift_in"]).then_inc(par_in, 16)
                sp.wait_ge(last_rows, 1)
                sp.dma_start(io["shift_out"], lastz[:]).then_inc(shift_dma, 16)
                sp.wait_ge(e3_free, 1)
                sp.dma_start(S0, io["wkv_in"]).then_inc(s0_in, 16)
                sp.wait_ge(s_out, NCH - 1)
                sp.dma_start(io["wkv_p"], S[:]).then_inc(out_dma, 16)
                sp.wait_ge(sf_out, 4)
                sp.dma_start(io["wkv_s"], S0).then_inc(out_dma, 16)
                sp.wait_ge(oa_ready, 4)
                sp.dma_start(io["oa_dram"], BD[:, :, 0:T]).then_inc(out_dma, 16)
                sp.wait_ge(shift_dma, 16)
                sp.wait_ge(out_dma, 48)

            @block.vector
            def _(dve):
                link = Chain(dve, dchain)
                V = nc.vector

                def bc(ap, shape):
                    return ap.to_broadcast(shape)

                link(V.tensor_copy(lastz[:, :, 0:1], z[:, :, TPR - 1:TPR]))
                link(V.tensor_copy(lastz[:, :, 1:1 + NB], z[:, :, TPR + TS - 1:T:TS]))
                dve.sem_inc(last_rows, 1)
                link(V.memset(zm[:, :, T:TP], 0.0))
                for tile in (BK, AR):
                    link(V.memset(tile[:, :, :, T:TP], 0.0))
                for tile in (BD, KD):
                    link(V.memset(tile[:, :, T:TP], 0.0))
                link(V.memset(SAT[:], 0.0))
                link(V.memset(S[:], 0.0))
                dve.sem_inc(s_init, 1)
                link(V.tensor_tensor(zm[:, :, 1:TPR], z[:, :, 0:TPR - 1], z[:, :, 1:TPR], ALU.subtract))
                link(V.tensor_scalar(zm[:, :, 0:1], z[:, :, 0:1], -1.0, None, ALU.mult))
                zs = z[:, :, TPR:T].rearrange("p c (b t) -> p c b t", t=TS)
                zms = zm[:, :, TPR:T].rearrange("p c (b t) -> p c b t", t=TS)
                for c in range(14):
                    link(V.tensor_tensor(zms[:, c, :, 1:TS], zs[:, c, :, 0:TS - 1], zs[:, c, :, 1:TS], ALU.subtract))
                dve.wait_ge(par_in, 16)
                link(V.tensor_tensor(zms[:, :, :, 0], shift[:], zs[:, :, :, 0], ALU.subtract))
                for c in (12, 13, 4, 5, 6, 7, 0, 1, 2, 3, 8, 9, 10, 11):
                    link(V.scalar_tensor_tensor(out=zm[:, c, 0:T], in0=zm[:, c, 0:T], scalar=Pm("mu", c), in1=z[:, c, 0:T],
                                                op0=ALU.mult, op1=ALU.add))
                    if c == 13:
                        dve.sem_inc(mixed, 1)
                dve.sem_inc(mixed, 1)
                for c in range(4):
                    link(V.tensor_scalar(kk[:, c, 0:T], k_[:, c, 0:T], Pm("k_k", c), None, ALU.mult))
                    link(V.tensor_tensor(kka[:, c, 0:T], kk[:, c, 0:T], kk[:, c, 0:T], ALU.mult))
                    dve.sem_inc(kk2_ready, 1)
                dve.wait_ge(lora_out, 12)
                link(V.tensor_scalar(lw[:, :, 0:T], lw[:, :, 0:T], DECAY, None, ALU.mult))
                for c in range(4):
                    link(V.tensor_tensor_scan(L[:, c, 0:T], cst["restart"], lw[:, c, 0:T], 0.0, ALU.mult, ALU.add))
                for c in range(4):
                    dve.wait_ge(kk_mm, c + 1)
                    link(V.tensor_scalar(kka[:, c, 0:T], wide(c), 1e-24, None, ALU.max))
                    dve.sem_inc(root_in, 1)
                    dve.wait_ge(root_out, c + 1)
                    link(V.reciprocal(kka[:, c, 0:T], kka[:, c, 0:T]))
                    link(V.tensor_tensor(kk[:, c, 0:T], kk[:, c, 0:T], kka[:, c, 0:T], ALU.mult))
                dve.sem_inc(kk_used, 1)
                link(V.tensor_tensor(KD[:, :, 0:T], L[:, :, 0:T], lw[:, :, 0:T], ALU.subtract))
                Lp = L[:, :, 0:TPR].rearrange("p a (c s) -> p a c s", s=CH)
                Ls = L[:, :, TPR:T].rearrange("p a (c s) -> p a c s", s=TS)
                dp = lw[:, :, 0:TPR].rearrange("p a (c s) -> p a c s", s=CH)
                ds_ = lw[:, :, TPR:T].rearrange("p a (c s) -> p a c s", s=TS)
                for c in range(4):
                    link(V.tensor_tensor(dp[:, c], bc(Lp[:, c, :, CH - 1:CH], [P, 8, CH]), Lp[:, c], ALU.subtract))
                    link(V.tensor_tensor(ds_[:, c], bc(Ls[:, c, :, TS - 1:TS], [P, NB, TS]), Ls[:, c], ALU.subtract))
                dve.sem_inc(L_ready, 1)
                link(V.tensor_tensor(kka[:, :, 0:T], kk[:, :, 0:T], a_[:, :, 0:T], ALU.mult))
                for c in range(4):
                    link(V.tensor_scalar(a_[:, c, 0:T], a_[:, c, 0:T], 1.0, Pm("k_a", c), ALU.subtract, ALU.mult))
                    link(V.scalar_tensor_tensor(out=k_[:, c, 0:T], in0=a_[:, c, 0:T], scalar=1.0, in1=k_[:, c, 0:T],
                                                op0=ALU.add, op1=ALU.mult))
                dve.wait_ge(exps, 1)
                link(V.scalar_tensor_tensor(out=AR[:, :, 0, 0:T], in0=kk[:, :, 0:T], scalar=-1.0, in1=KD[:, :, 0:T],
                                            op0=ALU.mult, op1=ALU.mult))
                dve.wait_ge(exps, 2)
                link(V.tensor_tensor(AR[:, :, 1, 0:T], r_[:, :, 0:T], BD[:, :, 0:T], ALU.mult))
                dve.wait_ge(exps, 3)
                link(V.tensor_tensor(BK[:, :, 0, 0:T], kka[:, :, 0:T], E3[:, :, 0:T], ALU.mult))
                link(V.tensor_tensor(BK[:, :, 1, 0:T], k_[:, :, 0:T], E3[:, :, 0:T], ALU.mult))
                dve.sem_inc(e3_free, 1)
                dve.wait_ge(exps, 5)
                link(V.tensor_tensor(BD[:, :, 0:T], kka[:, :, 0:T], lw[:, :, 0:T], ALU.mult))
                link(V.tensor_tensor(KD[:, :, 0:T], k_[:, :, 0:T], lw[:, :, 0:T], ALU.mult))
                for c in range(4):
                    link(V.scalar_tensor_tensor(out=kka[:, c, 0:T], in0=r_[:, c, 0:T], scalar=Pm("r_k", c),
                                                in1=k_[:, c, 0:T], op0=ALU.mult, op1=ALU.mult))
                dve.sem_inc(ops_ready, 1)
                for c in range(4):
                    dve.wait_ge(bonus_mm, c + 1)
                    link(V.tensor_tensor(a_[:, c, 0:T], wide(c), v_[:, c, 0:T], ALU.mult))
                dve.sem_inc(bonus_out, 1)
                for c in range(NCH):
                    kind = "s" if c == NCH - 1 else "p"
                    dve.wait_ge(gram, c + 1)
                    if c:
                        dve.wait_ge(y_mm, c)
                    mG = cst["gram_" + kind].rearrange("p (b s) -> p b s", b=2)
                    m0 = cst["lvl0_" + kind].rearrange("p (b s) -> p b s", b=2)
                    for k2 in range(2):
                        link(V.tensor_tensor(G[:, k2], psG[:, k2], bc(mG.unsqueeze(1), [P, 4, 2, CH]), ALU.mult))
                    mL = cst["levels"].rearrange("p (l s) -> p l s", l=LV)
                    link(V.tensor_tensor(NT[:], bc(G[:, 0, :, 0, :].unsqueeze(2), [P, 4, LV, CH]),
                                         bc(mL.unsqueeze(1), [P, 4, LV, CH]), ALU.mult))
                    link(V.tensor_tensor(TB[:, :, 0, :], psN, bc(m0[:, 0:1, :], [P, 4, CH]), ALU.mult))
                    link(V.tensor_tensor(TB[:, :, 1, :], G[:, 0, :, 0, :], bc(m0[:, 1:2, :], [P, 4, CH]), ALU.mult))
                    link(V.tensor_tensor(TB[:].rearrange("p a b s -> p (a b) s"), TB[:].rearrange("p a b s -> p (a b) s"),
                                         bc(cst["eye2"].unsqueeze(1), [P, 8, CH]), ALU.add))
                    dve.sem_inc(gram_out, 1)
                    for l in range(LV):
                        dve.wait_ge(t_mm, c * LV + l + 1)
                        V.tensor_tensor(TB[:], TB[:], psT, ALU.add).then_inc(t_out, 1)
                        dve.wait_ge(t_out, c * LV + l + 1)
                    dve.wait_ge(u_mm, c + 1)
                    V.tensor_copy(U[:], psU).then_inc(u_out, 1)
                    if c < NCH - 1:
                        dve.wait_ge(y_mm, c + 1)
                        link(V.tensor_tensor(S[:], S[:], bc(wc[:, :, c:c + 1], [P, 4, HD]), ALU.mult))
                        dve.wait_ge(s_mm, c + 1)
                        V.tensor_tensor(S[:], S[:], psS, ALU.add).then_inc(s_out, 1)
                        dve.wait_ge(s_out, c + 1)
                dve.wait_ge(u_out, NCH)
                seq = bc(cst["seq"].unsqueeze(2), [P, NB, HD])
                for pr in range(4):
                    if pr:
                        dve.wait_ge(sf_mm, pr)
                    link(V.tensor_tensor(expd[:, 0], bc(U[:, pr, :].unsqueeze(1), [P, NB, HD]), seq, ALU.mult))
                    link(V.tensor_tensor(expd[:, 1], bc(tok[:, 0, pr, :].unsqueeze(1), [P, NB, HD]), seq, ALU.mult))
                    dve.sem_inc(exp_out, 1)
                    link(V.tensor_tensor(S0[:, pr], S0[:, pr], bc(wc[:, pr, 8:16].unsqueeze(2), [P, NB, HD]), ALU.mult))
                    dve.wait_ge(sf_mm, pr + 1)
                    V.tensor_tensor(S0[:, pr], S0[:, pr], PS[:, 0:512].rearrange("p (b i) -> p b i", b=NB),
                                    ALU.add).then_inc(sf_out, 1)
                dve.wait_ge(y_out, NCH)
                Yf = Yt[:].rearrange("p c a i -> p (c a) i")
                sqv = kk[:, :, :].rearrange("p a (c i) -> p (a c) i", i=HD)
                link(V.reduce_sum(st1[:], Yf, AX_X))
                link(V.tensor_scalar(st1[:], st1[:], 1.0 / HD, None, ALU.mult))
                link(V.tensor_tensor(Yf, Yf, bc(st1[:].unsqueeze(2), [P, NCH * 4, HD]), ALU.subtract))
                link(V.tensor_tensor(sqv, Yf, Yf, ALU.mult))
                link(V.reduce_sum(st2[:], sqv, AX_X))
                link(V.tensor_scalar(st2[:], st2[:], 1.0 / HD, GN_EPS, ALU.mult, ALU.add))
                dve.sem_inc(root_in, 1)
                dve.wait_ge(root_out, 5)
                link(V.reciprocal(st2[:], st2[:]))
                link(V.tensor_tensor(Yf, Yf, bc(st2[:].unsqueeze(2), [P, NCH * 4, HD]), ALU.mult))
                dve.sem_inc(gn_ready, 1)
                for pr in range(4):
                    dve.wait_ge(back_mm, pr + 1)
                    link(V.tensor_scalar(BD[:, pr, 0:T], PS[:, pr * 1024:pr * 1024 + T], Pm("ln_w", pr), Pm("ln_b", pr),
                                         ALU.mult, ALU.add))
                    link(V.tensor_tensor(BD[:, pr, 0:T], BD[:, pr, 0:T], a_[:, pr, 0:T], ALU.add))
                    V.tensor_tensor(BD[:, pr, 0:T], BD[:, pr, 0:T], g_[:, pr, 0:T], ALU.mult).then_inc(oa_ready, 1)

            @block.scalar
            def _(act):
                link = Chain(act, achain)
                A = nc.scalar.activation
                act.wait_ge(mixed, 1)
                link(A(tw, zm[0:32, 12, 0:T], ACT.Tanh))
                link(A(sg, zm[0:96, 13, 0:T], ACT.Sigmoid))
                act.sem_inc(lora_in, 1)
                act.wait_ge(mixed, 2)
                for c in range(4):
                    act.wait_ge(lora_mm, 3 * c + 1)
                    A(lw[:, c, 0:T], wide(3 * c), ACT.Sigmoid, bias=Pm("w0", c)).then_inc(lora_out, 1)
                    act.wait_ge(lora_mm, 3 * c + 2)
                    A(a_[:, c, 0:T], wide(3 * c + 1), ACT.Sigmoid, bias=Pm("a0", c)).then_inc(lora_out, 1)
                    act.wait_ge(lora_mm, 3 * c + 3)
                    A(g_[:, c, 0:T], wide(3 * c + 2), ACT.Copy).then_inc(lora_out, 1)
                for c in range(4):
                    act.wait_ge(root_in, c + 1)
                    A(kka[:, c, 0:T], kka[:, c, 0:T], ACT.Sqrt).then_inc(root_out, 1)
                act.wait_ge(L_ready, 1)
                A(KD[:, :, 0:T], KD[:, :, 0:T], ACT.Exp).then_inc(exps, 1)
                A(BD[:, :, 0:T], L[:, :, 0:T], ACT.Exp).then_inc(exps, 1)
                A(E3[:, :, 0:T], L[:, :, 0:T], ACT.Exp, scale=-1.0).then_inc(exps, 1)
                A(lw[:, :, 0:T], lw[:, :, 0:T], ACT.Exp).then_inc(exps, 1)
                A(wc[:, :, 0:8], L[:, :, CH - 1:TPR:CH], ACT.Exp)
                A(wc[:, :, 8:16], L[:, :, TPR + TS - 1:T:TS], ACT.Exp).then_inc(exps, 1)
                for c in range(NCH):
                    if c == NCH - 1:
                        act.wait_ge(s_init, 1)
                        act.wait_ge(sat_mm, 1)
                        A(SAT[:, :, :, 0:TSM], psSAT[:, :, :, 0:TSM], ACT.Copy).then_inc(sat_out, 1)
                    act.wait_ge(gram, c + 1)
                    if c:
                        act.wait_ge(s_mm, c)
                    A(tok[:], psTok, ACT.Copy).then_inc(tok_out, 1)
                    for l in range(LV):
                        act.wait_ge(x_mm, c * LV + l + 1)
                        A(X[:], psX, ACT.Copy).then_inc(x_out, 1)
                    act.wait_ge(u0_mm, c + 1)
                    A(U0[:], psU0, ACT.Copy).then_inc(u0_out, 1)
                    act.wait_ge(y_mm, c + 1)
                    A(Yt[:, c], psY, ACT.Copy).then_inc(y_out, 1)
                act.wait_ge(root_in, 5)
                A(st2[:], st2[:], ACT.Sqrt).then_inc(root_out, 1)

            @block.tensor
            def _(pe):
                M = nc.tensor.matmul
                pe.wait_ge(lora_w, 32)
                pe.wait_ge(lora_in, 1)
                for c in range(4):
                    cs = slice(c * P, (c + 1) * P)
                    for j, (lhsT, rhs) in enumerate(((wup[0:32, cs], tw), (wup[32:64, cs], zm[32:64, 12, 0:T]),
                                                     (wgu[:, cs], sg))):
                        u = 3 * c + j
                        if u >= 4:
                            pe.wait_ge(lora_out, u - 3)
                        mmT(u, P, lhsT, rhs).then_inc(lora_mm, 1)
                for c in range(4):
                    pe.wait_ge(kk2_ready, c + 1)
                    pe.wait_ge(lora_out, 9 + c)
                    mmT(c, P, cst["blockones"], kka[:, c, 0:T]).then_inc(kk_mm, 1)
                pe.wait_ge(kk_used, 1)
                pe.wait_ge(ops_ready, 1)
                for c in range(4):
                    mmT(c, P, cst["blockones"], kka[:, c, 0:T]).then_inc(bonus_mm, 1)
                pe.wait_ge(bonus_out, 1)
                pe.wait_ge(s_init, 1)
                for c in range(NCH):
                    ts = slice(c * CH, (c + 1) * CH)
                    if c == NCH - 1:
                        pe.wait_ge(s0_in, 16)
                        for pr in range(4):
                            for b in range(NB):
                                for h in halves:
                                    s4 = slice(TPR + TS * b, TPR + TS * b + TS)
                                    last = M(psSAT[h, pr, :, TS * b:TS * b + TS], S0[h, pr, b, :], AR[h, pr, :, s4],
                                             start=True, stop=True)
                        last.then_inc(sat_mm, 1)
                        pe.wait_ge(sat_out, 1)
                    if c:
                        pe.wait_ge(tok_out, c)
                    for pr in range(4):
                        for h in halves:
                            for k2 in range(2):
                                M(psG[h, k2, pr], BK[h, pr, k2, ts], AR[h, pr, :, ts], start=True, stop=True)
                            M(psN[h, pr], AR[h, pr, 0, ts], BK[h, pr, 0, ts], start=True, stop=True)
                            for k3, src in enumerate((v_, BD, KD)):
                                last = M(psTok[h, k3, pr], src[h, pr, ts], cst["eye2"][h, :], start=True, stop=True)
                    last.then_inc(gram, 1)
                    pe.wait_ge(gram_out, c + 1)
                    for l in range(LV):
                        n = c * LV + l
                        if l:
                            pe.wait_ge(t_out, n)
                        for pr in range(4):
                            for h in halves:
                                last = M(psX[h, pr], NT[h, pr, l], TB[h, pr, 0], start=True, stop=True)
                        last.then_inc(x_mm, 1)
                        pe.wait_ge(x_out, n + 1)
                        for pr in range(4):
                            for h in halves:
                                M(psT[h, pr, 0], TB[h, pr, 1], X[h, pr], start=True, stop=True)
                                last = M(psT[h, pr, 1], X[h, pr], TB[h, pr, 1], start=True, stop=True)
                        last.then_inc(t_mm, 1)
                    pe.wait_ge(t_out, (c + 1) * LV)
                    pe.wait_ge(tok_out, c + 1)
                    if c:
                        pe.wait_ge(s_out, min(c, NCH - 1))
                    for pr in range(4):
                        for h in halves:
                            if c < NCH - 1:
                                M(psU0[h, pr], AR[h, pr, 0, ts], S[h, pr], start=True, stop=False)
                            else:
                                M(psU0[h, pr], SAT[h, pr, 0], cst["eye2"][h, :], start=True, stop=False)
                            last = M(psU0[h, pr], G[h, 1, pr, 0], tok[h, 0, pr], start=False, stop=True)
                    last.then_inc(u0_mm, 1)
                    pe.wait_ge(u0_out, c + 1)
                    for pr in range(4):
                        for h in halves:
                            last = M(psU[h, pr], TB[h, pr, 1], U0[h, pr], start=True, stop=True)
                    last.then_inc(u_mm, 1)
                    pe.wait_ge(u_out, c + 1)
                    if c:
                        pe.wait_ge(y_out, c)
                    for pr in range(4):
                        for h in halves:
                            if c < NCH - 1:
                                M(psY[h, pr], AR[h, pr, 1, ts], S[h, pr], start=True, stop=False)
                            else:
                                M(psY[h, pr], SAT[h, pr, 1], cst["eye2"][h, :], start=True, stop=False)
                            M(psY[h, pr], G[h, 1, pr, 1], tok[h, 0, pr], start=False, stop=False)
                            last = M(psY[h, pr], G[h, 0, pr, 1], U[h, pr], start=False, stop=True)
                    last.then_inc(y_mm, 1)
                    if c < NCH - 1:
                        for pr in range(4):
                            for h in halves:
                                M(psS[h, pr], tok[h, 1, pr], U[h, pr], start=True, stop=False)
                                last = M(psS[h, pr], tok[h, 2, pr], tok[h, 0, pr], start=False, stop=True)
                        last.then_inc(s_mm, 1)
                for pr in range(4):
                    pe.wait_ge(exp_out, pr + 1)
                    if pr:
                        pe.wait_ge(sf_out, pr)
                    for h in halves:
                        M(PS[h, 0:512], tok[h, 1, pr], expd[h, 0], start=True, stop=False)
                        last = M(PS[h, 0:512], tok[h, 2, pr], expd[h, 1], start=False, stop=True)
                    last.then_inc(sf_mm, 1)
                pe.wait_ge(gn_ready, 1)
                pe.wait_ge(sf_out, 4)
                for pr in range(4):
                    for c in range(NCH):
                        for h in halves:
                            o = pr * 1024 + c * CH
                            last = M(PS[h, o:o + CH], Yt[h, c, pr], cst["eye2"][h, :], start=True, stop=True)
                    last.then_inc(back_mm, 1)


def load_pages(eng, table, dst, pool, half, arrived):
    for b in range(4):
        with eng.Fori(0, NPAGES) as i:
            page = eng.value_load(table[0:1, bass.ds(i + (4 * half + b) * NPAGES, 1)], min_val=0,
                                  max_val=pool.shape[0] - 1)
            src = pool[bass.ds(page, 1)].rearrange("a p k t -> p (a k) t")
            eng.dma_start(dst(b, i), src).then_inc(arrived, 16)


def compress(nc, io, PS, sem, cst, kcT_p, vc_p, kcT_s, vc_s):
    with ExitStack() as ctx:
        def t(name, shape, dt=F32):
            return ctx.enter_context(nc.sbuf_tensor(name, shape, dt))

        w1 = t("c_w1", [P, 2, 32, P])
        w2 = t("c_w2", [P, 2, P])
        pe2 = t("c_pe", [P, 2, 32])
        gain = t("c_gain", [P, HD])
        table = t("c_table", [1, NB * NPAGES], I32)
        rows = t("c_rows", [P, 4, 256])
        cTp = t("c_cTp", [P, 2, TPR])
        cT = [t(f"c_cT{h}", [P, 4, 2, PAST]) for h in range(2)]
        bias = t("c_bias", [P, 2])
        hid = t("c_hid", [P, 2, 512])
        kraw = t("c_kraw", [P, 4, 2, P])
        ksq = t("c_ksq", [P, 4, P])
        ss = t("c_ss", [P, 8])
        kdup = t("c_kdup", [P, 2, 2, HD])

        w_in, rows_in, pages = sem("c_w_in"), sem("c_rows_in"), [sem("c_pages0"), sem("c_pages1")]
        zeroed, tr_mm, tr_out = sem("c_zeroed"), sem("c_tr_mm"), sem("c_tr_out")
        bias_mm, bias_out, hid_mm, hid_out = sem("c_bias_mm"), sem("c_bias_out"), sem("c_hid_mm"), sem("c_hid_out")
        kc_mm, kc_out, root_in, root_out = sem("c_kc_mm"), sem("c_kc_out"), sem("c_root_in"), sem("c_root_out")
        normed, kT_mm, kT_out, dchain = sem("c_normed"), sem("c_kT_mm"), sem("c_kT_out"), sem("c_dchain")
        ins = [(NKC_P, 1), (4 * NKC_S, 4), (4 * NKC_S, 4)]

        with nc.Block() as block:
            @block.sync
            def _(sp):
                sp.dma_start(table[:], io["page_table"]).then_inc(rows_in, 16)
                sp.dma_start(rows[:], io["kvc"][0:TPR, :].rearrange("(i p) n -> p i n", p=P)).then_inc(rows_in, 16)
                sp.wait_ge(zeroed, 2)
                for g in range(2):
                    h = slice(64 * g, 64 * g + 64)
                    sp.dma_start(w1[h, :, :, h], io["cmp_w1"]).then_inc(w_in, 16)
                    sp.dma_start(w2[h, :, h], io["cmp_w2"]).then_inc(w_in, 16)
                    sp.dma_start(pe2[h], io["cmp_pe"]).then_inc(w_in, 16)
                sp.dma_start(gain[:], io["kc_gain"]).then_inc(w_in, 16)
                sp.wait_ge(rows_in, 32)
                for hf in range(2):
                    load_pages(sp, table, lambda b, i: cT[hf][:, b, :, bass.ds(i * PAGE, PAGE)], io["cmp_pool"], hf,
                               pages[hf])

            @block.gpsimd
            def _(pool):
                nc.gpsimd.memset(w1[:], 0.0).then_inc(zeroed, 1)
                nc.gpsimd.memset(w2[:], 0.0).then_inc(zeroed, 1)

            @block.tensor
            def _(pe):
                M = nc.tensor.matmul
                pe.wait_ge(rows_in, 32)
                for kv in range(2):
                    for i in range(4):
                        last = nc.tensor.transpose(PS[:, kv * 512 + i * P:kv * 512 + i * P + P],
                                                   rows[:, i, kv * P:kv * P + P], cst["ident"])
                last.then_inc(tr_mm, 1)
                pe.wait_ge(w_in, 112)
                for kv in range(2):
                    for l in range(32):
                        last = M(PS[:, 1024 + kv:1025 + kv], w1[:, kv, l, :], pe2[:, kv, l:l + 1],
                                 start=(l == 0), stop=(l == 31))
                last.then_inc(bias_mm, 1)
                pe.wait_ge(tr_out, 1)
                for r, (n, nb) in enumerate(ins):
                    if r:
                        pe.wait_ge(pages[r - 1], 16 * 4 * NPAGES)
                    for kv in range(2):
                        if r:
                            pe.wait_ge(hid_out, 2 * r - 1 + kv)
                        for l in range(32):
                            if r == 0:
                                rhs = cTp[:, kv, l:l + 16 * (NKC_P - 1) + 1:16]
                            else:
                                rhs = cT[r - 1][:, :, kv, l:l + 16 * (NKC_S - 1) + 1:16]
                            last = M(PS[:, 2048 + 512 * kv:2048 + 512 * kv + n], w1[:, kv, l, :], rhs,
                                     start=(l == 0), stop=(l == 31))
                        last.then_inc(hid_mm, 1)
                    pe.wait_ge(hid_out, 2 * r + 2)
                    if r:
                        pe.wait_ge(kc_out, r)
                    nk = n // nb
                    for b in range(nb):
                        for kv in range(2):
                            o = 3072 + (b * 2 + kv) * P
                            last = M(PS[0:nk, o:o + P], hid[:, kv, b * nk:b * nk + nk], w2[:, kv, :],
                                     start=True, stop=True)
                    last.then_inc(kc_mm, 1)
                    pe.wait_ge(normed, r + 1)
                    if r == 0:
                        for g in range(2):
                            last = nc.tensor.transpose(PS[:, 1536 + g * 32:1536 + g * 32 + nk],
                                                       kdup[0:nk, g].rearrange("p a d -> p (a d)"), cst["ident"][0:nk, 0:nk])
                    else:
                        pe.wait_ge(kT_out, r)
                        for b in range(nb):
                            last = nc.tensor.transpose(PS[:, 1536 + b * P:1536 + b * P + nk], kraw[0:nk, b, 0, :],
                                                       cst["ident"][0:nk, 0:nk])
                    last.then_inc(kT_mm, 1)

            @block.scalar
            def _(act):
                A = nc.scalar.activation
                act.wait_ge(tr_mm, 1)
                A(cTp[:], PS[:, 0:1024].rearrange("p (k t) -> p k t", k=2), ACT.Copy).then_inc(tr_out, 1)
                act.wait_ge(bias_out, 1)
                for r, (n, nb) in enumerate(ins):
                    nk = n // nb
                    for kv in range(2):
                        act.wait_ge(hid_mm, 2 * r + kv + 1)
                        if r:
                            act.wait_ge(kc_mm, r)
                        A(hid[:, kv, 0:n], PS[:, 2048 + 512 * kv:2048 + 512 * kv + n], ACT.Silu,
                          bias=bias[:, kv:kv + 1]).then_inc(hid_out, 1)
                    act.wait_ge(root_in, r + 1)
                    A(ss[0:nk, 0:2 * nb], ss[0:nk, 0:2 * nb], ACT.Sqrt).then_inc(root_out, 1)

            @block.vector
            def _(dve):
                link = Chain(dve, dchain)
                V = nc.vector
                dve.wait_ge(bias_mm, 1)
                par = io["P"]
                for kv, name in enumerate(("b1k", "b1v")):
                    link(V.tensor_tensor(bias[:, kv:kv + 1], PS[:, 1024 + kv:1025 + kv], par(name), ALU.add))
                dve.sem_inc(bias_out, 1)
                dve.wait_ge(w_in, 112)
                for r, (n, nb) in enumerate(ins):
                    nk = n // nb
                    dve.wait_ge(kc_mm, r + 1)
                    if r:
                        dve.wait_ge(kT_mm, r)
                    ps = PS[0:nk, 3072:3072 + nb * 256].rearrange("p (b k n) -> p b k n", b=nb, k=2)
                    link(V.tensor_copy(kraw[0:nk, 0:nb], ps))
                    dve.sem_inc(kc_out, 1)
                    k = kraw[0:nk, 0:nb, 0, :].rearrange("p b (g d) -> p b g d", g=2)
                    q = ksq[0:nk, 0:nb].rearrange("p b (g d) -> p b g d", g=2)
                    s = ss[0:nk, 0:2 * nb]
                    s3 = s.rearrange("p (b g) -> p b g", g=2)
                    link(V.tensor_tensor(q, k, k, ALU.mult))
                    link(V.reduce_sum(s3, q, AX_X))
                    link(V.tensor_scalar(s, s, 1.0 / HD, RMS_EPS, ALU.mult, ALU.add))
                    dve.sem_inc(root_in, 1)
                    dve.wait_ge(root_out, r + 1)
                    link(V.reciprocal(s, s))
                    link(V.tensor_tensor(k, k, s3.unsqueeze(3).to_broadcast([nk, nb, 2, HD]), ALU.mult))
                    gb = gain[0:nk].unsqueeze(1).unsqueeze(1).to_broadcast([nk, nb, 2, HD])
                    link(V.tensor_tensor(k, k, gb, ALU.mult))
                    if r == 0:
                        for a in range(2):
                            link(V.tensor_copy(kdup[0:nk, :, a, :], k[:, 0]))
                        link(V.tensor_copy(vc_p[0:nk, :], kraw[0:nk, 0, 1, :]))
                        dve.sem_inc(normed, 1)
                        dve.wait_ge(kT_mm, 1)
                        link(V.tensor_copy(kcT_p[:], PS[:, 1536:1600].rearrange("p (g n) -> p g n", g=2)[:, :, 0:nk]))
                    else:
                        b0 = 4 * (r - 1)
                        link(V.tensor_copy(vc_s[0:nk, b0:b0 + 4, :], kraw[0:nk, :, 1, :]))
                        dve.sem_inc(normed, 1)
                        dve.wait_ge(kT_mm, r + 1)
                        link(V.tensor_copy(kcT_s[:, b0:b0 + 4, :],
                                           PS[:, 1536:2048].rearrange("p (b n) -> p b n", b=4)[:, :, 0:nk]))
                    dve.sem_inc(kT_out, 1)


def prompt_attention(nc, io, PS, sem, cst, kcT_p, vc_p):
    with ExitStack() as ctx:
        def t(name, shape, dt=F32):
            return ctx.enter_context(nc.sbuf_tensor(name, shape, dt))

        qrow = t("a_qrow", [P, 4, 512])
        krow = t("a_krow", [P, 2, 4, 2, 2, HD])
        vrow = t("a_vrow", [P, 2, 4, P])
        gate = t("a_gate", [P, 4, 3, 8])
        qT = t("a_qT", [P, 4, TPR])
        kT = t("a_kT", [P, 2, 2, TPR])
        E = t("a_E", [P, 2, 2, TPR])
        Ec = t("a_Ec", [P, 2, 16, NKC_P])
        pT = t("a_pT", [P, 2, 2, TPR])
        pcT = t("a_pcT", [32, 4, 8, P])
        cm, cs = t("a_cm", [P, 2, 16]), t("a_cs", [P, 2, 16])
        mx = t("a_mx", [P, 2, 2])
        sm = t("a_sm", [P, 2, 2])
        co = t("a_co", [P, 3, 2])
        ob = t("a_ob", [P, 4, 512])
        obT = t("a_obT", [P, 4, TPR])

        units = [(i, hh) for i in range(4) for hh in range(8)]
        N = len(units)
        rows_in, tr_mm, tr_out = sem("a_rows_in"), sem("a_tr_mm"), sem("a_tr_out")
        score_mm, masked, exped = sem("a_score_mm"), sem("a_masked"), sem("a_exped")
        c_mm, c_in, c_exp, c_ready = sem("a_c_mm"), sem("a_c_in"), sem("a_c_exp"), sem("a_c_ready")
        cT_mm, cT_out, co_mm, co_out = sem("a_cT_mm"), sem("a_cT_out"), sem("a_co_mm"), sem("a_co_out")
        pT_mm, pT_act, pT_dve = sem("a_pT_mm"), sem("a_pT_act"), sem("a_pT_dve")
        o_mm, o_out, ob_mm, ob_out = sem("a_o_mm"), sem("a_o_out"), sem("a_ob_mm"), sem("a_ob_out")
        dchain, stored = sem("a_dchain"), sem("a_stored")

        def psS(u, br):
            return PS[:, 1024 * (u % 2) + 512 * br:1024 * (u % 2) + 512 * br + 512]

        def psP(br):
            return PS[:, 2048 + 512 * br:2560 + 512 * br]

        def psO(u):
            return PS[:, 3072 + 512 * (u % 2):3072 + 512 * (u % 2) + 128].rearrange("p (b d) -> p b d", b=2)

        with nc.Block() as block:
            @block.sync
            def _(sp):
                sp.dma_start(qrow[:], io["q_dram"][0:TPR, :].rearrange("(i p) n -> p i n", p=P)).then_inc(rows_in, 16)
                for br, src in enumerate((io["kvs"], io["kvw"])):
                    rr = src[0:TPR, :].rearrange("(i p) n -> p i n", p=P)
                    for i in range(4):
                        for a in range(2):
                            sp.dma_start(krow[:, br, i, :, a, :], rr[:, i, 0:P].rearrange("p (g d) -> p g d", g=2)
                                         ).then_inc(rows_in, 16)
                    sp.dma_start(vrow[:, br], rr[:, :, P:256]).then_inc(rows_in, 16)
                sp.dma_start(gate[:], io["gate_dram"][0:TPR, :].rearrange("(i p) (b h) -> p i b h", p=P, b=3)).then_inc(rows_in, 16)
                sp.wait_ge(ob_out, 4)
                sp.dma_start(io["ob_dram"][:, :, 0:TPR], obT[:]).then_inc(stored, 16)
                sp.dma_start(io["win_s"][:, 0:508], io["win_cache"][:, TS:512]).then_inc(stored, 16)
                sp.dma_start(io["win_s"][:, 508:512], io["kvw"][TPR:T, :].rearrange("(b t) n -> b t n", b=NB)
                             ).then_inc(stored, 16)
                sp.wait_ge(stored, 48)

            n_in = 16 * 20

            @block.tensor
            def _(pe):
                M, X = nc.tensor.matmul, nc.tensor.transpose
                pe.wait_ge(rows_in, n_in)
                for j in range(8):
                    o = 512 * j
                    for i in range(4):
                        src = qrow[:, i, j * P:j * P + P] if j < 4 else \
                            krow[:, (j - 4) // 2, i, (j - 4) % 2].rearrange("p a d -> p (a d)")
                        last = X(PS[:, o + i * P:o + i * P + P], src, cst["ident"])
                    last.then_inc(tr_mm, 1)
                pe.wait_ge(tr_out, 8)
                for i, hh in units:
                    h = slice(64 * (hh % 2), 64 * (hh % 2) + 64)
                    o = 512 * (hh % 2) + NKC_P * (4 * i + hh // 2)
                    last = M(PS[:, o:o + NKC_P], qT[h, hh // 2, i * P:i * P + P], kcT_p[h, hh // 4, :],
                             start=True, stop=True)
                    if hh % 2:
                        last.then_inc(c_mm, 1)
                pe.wait_ge(c_ready, 1)
                for i in range(4):
                    for hh in range(8):
                        o = 1024 * i + P * hh
                        last = X(PS[0:NKC_P, o:o + P], Ec[:, hh % 2, 4 * i + hh // 2, :], cst["ident"])
                    last.then_inc(cT_mm, 1)
                pe.wait_ge(cT_out, 4)
                for u, (i, hh) in enumerate(units):
                    last = M(PS[:, HD * u:HD * u + HD], pcT[0:NKC_P, i, hh, :], vc_p[0:NKC_P, 64 * (hh // 4):64 * (hh // 4) + 64],
                             start=True, stop=True)
                last.then_inc(co_mm, 1)
                pe.wait_ge(co_out, 1)

                def scores(u):
                    i, hh = units[u]
                    h = slice(64 * (hh % 2), 64 * (hh % 2) + 64)
                    q = qT[h, hh // 2, i * P:i * P + P]
                    if u >= 2:
                        pe.wait_ge(exped, u - 1)
                    n = P * (i + 1)
                    for br in range(2):
                        last = M(psS(u, br)[:, 0:n], q, kT[h, br, hh // 4, 0:n], start=True, stop=True)
                    last.then_inc(score_mm, 1)

                def turn(u):
                    i, hh = units[u]
                    pe.wait_ge(exped, u + 1)
                    if u:
                        pe.wait_ge(pT_act, u)
                        pe.wait_ge(pT_dve, u)
                    for br in range(2):
                        for j in range(i + 1):
                            last = X(psP(br)[:, j * P:j * P + P], E[:, u % 2, br, j * P:j * P + P], cst["ident"])
                    last.then_inc(pT_mm, 1)

                def values(u):
                    i, hh = units[u]
                    g = slice(64 * (hh // 4), 64 * (hh // 4) + 64)
                    pe.wait_ge(pT_act, u + 1)
                    pe.wait_ge(pT_dve, u + 1)
                    if u >= 2:
                        pe.wait_ge(o_out, u - 1)
                    for br in range(2):
                        for j in range(i + 1):
                            last = M(psO(u)[:, br], pT[:, u % 2, br, j * P:j * P + P], vrow[:, br, j, g],
                                     start=(j == 0), stop=(j == i))
                    last.then_inc(o_mm, 1)
                    if hh == 7:
                        pe.wait_ge(o_out, u + 1)
                        pe.wait_ge(pT_act, u + 1)
                        if i < 3:
                            pe.wait_ge(pT_act, u + 2)
                            pe.wait_ge(pT_dve, u + 2)
                        for c in range(4):
                            last = X(psP(0)[:, c * P:c * P + P], ob[:, i, c * P:c * P + P], cst["ident"])
                        last.then_inc(ob_mm, 1)
                        pe.wait_ge(ob_out, i + 1)

                for k in range(N + 2):
                    if k < N:
                        scores(k)
                    if 1 <= k <= N:
                        turn(k - 1)
                    if k >= 2:
                        values(k - 2)

            @block.vector
            def _(dve):
                link = Chain(dve, dchain)
                V = nc.vector
                for j in range(1, 8, 2):
                    dve.wait_ge(tr_mm, j + 1)
                    dst = qT[:, j, :] if j < 4 else kT[:, (j - 4) // 2, (j - 4) % 2, :]
                    link(V.tensor_copy(dst, PS[:, 512 * j:512 * j + 512]))
                    dve.sem_inc(tr_out, 1)
                def tiles(ap):
                    return ap.rearrange("p (i h) n -> p i h n", i=4)

                neg, keep = (cst[n].rearrange("p (i n) -> p i n", i=4).unsqueeze(2).to_broadcast([P, 4, 4, NKC_P])
                             for n in ("cmpneg_p", "cmp_p"))
                dve.wait_ge(c_mm, 16)
                for par in range(2):
                    src = PS[:, 512 * par:512 * par + 16 * NKC_P].rearrange("p (u n) -> p u n", n=NKC_P)
                    link(V.tensor_tensor(tiles(Ec[:, par]), tiles(src), neg, ALU.add))
                link(V.reduce_max(cm[:], Ec[:], AX_X))
                link(V.tensor_tensor(Ec[:], Ec[:], cm[:].unsqueeze(3).to_broadcast([P, 2, 16, NKC_P]), ALU.subtract))
                dve.sem_inc(c_in, 1)
                dve.wait_ge(c_exp, 1)
                for par in range(2):
                    link(V.tensor_tensor(tiles(Ec[:, par]), tiles(Ec[:, par]), keep, ALU.mult))
                link(V.reduce_sum(cs[:], Ec[:], AX_X))
                link(V.tensor_scalar(cs[:], cs[:], 1e-30, None, ALU.max))
                link(V.reciprocal(cs[:], cs[:]))
                for par in range(2):
                    c3 = cs[:, par].rearrange("p (i h) -> p i h", i=4)
                    link(V.tensor_tensor(c3, c3, gate[:, :, 0, par:8:2], ALU.mult))
                link(V.tensor_tensor(Ec[:], Ec[:], cs[:].unsqueeze(3).to_broadcast([P, 2, 16, NKC_P]), ALU.mult))
                dve.sem_inc(c_ready, 1)
                for i in (1, 3):
                    dve.wait_ge(cT_mm, i + 1)
                    V.tensor_copy(pcT[0:NKC_P, i], PS[0:NKC_P, 1024 * i:1024 * i + 1024].rearrange("p (h t) -> p h t", h=8)
                                  ).then_inc(cT_out, 1)
                dve.wait_ge(co_mm, 1)
                link(V.tensor_copy(ob[:], PS[:, 0:2048].rearrange("p (i n) -> p i n", i=4)))
                dve.sem_inc(co_out, 1)

                def mask(u):
                    i, hh = units[u]
                    dve.wait_ge(score_mm, u + 1)
                    n = P * (i + 1)
                    for br in range(2):
                        s = psS(u, br)
                        link(V.tensor_tensor(s[:, n - P:n], s[:, n - P:n], cst["tri"], ALU.add))
                        link(V.reduce_max(mx[:, u % 2, br:br + 1], s[:, 0:n], AX_X))
                    V.tensor_scalar(mx[:, u % 2, :], mx[:, u % 2, :], -0.125, None, ALU.mult).then_inc(masked, 1)

                def weigh(u):
                    i, hh = units[u]
                    dve.wait_ge(exped, u + 1)
                    c = co[:, u % 3, :]
                    link(V.reciprocal(c, sm[:, u % 2, :]))
                    link(V.tensor_tensor(c, c, gate[:, i, 1:3, hh], ALU.mult))
                    dve.wait_ge(pT_mm, u + 1)
                    if u >= 2:
                        dve.wait_ge(o_mm, u - 1)
                    n = P * (i + 1)
                    V.tensor_copy(pT[:, u % 2, 1, 0:n], psP(1)[:, 0:n]).then_inc(pT_dve, 1)

                def gather(u):
                    i, hh = units[u]
                    dve.wait_ge(o_mm, u + 1)
                    c, o = co[:, u % 3, :], ob[:, i, hh * HD:hh * HD + HD]
                    link(V.scalar_tensor_tensor(out=o, in0=psO(u)[:, 0], scalar=c[:, 0:1], in1=o,
                                                op0=ALU.mult, op1=ALU.add))
                    V.scalar_tensor_tensor(out=o, in0=psO(u)[:, 1], scalar=c[:, 1:2], in1=o,
                                           op0=ALU.mult, op1=ALU.add).then_inc(o_out, 1)
                    dve.wait_ge(o_out, u + 1)

                for k in range(N + 2):
                    if k < N:
                        mask(k)
                    if 1 <= k <= N:
                        weigh(k - 1)
                    if k >= 2:
                        gather(k - 2)

            @block.scalar
            def _(act):
                A = nc.scalar.activation

                def ob_copy(i):
                    act.wait_ge(ob_mm, i + 1)
                    nc.scalar.activation(obT[:, :, i * P:i * P + P], psP(0).rearrange("p (c t) -> p c t", c=4),
                                         ACT.Copy).then_inc(ob_out, 1)

                for j in range(0, 8, 2):
                    act.wait_ge(tr_mm, j + 1)
                    dst = qT[:, j, :] if j < 4 else kT[:, (j - 4) // 2, (j - 4) % 2, :]
                    A(dst, PS[:, 512 * j:512 * j + 512], ACT.Copy).then_inc(tr_out, 1)
                act.wait_ge(c_in, 1)
                A(Ec[:], Ec[:], ACT.Exp, scale=0.125).then_inc(c_exp, 1)
                for i in (0, 2):
                    act.wait_ge(cT_mm, i + 1)
                    A(pcT[0:NKC_P, i], PS[0:NKC_P, 1024 * i:1024 * i + 1024].rearrange("p (h t) -> p h t", h=8), ACT.Copy
                      ).then_inc(cT_out, 1)
                for k in range(N + 1):
                    if k < N:
                        i, hh = units[k]
                        n = P * (i + 1)
                        act.wait_ge(masked, k + 1)
                        if k >= 2:
                            act.wait_ge(pT_mm, k - 1)
                            act.wait_ge(pT_dve, k - 1)
                        for br in range(2):
                            last = A(E[:, k % 2, br, 0:n], psS(k, br)[:, 0:n], ACT.Exp, bias=mx[:, k % 2, br:br + 1],
                                     scale=0.125, accum_out=sm[:, k % 2, br:br + 1])
                        last.then_inc(exped, 1)
                    if k >= 1:
                        u = k - 1
                        i, hh = units[u]
                        act.wait_ge(pT_mm, u + 1)
                        if u >= 2:
                            act.wait_ge(o_mm, u - 1)
                        A(pT[:, u % 2, 0, 0:P * (i + 1)], psP(0)[:, 0:P * (i + 1)], ACT.Copy).then_inc(pT_act, 1)
                        if u >= 1 and units[u - 1][1] == 7:
                            ob_copy(units[u - 1][0])
                ob_copy(3)


def sample_attention(nc, io, PS, sem, cst, kcT_s, vc_s):
    with ExitStack() as ctx:
        def t(name, shape, dt=F32):
            return ctx.enter_context(nc.sbuf_tensor(name, shape, dt))

        table = t("s_table", [1, NB * NPAGES], I32)
        kv = t("s_kv", [P, 4, NPAGES, 2, PAGE])
        wkv = t("s_wkv", [P, 4, 4, 2, P])
        qrow = t("s_qrow", [TSM, 512])
        nrow = t("s_nrow", [TSM, 2, 256])
        gate = t("s_gate", [TSM, 24])
        Q = t("s_Q", [P, NB, 32])
        nT = t("s_nT", [P, 2, TSM])
        gr = t("s_gr", [P, 24])
        g3 = t("s_g3", [P, 3])
        Es = t("s_Es", [P, PAST + TSM])
        Ew = t("s_Ew", [P, 512 + TSM])
        Ec = t("s_Ec", [P, 128])
        mx, sm = t("s_mx", [P, 3]), t("s_sm", [P, 3])
        pT = t("s_pT", [P, 20, P])
        nTp = t("s_nTp", [TSM, 2, P])
        pcT = t("s_pcT", [P, P])
        imp0, imp, top = t("s_imp0", [P, NSB]), t("s_imp", [P, NSB]), t("s_top", [P, 8])
        ot, o64 = t("s_ot", [P, P]), t("s_o64", [P, HD])
        obT = t("s_obT", [P, 4, TSM])

        rows_in, pages, win_in = sem("s_rows_in"), [sem("s_pages0"), sem("s_pages1")], sem("s_win_in")
        zeroed, prep_mm, prep_out = sem("s_zeroed"), sem("s_prep_mm"), sem("s_prep_out")
        small_mm, small_used, sel_mm, sel_read = sem("s_small_mm"), sem("s_small_used"), sem("s_sel_mm"), sem("s_sel_read")
        cexp_in, cexp_out, pc_ready = sem("s_cexp_in"), sem("s_cexp_out"), sem("s_pc_ready")
        pc_mm, pc_out, imp_mm, imp_out = sem("s_pc_mm"), sem("s_pc_out"), sem("s_imp_mm"), sem("s_imp_out")
        e_in, e_out, turn_mm, turn_out = sem("s_e_in"), sem("s_e_out"), sem("s_turn_mm"), sem("s_turn_out")
        o_mm, o_out, back_mm, back_out = sem("s_o_mm"), sem("s_o_out"), sem("s_back_mm"), sem("s_back_out")
        dchain, stored = sem("s_dchain"), sem("s_stored")
        NEWC, WNEWC, CMPC = 2048, 2048 + 64, 2048 + 128
        WINB, MISC, OB = 2560, 3072, 3584
        turns = [5, 5, 5, 5, 2]

        with nc.Block() as block:
            @block.sync
            def _(sp):
                sp.dma_start(table[:], io["page_table"]).then_inc(rows_in, 16)
                sp.dma_start(qrow[:], io["q_dram"][TPR:T, :]).then_inc(rows_in, 16)
                sp.dma_start(nrow[:, 0], io["kvs"][TPR:T, :]).then_inc(rows_in, 16)
                sp.dma_start(nrow[:, 1], io["kvw"][TPR:T, :]).then_inc(rows_in, 16)
                sp.dma_start(gate[:], io["gate_dram"][TPR:T, :]).then_inc(rows_in, 16)
                sp.wait_ge(rows_in, 80)
                for hf in range(2):
                    if hf:
                        sp.wait_ge(o_mm, 1)
                    for b in range(4):
                        sp.dma_start(wkv[:, b], io["win_kv"][4 * hf + b]).then_inc(win_in, 16)
                    load_pages(sp, table, lambda b, i: kv[:, b, bass.ds(i, 1)].rearrange("p a k t -> p (a k) t"),
                               io["slc_pool"], hf, pages[hf])
                sp.wait_ge(back_out, 2)
                sp.dma_start(io["ob_dram"][:, :, TPR:T], obT[:]).then_inc(stored, 16)
                sp.wait_ge(stored, 16)

            @block.tensor
            def _(pe):
                M, X = nc.tensor.matmul, nc.tensor.transpose
                id32 = cst["ident"][0:TSM, 0:TSM]
                pe.wait_ge(rows_in, 80)
                for c in range(4):
                    X(PS[:, 32 * c:32 * c + 32], qrow[:, c * P:c * P + P], id32)
                for br in range(2):
                    last = X(PS[:, 128 + 32 * br:160 + 32 * br], nrow[:, br, 0:P], id32)
                last.then_inc(prep_mm, 1)
                pe.wait_ge(prep_out, 1)
                for hf in range(2):
                    if hf:
                        pe.wait_ge(small_used, 1)
                        pe.wait_ge(o_out, 1)
                        pe.wait_ge(back_out, 1)
                    M(PS[:, MISC:MISC + 24], cst["rowtok"][0:TSM, hf * P:hf * P + P], gate[:], start=True, stop=True)
                    pe.wait_ge(win_in, 64 * (hf + 1))
                    for b in range(4):
                        r, q = slice(32 * b, 32 * b + 32), Q[:, 4 * hf + b, :]
                        M(PS[r, CMPC:CMPC + NKC_S], q, kcT_s[:, 4 * hf + b, :], start=True, stop=True)
                        M(PS[r, NEWC:NEWC + 32], q, nT[:, 0, :], start=True, stop=True)
                        M(PS[r, WNEWC:WNEWC + 32], q, nT[:, 1, :], start=True, stop=True)
                        last = M(PS[r, WINB:WINB + 512], q, wkv[:, b, :, 0, :], start=True, stop=True)
                    last.then_inc(small_mm, 1)
                    pe.wait_ge(pages[hf], 16 * 4 * NPAGES)
                    for b in range(4):
                        r, q = slice(32 * b, 32 * b + 32), Q[:, 4 * hf + b, :]
                        for c in range(4):
                            last = M(PS[r, 512 * c:512 * c + 512], q, kv[:, b, 4 * c:4 * c + 4, 0, :],
                                     start=True, stop=True)
                    last.then_inc(sel_mm, 1)
                    pe.wait_ge(pc_ready, hf + 1)
                    X(PS[0:NKC_S, MISC:MISC + P], Ec[:, 0:NKC_S], cst["ident"]).then_inc(pc_mm, 1)
                    pe.wait_ge(pc_out, hf + 1)
                    M(PS[:, MISC + 128:MISC + 128 + NSB], pcT[0:NKC_S, :], cst["overlap"][0:NKC_S, :],
                      start=True, stop=True).then_inc(imp_mm, 1)
                    pe.wait_ge(imp_out, 2 * hf + 1)
                    M(PS[:, MISC + 192:MISC + 192 + NSB], cst["sumheads"], imp0[:], start=True, stop=True).then_inc(imp_mm, 1)
                    pe.wait_ge(e_out, hf + 1)
                    k = 0
                    for rnd, n in enumerate(turns):
                        at = hf * 5 + rnd
                        o = 1024 * (rnd % 2)
                        if rnd >= 2:
                            pe.wait_ge(turn_out, at - 1)
                        for j in range(n):
                            if rnd == 4:
                                src, w = ((Es, PAST), (Ew, 512))[j]
                                last = X(PS[0:TSM, o + j * P:o + j * P + P], src[:, w:w + TSM], cst["ident"])
                            else:
                                src = Es[:, k * P:k * P + P] if k < 16 else Ew[:, (k - 16) * P:(k - 15) * P]
                                last = X(PS[:, o + j * P:o + j * P + P], src, cst["ident"])
                                k += 1
                        last.then_inc(turn_mm, 1)
                    pe.wait_ge(turn_out, 5 * hf + 5)
                    for b in range(4):
                        r = slice(32 * b, 32 * b + 32)
                        o = OB
                        for c in range(16):
                            M(PS[r, o:o + P], pT[:, c, r], kv[:, b, c, 1, :], start=(c == 0), stop=False)
                        M(PS[r, o:o + P], nTp[:, 0, r], nrow[:, 0, P:256], start=False, stop=True)
                        o = OB + P
                        for c in range(4):
                            M(PS[r, o:o + P], pT[:, 16 + c, r], wkv[:, b, c, 1, :], start=(c == 0), stop=False)
                        M(PS[r, o:o + P], nTp[:, 1, r], nrow[:, 1, P:256], start=False, stop=True)
                        o = OB + 2 * P
                        last = M(PS[r, o:o + P], pcT[0:NKC_S, r], vc_s[0:NKC_S, 4 * hf + b, :], start=True, stop=True)
                    last.then_inc(o_mm, 1)
                    pe.wait_ge(o_out, hf + 1)
                    X(PS[0:HD, MISC + 256:MISC + 384], o64[:], cst["ident"]).then_inc(back_mm, 1)

            @block.scalar
            def _(act):
                A = nc.scalar.activation
                for hf in range(2):
                    act.wait_ge(cexp_in, hf + 1)
                    A(Ec[:, 0:NKC_S], Ec[:, 0:NKC_S], ACT.Exp, bias=mx[:, 0:1], scale=0.125,
                      accum_out=sm[:, 0:1]).then_inc(cexp_out, 1)
                    act.wait_ge(e_in, hf + 1)
                    A(Es[:], Es[:], ACT.Exp, bias=mx[:, 1:2], scale=0.125, accum_out=sm[:, 1:2])
                    A(Ew[:], Ew[:], ACT.Exp, bias=mx[:, 2:3], scale=0.125, accum_out=sm[:, 2:3]).then_inc(e_out, 1)

            @block.vector
            def _(dve):
                link = Chain(dve, dchain)
                V = nc.vector
                link(V.memset(Q[:], 0.0))
                dve.wait_ge(prep_mm, 1)
                for hh in range(8):
                    g, par = hh // 4, hh % 2
                    src = PS[64 * par:64 * par + 64, 32 * (hh // 2):32 * (hh // 2) + 32]
                    link(V.tensor_copy(Q[64 * g:64 * g + 64, :, g * 16 + hh % 4 * 4:g * 16 + hh % 4 * 4 + 4],
                                       src.rearrange("p (b t) -> p b t", t=TS)))
                link(V.tensor_copy(nT[:], PS[:, 128:192].rearrange("p (k t) -> p k t", k=2)))
                dve.sem_inc(prep_out, 1)
                for hf in range(2):
                    new = cst["new_s"][:, hf * TSM:hf * TSM + TSM]
                    dve.wait_ge(small_mm, hf + 1)
                    link(V.tensor_tensor(gr[:], PS[:, MISC:MISC + 24], cst["rowhead"], ALU.mult))
                    link(V.reduce_sum(g3[:], gr[:].rearrange("p (b h) -> p b h", b=3), AX_X))
                    link(V.tensor_copy(Ec[:, 0:NKC_S], PS[:, CMPC:CMPC + NKC_S]))
                    link(V.reduce_max(mx[:, 0:1], Ec[:, 0:NKC_S], AX_X))
                    link(V.tensor_scalar(mx[:, 0:1], mx[:, 0:1], -0.125, None, ALU.mult))
                    dve.sem_inc(cexp_in, 1)
                    link(V.tensor_tensor(Ew[:, 0:TS], PS[:, WINB:WINB + TS], cst["win_old"], ALU.add))
                    link(V.tensor_copy(Ew[:, TS:512], PS[:, WINB + TS:WINB + 512]))
                    link(V.tensor_tensor(Ew[:, 512:512 + TSM], PS[:, WNEWC:WNEWC + TSM], new, ALU.add))
                    link(V.reduce_max(mx[:, 2:3], Ew[:], AX_X))
                    dve.wait_ge(cexp_out, hf + 1)
                    link(V.reciprocal(sm[:, 0:1], sm[:, 0:1]))
                    link(V.tensor_scalar(Ec[:, 0:NKC_S], Ec[:, 0:NKC_S], sm[:, 0:1], None, ALU.mult))
                    dve.sem_inc(pc_ready, 1)
                    dve.wait_ge(pc_mm, hf + 1)
                    link(V.tensor_copy(pcT[0:NKC_S, :], PS[0:NKC_S, MISC:MISC + P]))
                    dve.sem_inc(pc_out, 1)
                    dve.wait_ge(imp_mm, 2 * hf + 1)
                    link(V.tensor_copy(imp0[:], PS[:, MISC + 128:MISC + 128 + NSB]))
                    dve.sem_inc(imp_out, 1)
                    dve.wait_ge(imp_mm, 2 * hf + 2)
                    link(V.tensor_copy(imp[:], PS[:, MISC + 192:MISC + 192 + NSB]))
                    dve.sem_inc(imp_out, 1)
                    link(V.memset(imp[:, 0:1], 1e6))
                    link(V.memset(imp[:, NSB - 2:NSB], 1e6))
                    for _ in range(2):
                        link(V.max(top[:], imp[:]))
                        link(V.match_replace(imp[:], top[:], imp[:], -1.0))
                    link(V.tensor_scalar(imp[:], imp[:], -1.0, NEG, ALU.not_equal, ALU.mult))
                    dve.wait_ge(sel_mm, hf + 1)
                    link(V.tensor_tensor(Es[:, 0:PAST].rearrange("p (j t) -> p j t", t=HD),
                                         PS[:, 0:PAST].rearrange("p (j t) -> p j t", t=HD),
                                         imp[:, 0:NSB - 1].unsqueeze(2).to_broadcast([P, NSB - 1, HD]), ALU.add))
                    link(V.tensor_tensor(Es[:, PAST:PAST + TSM], PS[:, NEWC:NEWC + TSM], new, ALU.add))
                    dve.sem_inc(small_used, 1)
                    link(V.reduce_max(mx[:, 1:2], Es[:], AX_X))
                    link(V.tensor_scalar(mx[:, 1:3], mx[:, 1:3], -0.125, None, ALU.mult))
                    dve.sem_inc(e_in, 1)
                    k = 0
                    for rnd, n in enumerate(turns):
                        dve.wait_ge(turn_mm, hf * 5 + rnd + 1)
                        o = 1024 * (rnd % 2)
                        if rnd == 4:
                            link(V.tensor_copy(nTp[:], PS[0:TSM, o:o + 2 * P].rearrange("p (k r) -> p k r", k=2)))
                        else:
                            link(V.tensor_copy(pT[:, k:k + n, :], PS[:, o:o + n * P].rearrange("p (k r) -> p k r", k=n)))
                            k += n
                        dve.sem_inc(turn_out, 1)
                    link(V.reciprocal(sm[:, 1:3], sm[:, 1:3]))
                    link(V.tensor_tensor(g3[:, 1:3], g3[:, 1:3], sm[:, 1:3], ALU.mult))
                    dve.wait_ge(o_mm, hf + 1)
                    link(V.tensor_scalar(ot[:], PS[:, OB + 2 * P:OB + 3 * P], g3[:, 0:1], None, ALU.mult))
                    for j in range(2):
                        link(V.scalar_tensor_tensor(out=ot[:], in0=PS[:, OB + j * P:OB + j * P + P],
                                                    scalar=g3[:, 1 + j:2 + j], in1=ot[:], op0=ALU.mult, op1=ALU.add))
                    link(V.tensor_scalar(o64[:], ot[:, 0:HD], cst["grp"][:, 0:1], None, ALU.mult))
                    link(V.scalar_tensor_tensor(out=o64[:], in0=ot[:, HD:P], scalar=cst["grp"][:, 1:2], in1=o64[:],
                                                op0=ALU.mult, op1=ALU.add))
                    dve.sem_inc(o_out, 1)
                    dve.wait_ge(back_mm, hf + 1)
                    src = PS[0:HD, MISC + 256:MISC + 384].rearrange("p (b c a t) -> p a c b t", b=4, c=4, a=2)
                    for par in range(2):
                        for c in range(4):
                            dst = obT[64 * par:64 * par + 64, c, 16 * hf:16 * hf + 16].rearrange("p (b t) -> p b t", t=TS)
                            link(V.tensor_copy(dst, src[:, par, c]))
                    dve.sem_inc(back_out, 1)


def merge_and_route(nc, io, PS, sem, cst, x1, wk):
    with ExitStack() as ctx:
        def t(name, shape, dt=F32, c=ctx):
            return c.enter_context(nc.sbuf_tensor(name, shape, dt))

        P = 128
        hT = t("m_hT", [P, KC, T])
        oT = t("m_oT", [P, 2, 4, T])
        wg = t("m_wg", [P, 2, 2, KC, P])
        wb = t("m_wb", [P, 2, 2, 4, P])
        mT = t("m_mT", [P, KC, T])
        sg = t("m_sg", [P, 2, T])
        wo = t("m_wo", [P, KC, D // 2])
        ss = t("m_ss", [P, 5])
        n2 = t("m_n2", [P, D])
        h2 = t("m_h2", [P, D])
        wr = t("m_wr", [P, KC, 36])
        br = t("m_br", [P, 36])
        lg = t("m_lg", [P, 5, 36])
        h2T = hT
        gl, g8, gi = t("m_gl", [P, 5, 8]), t("m_g8", [P, 5, 8]), t("m_gi", [P, 5, 8], U32)
        gf, em = t("m_gf", [P, 5, 1]), t("m_em", [P, 5, NE])
        e8, ei, ef = t("m_e8", [P, 5, 8]), t("m_ei", [P, 5, 8], U32), t("m_ef", [P, 5, 2])
        ge, gs, dd = t("m_ge", [P, 5, 4]), t("m_gs", [P, 5]), t("m_dd", [P, 5, 1])
        oh, ohs = t("m_oh", [P, 2, 5, NE]), t("m_ohs", [P, 5, NE])
        rk, kk, ad, tm = t("m_rk", [P, 5, NE]), t("m_kk", [P, 5, NE]), t("m_ad", [P, 5, NE]), t("m_tm", [P, 5, NE])
        cnt, nov, inc, exc = t("m_cnt", [P, NE]), t("m_nov", [P, NE]), t("m_inc", [P, NE]), t("m_exc", [P, NE])
        addr, addri = t("m_addr", [P, 5, 2]), t("m_addri", [P, 5, 2], I32)
        ov, ovs, ids = t("m_ov", [P, NOV, NE]), t("m_ovs", [P, NOV]), t("m_ids", [P, NBLK], I32)
        slotv = t("m_slotv", [P, 10], I32)
        big = t("m_big", [P, NBLK], I32)

        ins, small_in = sem("m_ins"), sem("m_small_in")
        wg_in, wo_in = [sem("m_wg_in0"), sem("m_wg_in1")], sem("m_wo_in")
        gates_mm, sig_out, merged = sem("m_gates_mm"), sem("m_sig_out"), sem("m_merged")
        out_mm, x1_ready = sem("m_out_mm"), sem("m_x1_ready")
        sq_out, root_in, root_out = sem("m_sq_out"), sem("m_root_in"), sem("m_root_out")
        h2_ready, h2T_mm, h2T_out, h2_stored = sem("m_h2_ready"), sem("m_h2T_mm"), sem("m_h2T_out"), sem("m_h2_stored")
        lg_mm, lg_out = sem("m_lg_mm"), sem("m_lg_out")
        exp_in, exp_out = sem("m_exp_in"), sem("m_exp_out")
        oh_ready, rank_mm, addr_ready, big_ready = sem("m_oh_ready"), sem("m_rank_mm"), sem("m_addr_ready"), sem("m_big_ready")
        filled, scattered, ids_out, dchain = sem("m_filled"), sem("m_scattered"), sem("m_ids_out"), sem("m_dchain")
        rows = [min(P, T - i * P) for i in range(5)]

        def gate_ps(k):
            return PS[:, 1024 * k:1024 * k + T]

        with nc.Block() as block:
            @block.sync
            def _(sp):
                sp.dma_start(hT[:], io["h_dram"]).then_inc(ins, 16)
                sp.dma_start(oT[:, 0], io["oa_dram"]).then_inc(ins, 16)
                sp.dma_start(oT[:, 1], io["ob_dram"]).then_inc(ins, 16)
                for j in range(KC):
                    if j >= 2:
                        sp.wait_ge(gates_mm, j - 1)
                    for k in range(2):
                        sp.dma_start(wg[:, j % 2, k], io["w_gates"][k, j]).then_inc(wg_in[j % 2], 16)
                        sp.dma_start(wb[:, j % 2, k], io["w_branch"][k, j]).then_inc(wg_in[j % 2], 16)
                for hf in range(2):
                    if hf:
                        sp.wait_ge(out_mm, 5)
                    sp.dma_start(wo[:], io["w_out"][hf]).then_inc(wo_in, 16)
                for i in range(5):
                    sp.wait_ge(h2_ready, i + 1)
                    sp.dma_start(io["h2_dram"][i * P:i * P + rows[i], :], h2[0:rows[i], :]).then_inc(h2_stored, 16)
                sp.wait_ge(ids_out, 1)
                sp.dma_start(io["ids_dram"], ids[0:1, :]).then_inc(h2_stored, 16)
                sp.wait_ge(h2_stored, 16 * 6)

            @block.gpsimd
            def _(pool):
                pool.dma_start(n2[:], io["norm2_rows"]).then_inc(small_in, 16)
                pool.dma_start(wr[:], io["w_route"]).then_inc(small_in, 16)
                pool.dma_start(br[:], io["b_route"]).then_inc(small_in, 16)
                for i in range(5):
                    pool.dma_start(x1[0:rows[i], i, :], io["x"][i * P:i * P + rows[i], :]).then_inc(small_in, 16)
                nc.gpsimd.memset(big[:], 1 << 20).then_inc(big_ready, 1)
                pool.wait_ge(big_ready, 1)
                pool.dma_start(io["slots_dram"].rearrange("(p n) a -> p (n a)", n=NBLK), big[:]).then_inc(filled, 16)
                pool.wait_ge(filled, 16)
                pool.wait_ge(addr_ready, 1)
                for i in range(5):
                    for k in range(2):
                        pool.indirect_dma_start(io["slots_dram"],
                                                bass.IndirectOffsetOnAxis(ap=addri[0:rows[i], i, k:k + 1], axis=0),
                                                slotv[0:rows[i], 2 * i + k:2 * i + k + 1], None).then_inc(scattered, 16)
                pool.wait_ge(scattered, 160)

            @block.tensor
            def _(pe):
                M = nc.tensor.matmul
                pe.wait_ge(ins, 48)
                for j in range(KC):
                    pe.wait_ge(wg_in[j % 2], 64 * (j // 2 + 1))
                    if j:
                        pe.wait_ge(merged, j)
                    for k in range(2):
                        for ns in (slice(0, 512), slice(512, T)):
                            for c in range(KC):
                                M(gate_ps(k)[:, ns], wg[:, j % 2, k, c, :], hT[:, c, ns], start=(c == 0), stop=(c == KC - 1))
                            for c in range(4):
                                last = M(gate_ps(2 + k)[:, ns], wb[:, j % 2, k, c, :], oT[:, k, c, ns],
                                         start=(c == 0), stop=(c == 3))
                    last.then_inc(gates_mm, 1)
                pe.wait_ge(merged, KC)
                for hf in range(2):
                    pe.wait_ge(wo_in, 16 * (hf + 1))
                    for i in range(5):
                        n = 5 * hf + i
                        if n >= 4:
                            pe.wait_ge(x1_ready, n - 3)
                        for c in range(KC):
                            last = M(PS[0:rows[i], 512 * (n % 4):512 * (n % 4) + 512], mT[:, c, i * P:i * P + rows[i]],
                                     wo[:, c, :], start=(c == 0), stop=(c == KC - 1))
                        last.then_inc(out_mm, 1)
                pe.wait_ge(small_in, 16 * 8)
                for i in range(5):
                    pe.wait_ge(h2_ready, i + 1)
                    if i:
                        pe.wait_ge(h2T_out, i)
                    for c in range(KC):
                        last = nc.tensor.transpose(PS[:, 2048 + c * P:2048 + c * P + rows[i]], h2[0:rows[i], c * P:c * P + P],
                                                   cst["ident"][0:rows[i], 0:rows[i]])
                    last.then_inc(h2T_mm, 1)
                pe.wait_ge(h2T_out, 5)
                for i in range(5):
                    for c in range(KC):
                        last = M(PS[0:rows[i], 3072 + 64 * i:3072 + 64 * i + 36], h2T[:, c, i * P:i * P + rows[i]],
                                 wr[:, c, :], start=(c == 0), stop=(c == KC - 1))
                last.then_inc(lg_mm, 1)
                pe.wait_ge(oh_ready, 1)
                for i in range(5):
                    for i2 in range(i + 1):
                        M(PS[0:rows[i], 3584 + 32 * i:3616 + 32 * i],
                          cst["ones"][0:rows[i2], 0:rows[i]] if i2 < i else cst["before"][0:rows[i2], 0:rows[i]],
                          ohs[0:rows[i2], i2, :], start=(i2 == 0), stop=(i2 == i))
                for i in range(5):
                    last = M(PS[:, 3584 + 192:3584 + 224], cst["ones"][0:rows[i], :], ohs[0:rows[i], i, :],
                             start=(i == 0), stop=(i == 4))
                last.then_inc(rank_mm, 1)

            @block.scalar
            def _(act):
                A = nc.scalar.activation
                for j in range(KC):
                    act.wait_ge(gates_mm, j + 1)
                    A(sg[:, 0, :], gate_ps(0), ACT.Sigmoid).then_inc(sig_out, 1)
                    A(sg[:, 1, :], gate_ps(1), ACT.Sigmoid).then_inc(sig_out, 1)
                    act.wait_ge(merged, j + 1)
                act.wait_ge(root_in, 1)
                for i in range(5):
                    r = rows[i]
                    A(h2[0:r, :], x1[0:r, i, :], ACT.Square, accum_out=ss[0:r, i:i + 1]).then_inc(sq_out, 1)
                    act.wait_ge(sq_out, i + 1)
                act.wait_ge(root_in, 2)
                A(ss[:], ss[:], ACT.Sqrt).then_inc(root_out, 1)
                for i in range(5):
                    act.wait_ge(h2T_mm, i + 1)
                    A(h2T[:, :, i * P:i * P + rows[i]],
                      PS[:, 2048:3072].rearrange("p (c t) -> p c t", c=KC)[:, :, 0:rows[i]], ACT.Copy).then_inc(h2T_out, 1)
                act.wait_ge(exp_in, 1)
                A(ge[:], ge[:], ACT.Exp)
                A(dd[:], dd[:], ACT.Exp).then_inc(exp_out, 1)

            @block.vector
            def _(dve):
                link = Chain(dve, dchain)
                V = nc.vector
                link(V.memset(ss[:], 1.0))
                link(V.memset(gl[:], NEG))
                link(V.memset(lg[:], 0.0))
                for j in range(KC):
                    dve.wait_ge(sig_out, 2 * j + 2)
                    for k in range(2):
                        link(V.tensor_tensor(sg[:, k], sg[:, k], gate_ps(2 + k), ALU.mult))
                    V.tensor_tensor(mT[:, j, :], sg[:, 0], sg[:, 1], ALU.add).then_inc(merged, 1)
                dve.wait_ge(small_in, 16 * 8)
                for n in range(10):
                    hf, i = n // 5, n % 5
                    dve.wait_ge(out_mm, n + 1)
                    xs = x1[0:rows[i], i, 512 * hf:512 * hf + 512]
                    V.tensor_tensor(xs, xs, PS[0:rows[i], 512 * (n % 4):512 * (n % 4) + 512], ALU.add).then_inc(x1_ready, 1)
                dve.wait_ge(x1_ready, 10)
                dve.sem_inc(root_in, 1)
                dve.wait_ge(sq_out, 5)
                link(V.tensor_scalar(ss[:], ss[:], 1.0 / D, RMS_EPS, ALU.mult, ALU.add))
                dve.sem_inc(root_in, 1)
                dve.wait_ge(root_out, 1)
                link(V.reciprocal(ss[:], ss[:]))
                for i in range(5):
                    if i:
                        dve.wait_ge(h2T_mm, i)
                        dve.wait_ge(h2_stored, 16 * i)
                    V.scalar_tensor_tensor(out=h2[0:rows[i], :], in0=x1[0:rows[i], i, :], scalar=ss[0:rows[i], i:i + 1],
                                           in1=n2[0:rows[i], :], op0=ALU.mult, op1=ALU.mult).then_inc(h2_ready, 1)
                dve.wait_ge(lg_mm, 1)
                for i in range(5):
                    link(V.tensor_tensor(lg[0:rows[i], i, :], PS[0:rows[i], 3072 + 64 * i:3072 + 64 * i + 36],
                                         br[0:rows[i], :], ALU.add))
                link(V.tensor_copy(gl[:, :, 0:4], lg[:, :, 0:4]))
                for i in range(5):
                    link(V.max(g8[:, i, :], gl[:, i, :]))
                    link(V.max_index(gi[:, i, :], g8[:, i, :], gl[:, i, :]))
                link(V.tensor_copy(gf[:], gi[:, :, 0:1]))
                link(V.tensor_tensor(ge[:], gl[:, :, 0:4], g8[:, :, 0:1].to_broadcast([P, 5, 4]), ALU.subtract))
                eg = cst["egroup"].unsqueeze(1).to_broadcast([P, 5, NE])
                link(V.tensor_tensor(em[:], eg, gf[:].to_broadcast([P, 5, NE]), ALU.not_equal))
                link(V.scalar_tensor_tensor(out=em[:], in0=em[:], scalar=NEG, in1=lg[:, :, 4:36], op0=ALU.mult, op1=ALU.add))
                for i in range(5):
                    link(V.max(e8[:, i, :], em[:, i, :]))
                    link(V.max_index(ei[:, i, :], e8[:, i, :], em[:, i, :]))
                link(V.tensor_copy(ef[:], ei[:, :, 0:2]))
                link(V.tensor_tensor(dd[:], e8[:, :, 1:2], e8[:, :, 0:1], ALU.subtract))
                dve.sem_inc(exp_in, 1)
                ie = cst["iota_e"].unsqueeze(1).to_broadcast([P, 5, NE])
                for k in range(2):
                    link(V.tensor_tensor(oh[:, k], ie, ef[:, :, k:k + 1].to_broadcast([P, 5, NE]), ALU.is_equal))
                link(V.tensor_tensor(ohs[:], oh[:, 0], oh[:, 1], ALU.add))
                dve.sem_inc(oh_ready, 1)
                dve.wait_ge(exp_out, 1)
                link(V.reduce_sum(gs[:], ge[:], AX_X))
                link(V.reciprocal(gs[:], gs[:]))
                link(V.tensor_scalar(wk[:, :, 0:1], dd[:], 1.0, None, ALU.add))
                link(V.reciprocal(wk[:, :, 0:1], wk[:, :, 0:1]))
                link(V.tensor_tensor(wk[:, :, 0:1], wk[:, :, 0:1], gs[:].unsqueeze(2), ALU.mult))
                link(V.tensor_tensor(wk[:, :, 1:2], wk[:, :, 0:1], dd[:], ALU.mult))
                dve.wait_ge(rank_mm, 1)
                link(V.memset(rk[:], 0.0))
                for i in range(5):
                    link(V.tensor_copy(rk[0:rows[i], i, :], PS[0:rows[i], 3584 + 32 * i:3616 + 32 * i]))
                link(V.tensor_copy(cnt[:], PS[:, 3584 + 192:3584 + 224]))
                steps = -(-T // CAP) - 1
                link(V.tensor_scalar(nov[:], cnt[:], float(CAP), None, ALU.is_gt))
                link(V.tensor_scalar(kk[:], rk[:], float(CAP), None, ALU.is_ge))
                for j in range(2, steps + 1):
                    link(V.scalar_tensor_tensor(out=nov[:], in0=cnt[:], scalar=float(CAP * j), in1=nov[:],
                                                op0=ALU.is_gt, op1=ALU.add))
                    link(V.scalar_tensor_tensor(out=kk[:], in0=rk[:], scalar=float(CAP * j), in1=kk[:],
                                                op0=ALU.is_ge, op1=ALU.add))
                link(V.tensor_tensor_scan(inc[:], cst["ones"][:, 0:NE], nov[:], 0.0, ALU.mult, ALU.add))
                link(V.tensor_tensor(exc[:], inc[:], nov[:], ALU.subtract))
                link(V.scalar_tensor_tensor(out=rk[:], in0=kk[:], scalar=-float(CAP), in1=rk[:], op0=ALU.mult, op1=ALU.add))
                link(V.scalar_tensor_tensor(out=tm[:], in0=kk[:], scalar=float(NE - 1),
                                            in1=exc[:].unsqueeze(1).to_broadcast([P, 5, NE]), op0=ALU.add, op1=ALU.add))
                link(V.tensor_tensor(tm[:], tm[:], ie, ALU.subtract))
                link(V.scalar_tensor_tensor(out=tm[:], in0=kk[:], scalar=0.5, in1=tm[:], op0=ALU.is_gt, op1=ALU.mult))
                link(V.tensor_tensor(tm[:], tm[:], ie, ALU.add))
                link(V.scalar_tensor_tensor(out=ad[:], in0=rk[:], scalar=float(NBLK), in1=tm[:], op0=ALU.mult, op1=ALU.add))
                for k in range(2):
                    link(V.tensor_tensor(tm[:], oh[:, k], ad[:], ALU.mult))
                    link(V.reduce_sum(addr[:, :, k:k + 1].rearrange("p a b -> p (a b)"), tm[:], AX_X))
                link(V.tensor_copy(addri[:], addr[:]))
                link(V.tensor_copy(slotv[:], cst["slotval"]))
                dve.sem_inc(addr_ready, 1)
                link(V.tensor_tensor(ov[:], inc[:].unsqueeze(1).to_broadcast([P, NOV, NE]),
                                     cst["iota_o"].unsqueeze(2).to_broadcast([P, NOV, NE]), ALU.is_le))
                link(V.reduce_sum(ovs[:], ov[:], AX_X))
                link(V.tensor_scalar(ovs[:], ovs[:], float(NE - 1), None, ALU.min))
                link(V.tensor_copy(ids[:, NE:NBLK], ovs[:]))
                link(V.tensor_copy(ids[:, 0:NE], cst["iota_e"]))
                dve.sem_inc(ids_out, 1)


def experts(nc, io, PS, sem, cst, x1, wk):
    with ExitStack() as ctx:
        def t(name, shape, dt=F32):
            return ctx.enter_context(nc.sbuf_tensor(name, shape, dt))

        DE = D // 2
        FC = DE // P
        wg, wu, wd = t("e_wg", [P, 2, KC, DE]), t("e_wu", [P, 2, KC, DE]), t("e_wd", [P, 2, FC, D])
        xe = t("e_xe", [P, 2, D])
        xT = t("e_xT", [P, 2, KC, P])
        sg = t("e_sg", [P, 2, DE])
        hT = t("e_hT", [P, 2, FC, P])
        ye = t("e_ye", [P, 2, D])
        slots = t("e_slots", [P, NBLK], I32)
        toks = t("e_toks", [P, NBLK], I32)
        ids = t("e_ids", [1, NBLK], I32)
        gi, si = t("e_gi", [P, 2], I32), t("e_si", [P, 2], I32)

        tables_in, toks_ready, zeroed = sem("e_tables_in"), sem("e_toks_ready"), sem("e_zeroed")
        g_in, u_in, d_in = ([sem(f"e_{n}_in{b}") for b in range(2)] for n in "gud")
        idx_ready, x_in, y_stored = sem("e_idx_ready"), [sem("e_x_in0"), sem("e_x_in1")], [sem("e_y_st0"), sem("e_y_st1")]
        xT_mm, xT_act, xT_dve = sem("e_xT_mm"), sem("e_xT_act"), sem("e_xT_dve")
        gate_mm, up_mm, silu, h_ready = sem("e_gate_mm"), sem("e_up_mm"), sem("e_silu"), sem("e_h_ready")
        hT_mm, hT_out, y_mm, y_act, y_dve = sem("e_hT_mm"), sem("e_hT_out"), sem("e_y_mm"), sem("e_y_act"), sem("e_y_dve")
        paced = sem("e_paced")
        HALF = NBLK // 2

        with nc.Block() as block:
            @block.sync
            def _(sp):
                sp.dma_start(ids[:], io["ids_dram"]).then_inc(tables_in, 16)
                sp.dma_start(slots[:], io["slots_dram"].rearrange("(p n) a -> p (n a)", n=NBLK)).then_inc(tables_in, 16)
                sp.wait_ge(tables_in, 32)

                def load(i, b):
                    e = sp.value_load(ids[0:1, bass.ds(2 * i + b, 1)], min_val=0, max_val=NE - 1)
                    for w, src, arrived in ((wg, io["w_exp_gate"], g_in), (wu, io["w_exp_up"], u_in), (wd, io["w_exp_down"], d_in)):
                        sp.dma_start(w[:, b], src[bass.ds(e, 1)].rearrange("a (p c) n -> p (a c) n", p=P)
                                     ).then_inc(arrived[b], 16)

                load(0, 0)
                load(0, 1)
                with sp.Fori(1, HALF) as i:
                    for b in range(2):
                        sp.wait_ge(y_mm, 2 * i + (b - 1))
                        load(i, b)

            @block.gpsimd
            def _(pool):
                pool.wait_ge(tables_in, 32)
                nc.gpsimd.memset(xe[:], 0.0).then_inc(zeroed, 1)
                pool.wait_ge(toks_ready, 1)
                pool.wait_ge(zeroed, 1)

                def wait(on, value):
                    pool.wait_ge(on, value)
                    pool.sem_inc(paced, 1)

                def gather(i, b, n):
                    nc.gpsimd.tensor_copy(gi[:, b:b + 1], toks[:, bass.ds(2 * i + b, 1)]).then_inc(idx_ready, 1)
                    wait(idx_ready, n)
                    pool.indirect_dma_start(xe[:, b, :], None, io["h2_dram"],
                                            bass.IndirectOffsetOnAxis(ap=gi[:, b:b + 1], axis=0),
                                            bounds_check=T - 1, oob_is_err=False).then_inc(x_in[b], 16)

                def scatter(i, b, n):
                    nc.gpsimd.tensor_copy(si[:, b:b + 1], slots[:, bass.ds(2 * i + b, 1)]).then_inc(idx_ready, 1)
                    wait(idx_ready, n)
                    pool.indirect_dma_start(io["y2_dram"], bass.IndirectOffsetOnAxis(ap=si[:, b:b + 1], axis=0),
                                            ye[:, b, :], None,
                                            bounds_check=2 * T - 1, oob_is_err=False).then_inc(y_stored[b], 16)

                gather(0, 0, 1)
                gather(0, 1, 2)
                with pool.Fori(0, HALF - 1) as i:
                    for b in range(2):
                        wait(xT_mm, 2 * i + (b + 1))
                        gather(i + 1, b, 4 * i + (2 * b + 3))
                        wait(y_act, 2 * i + (b + 1))
                        wait(y_dve, 2 * i + (b + 1))
                        scatter(i, b, 4 * i + (2 * b + 4))
                for b in range(2):
                    pool.wait_ge(y_act, 2 * (HALF - 1) + b + 1)
                    pool.wait_ge(y_dve, 2 * (HALF - 1) + b + 1)
                    scatter(HALF - 1, b, 4 * (HALF - 1) + b + 3)
                for b in range(2):
                    pool.wait_ge(y_stored[b], 16 * HALF)

            @block.tensor
            def _(pe):
                M, X = nc.tensor.matmul, nc.tensor.transpose

                def body(i, b, first):
                    n = 2 * i + b
                    pe.wait_ge(x_in[b], 16 * i + 16)
                    if not first:
                        pe.wait_ge(xT_act, n)
                        pe.wait_ge(xT_dve, n)
                    for c in range(KC):
                        last = X(PS[:, c * P:c * P + P], xe[:, b, c:D:KC], cst["ident"])
                    last.then_inc(xT_mm, 1)
                    pe.wait_ge(xT_act, n + 1)
                    pe.wait_ge(xT_dve, n + 1)
                    pe.wait_ge(g_in[b], 16 * i + 16)
                    if not first:
                        pe.wait_ge(h_ready, n)
                    for c in range(KC):
                        last = M(PS[:, 1024:1536], xT[:, b, c, :], wg[:, b, c, :], start=(c == 0), stop=(c == KC - 1))
                    last.then_inc(gate_mm, 1)
                    pe.wait_ge(u_in[b], 16 * i + 16)
                    for c in range(KC):
                        last = M(PS[:, 1536:2048], xT[:, b, c, :], wu[:, b, c, :], start=(c == 0), stop=(c == KC - 1))
                    last.then_inc(up_mm, 1)
                    pe.wait_ge(h_ready, n + 1)
                    if not first:
                        pe.wait_ge(hT_out, n)
                    for c in range(FC):
                        last = X(PS[:, 2048 + c * P:2048 + c * P + P], sg[:, b, c:DE:FC], cst["ident"])
                    last.then_inc(hT_mm, 1)
                    pe.wait_ge(hT_out, n + 1)
                    pe.wait_ge(d_in[b], 16 * i + 16)
                    if not first:
                        pe.wait_ge(y_act, n)
                        pe.wait_ge(y_dve, n)
                    for hf in range(2):
                        for c in range(FC):
                            last = M(PS[:, 2560 + 512 * hf:3072 + 512 * hf], hT[:, b, c, :],
                                     wd[:, b, c, 512 * hf:512 * hf + 512], start=(c == 0), stop=(c == FC - 1))
                    last.then_inc(y_mm, 1)

                body(0, 0, True)
                body(0, 1, False)
                with pe.Fori(1, HALF) as i:
                    body(i, 0, False)
                    body(i, 1, False)

            @block.scalar
            def _(act):
                A = nc.scalar.activation

                def body(i, b, first):
                    n = 2 * i + b
                    act.wait_ge(xT_mm, n + 1)
                    if not first:
                        act.wait_ge(y_mm, n + (-1))
                    A(xT[:, b, 0:4, :], PS[:, 0:512].rearrange("p (c t) -> p c t", c=4), ACT.Copy).then_inc(xT_act, 1)
                    act.wait_ge(gate_mm, n + 1)
                    A(sg[:, b, :], PS[:, 1024:1536], ACT.Silu).then_inc(silu, 1)
                    act.wait_ge(y_mm, n + 1)
                    if not first:
                        act.wait_ge(y_stored[b], 16 * i)
                    A(ye[:, b, 0:512], PS[:, 2560:3072], ACT.Copy).then_inc(y_act, 1)

                body(0, 0, True)
                body(0, 1, True)
                with act.Fori(1, HALF) as i:
                    body(i, 0, False)
                    body(i, 1, False)

            @block.vector
            def _(dve):
                V = nc.vector
                dve.wait_ge(tables_in, 32)
                V.tensor_scalar(toks[:], slots[:], 1, None, ALU.arith_shift_right).then_inc(toks_ready, 1)

                def body(i, b, first):
                    n = 2 * i + b
                    dve.wait_ge(xT_mm, n + 1)
                    V.tensor_copy(xT[:, b, 4:8, :], PS[:, 512:1024].rearrange("p (c t) -> p c t", c=4)).then_inc(xT_dve, 1)
                    dve.wait_ge(silu, n + 1)
                    dve.wait_ge(up_mm, n + 1)
                    V.tensor_tensor(sg[:, b, :], sg[:, b, :], PS[:, 1536:2048], ALU.mult).then_inc(h_ready, 1)
                    dve.wait_ge(hT_mm, n + 1)
                    V.tensor_copy(hT[:, b], PS[:, 2048:2560].rearrange("p (c t) -> p c t", c=FC)).then_inc(hT_out, 1)
                    dve.wait_ge(y_mm, n + 1)
                    if not first:
                        dve.wait_ge(y_stored[b], 16 * i)
                    V.tensor_copy(ye[:, b, 512:1024], PS[:, 3072:3584]).then_inc(y_dve, 1)

                body(0, 0, True)
                body(0, 1, True)
                with dve.Fori(1, HALF) as i:
                    body(i, 0, False)
                    body(i, 1, False)


def combine(nc, io, PS, sem, x1, wk):
    with ExitStack() as ctx:
        y2 = ctx.enter_context(nc.sbuf_tensor("f_y2", [P, 5, 2, D], F32))
        y_in, done, stored = sem("f_y_in"), sem("f_done"), sem("f_stored")
        rows = [min(P, T - i * P) for i in range(5)]
        with nc.Block() as block:
            @block.sync
            def _(sp):
                for i in range(5):
                    sp.dma_start(y2[0:rows[i], i], io["y2_dram"][2 * i * P:2 * (i * P + rows[i]), :].rearrange(
                        "(p k) n -> p k n", k=2)).then_inc(y_in, 16)
                for i in range(5):
                    sp.wait_ge(done, 2 * i + 2)
                    sp.dma_start(io["y"][i * P:i * P + rows[i], :], x1[0:rows[i], i, :]).then_inc(stored, 16)
                sp.wait_ge(stored, 80)

            @block.vector
            def _(dve):
                dve.wait_ge(y_in, 80)
                for i in range(5):
                    r = rows[i]
                    for k in range(2):
                        nc.vector.scalar_tensor_tensor(out=x1[0:r, i, :], in0=y2[0:r, i, k, :], scalar=wk[0:r, i, k:k + 1],
                                                       in1=x1[0:r, i, :], op0=ALU.mult, op1=ALU.add).then_inc(done, 1)
                        dve.wait_ge(done, 2 * i + k + 1)


def build(nc, io):
    with ExitStack() as ctx:
        def stage(run, *args):
            own = []

            def sem(name):
                own.append(nc.alloc_semaphore(name))
                return own[-1]

            run(nc, io, PS, sem, *args)
            nc.clear_and_free_semaphores(own)
            nc.all_engine_barrier()

        PS = ctx.enter_context(nc.psum_tensor("PS", [P, 4096], F32))
        cst_t = ctx.enter_context(nc.sbuf_tensor("cst", [P, CONSTS.shape[1]], F32))
        par = ctx.enter_context(nc.sbuf_tensor("par", [P, NPAR], F32))

        class Consts(dict):
            def __missing__(self, name):
                at, width = CONST_AT[name]
                return cst_t[:, at:at + width]

            def __getitem__(self, name):
                return cst_t[:] if isinstance(name, slice) else self.__missing__(name)

        cst = Consts()
        io["par_sb"] = par
        io["P"] = lambda name, c=0: par[:, PAR_AT[name][0] + c:PAR_AT[name][0] + c + 1]
        with nc.sbuf_tensor("z", [P, 14, TP], F32) as z:
            stage(project_inputs, cst, z)
            stage(rwkv, cst, z)
        with ExitStack() as c2:
            kcT_p = c2.enter_context(nc.sbuf_tensor("kcT_p", [P, 2, NKC_P], F32))
            vc_p = c2.enter_context(nc.sbuf_tensor("vc_p", [32, P], F32))
            kcT_s = c2.enter_context(nc.sbuf_tensor("kcT_s", [P, NB, NKC_S], F32))
            vc_s = c2.enter_context(nc.sbuf_tensor("vc_s", [P, NB, P], F32))
            stage(compress, cst, kcT_p, vc_p, kcT_s, vc_s)
            stage(prompt_attention, cst, kcT_p, vc_p)
            stage(sample_attention, cst, kcT_s, vc_s)
        x1 = ctx.enter_context(nc.sbuf_tensor("x1", [P, 5, D], F32))
        wk = ctx.enter_context(nc.sbuf_tensor("wk", [P, 5, 2], F32))
        stage(merge_and_route, cst, x1, wk)
        stage(experts, cst, x1, wk)
        stage(combine, x1, wk)




def chan(v, cols):
    return np.ascontiguousarray(v.reshape(cols, P).T)


def low_rank(v):
    lead = v.shape[:-1]
    o = np.zeros(lead + (14, P), v.dtype)
    o[..., 0:12, :] = v[..., 0:1536].reshape(lead + (12, P))
    o[..., 12, 0:64] = v[..., 1536:1600]
    o[..., 13, 0:96] = v[..., 1600:1696]
    return o


def slab(w):
    return np.ascontiguousarray(w.reshape(KC, P, -1).transpose(1, 0, 2))


def kernel(**inputs):
    import concourse.bacc as _bacc
    from concourse.bass_utils import run_bass_kernel_spmd as _run

    x = {k: np.asarray(v) for k, v in inputs.items()}
    w = {k: (v if k in ("x_prompt", "x_sample", "page_table") else v[0]) for k, v in x.items()}
    nc = _bacc.Bacc("TRN2", target_bir_lowering=False, num_devices=1)
    arrays, io = {}, {}

    def give(name, a):
        a = np.ascontiguousarray(a)
        arrays["in_" + name] = a
        io[name] = nc.dram_tensor("in_" + name, a.shape, mybir.dt.from_np(a.dtype), kind="ExternalInput").ap()

    def take(name, shape):
        io[name] = nc.dram_tensor("out_" + name, shape, F32, kind="ExternalOutput").ap()

    def scratch(name, shape, dt=F32):
        io[name] = nc.dram_tensor("scratch_" + name, shape, dt, kind="Internal").ap()

    tokens = np.concatenate([w["x_prompt"].reshape(TPR, D), w["x_sample"].reshape(TSM, D)], 0)
    give("x", tokens)
    give("xT", slab(tokens.T))
    give("consts", CONSTS)
    par = [low_rank(w["mu_shift"]).T] + [chan(w[k], 4) for k in ("w0", "a0", "k_k", "k_a")]
    par += [chan(w["r_k"].reshape(-1), 4), chan(w["ln_x_w"], 4), chan(w["ln_x_b"], 4), chan(w["norm1"], KC)]
    par += [np.concatenate([w[k]] * 2)[:, None] for k in ("cmp_b1_k", "cmp_b1_v")] + [chan(w["norm2"], KC)]
    give("par", np.concatenate(par, 1))
    give("gains", np.broadcast_to(np.stack([w[k] for k in ("q_norm", "ks_norm", "kw_norm")])[None], (P, 3, HD)))
    wi, cuts = w["w_in"], [(0, 512), (512, 1024), (1024, 1536), (1536, 1696), (1696, 2208), (2208, 2720), (2720, 3000)]
    for i, (a, b) in enumerate(cuts):
        give(f"w_in{i}", slab(wi[:, a:b]))
    io["w_in"] = [io[f"w_in{i}"] for i in range(len(cuts))]
    give("w_lora_up", np.concatenate([w["w_decay_up"], w["w_iclr_up"]], 0))
    give("w_gate_up", w["w_gate_up"])
    give("shift_in", low_rank(w["state_shift"]).transpose(2, 1, 0))
    give("wkv_in", w["state_wkv"].reshape(NB, 4, 2, HD, HD).transpose(2, 4, 1, 0, 3).reshape(P, 4, NB, HD))
    take("kvc", (T, 256))
    take("kvs", (T, 256))
    take("kvw", (T, 256))
    take("shift_out", (P, 14, 1 + NB))
    take("wkv_p", (P, 4, HD))
    take("wkv_s", (P, 4, NB, HD))
    take("y", (T, D))
    take("win_s", (NB, 512, 256))
    give("win_cache", w["cache_win_kv"].reshape(NB, 512, 256))
    scratch("q_dram", (T, 512))
    scratch("gate_dram", (T, 24))
    scratch("oa_dram", (P, 4, T))
    scratch("h_dram", (P, KC, T))
    scratch("ob_dram", (P, 4, T))
    scratch("h2_dram", (T, D))
    scratch("y2_dram", (2 * T, D))
    scratch("slots_dram", (P * NBLK, 1), I32)
    scratch("ids_dram", (1, NBLK), I32)
    give("page_table", w["page_table"].reshape(1, -1).astype(np.int32))
    pool_c = w["cache_cmp_kv"].reshape(-1, PAGE, 2, P)
    give("cmp_pool", pool_c.transpose(0, 3, 2, 1))
    pool_s = w["cache_slc_kv"].reshape(-1, PAGE, 2, P)
    give("slc_pool", np.stack([pool_s[:, :, 0].transpose(0, 2, 1), pool_s[:, :, 1]], 2))
    win = w["cache_win_kv"].reshape(NB, 4, P, 2, P)
    give("win_kv", np.stack([win[:, :, :, 0].transpose(0, 3, 1, 2), win[:, :, :, 1].transpose(0, 2, 1, 3)], 3))
    give("cmp_w1", np.stack([w["cmp_w1_k"], w["cmp_w1_v"]]).transpose(2, 0, 1, 3))
    give("cmp_w2", np.stack([w["cmp_w2_k"], w["cmp_w2_v"]]).transpose(1, 0, 2))
    give("cmp_pe", np.stack([w["cmp_pe_k"], w["cmp_pe_v"]]).transpose(2, 0, 1))
    give("kc_gain", np.broadcast_to(w["kc_norm"][None], (P, HD)))
    give("w_gates", wi[:, 3000:5048].reshape(KC, P, 2, KC, P).transpose(2, 3, 1, 0, 4))
    give("w_branch", np.stack([w["w_branch_a"], w["w_branch_b"]]).reshape(2, 4, P, KC, P).transpose(0, 3, 2, 1, 4))
    give("w_out", w["w_out"].reshape(KC, P, 2, D // 2).transpose(2, 1, 0, 3))
    give("norm2_rows", np.broadcast_to(w["norm2"][None], (P, D)))
    give("w_route", slab(np.concatenate([w["w_route_group"], w["w_route_expert"]], 1)))
    give("b_route", np.broadcast_to(np.concatenate([w["b_route_group"], w["b_route_expert"]])[None], (P, 36)))
    for k in ("w_exp_gate", "w_exp_up", "w_exp_down"):
        give(k, w[k])
    build(nc, io)
    got = _run(nc, [arrays], core_ids=[0]).results[0]
    o = {k[4:]: np.asarray(got[k]) for k in got if k.startswith("out_")}

    def rows(a):
        return a[0:TPR].reshape(1, 1, TPR, 2, 2, HD), a[TPR:].reshape(1, NB, TS, 2, 2, HD)

    (cp, cs), (sp, ss), (wp, ws) = rows(o["kvc"]), rows(o["kvs"]), rows(o["kvw"])
    sh = o["shift_out"].transpose(2, 1, 0)
    sh = np.concatenate([sh[:, 0:12].reshape(9, 1536), sh[:, 12, 0:64], sh[:, 13, 0:96]], 1)
    wkv_p = o["wkv_p"].reshape(2, HD, 4, HD).transpose(2, 0, 3, 1).reshape(1, 1, 8, HD, HD)
    wkv_s = o["wkv_s"].reshape(2, HD, 4, NB, HD).transpose(3, 2, 0, 4, 1).reshape(1, NB, 8, HD, HD)
    return (o["y"][0:TPR].reshape(1, TPR, D), o["y"][TPR:].reshape(NB, TS, D), cp, sp, wp, wkv_p, sh[None, 0:1],
            cs, ss, o["win_s"].reshape(1, NB, 512, 2, 2, HD), wkv_s, sh[None, 1:])
```

```python
from contextlib import ExitStack

import concourse.bass as bass
from concourse import mybir
import numpy as np

F32 = mybir.dt.float32
F32R = mybir.dt.float32r
I32 = mybir.dt.int32
U32 = mybir.dt.uint32
ALU = mybir.AluOpType
ACT = mybir.ActivationFunctionType
AX_X = mybir.AxisListType.X

P = 128
D = 1024
KC = D // P
TPR, NB, TS = 512, 8, 4
TSM = NB * TS
T = TPR + TSM
TH = T // 2
HD = 64
RW_IN = 1696
CH = 64
NCH = TPR // CH + 1
TP = NCH * CH
LV = 5
PAGE, NPAGES, PAST = 128, 16, 2048
NKC_P = (TPR - 32) // 16 + 1
NKC_S = (PAST + TS - 32) // 16 + 1
NSB = -(-(PAST + TS) // HD)
HR = 128
NE, CAP = 32, 64
NOV = (2 * T - 1) // CAP
NBLK = NE + NOV
HW = D * (D // 2) // P // 2
NEG = -1e30
RMS_EPS, GN_EPS = 1e-6, 64e-5
DECAY = -float(np.exp(-0.5))



def shape_constants():
    c = {}
    p = np.arange(P)
    c["ident"] = np.eye(P)
    c["blockones"] = (p[:, None] // HD == p[None, :] // HD)
    c["ones"] = np.ones((P, P))
    c["tri"] = np.where(p[None, :] <= p[:, None], 0.0, NEG)
    s, t = p[:, None] % CH, np.arange(CH)[None, :]
    for name, same in (("p", np.ones((P, CH), bool)), ("s", s // TS == t // TS)):
        c["gram_" + name] = np.concatenate([(s < t) & same, (s <= t) & same], 1)
        c["lvl0_" + name] = np.concatenate([(t < s) & (t // 2 == s // 2) & same, (s < t) & (t // 2 == s // 2) & same], 1)
    c["eye2"] = (s == t)
    lv = []
    for l in range(1, LV + 1):
        b = 2 ** l
        lv.append((s // (2 * b) == t // (2 * b)) & (s // b % 2 == 0) & (t // b % 2 == 1))
    c["levels"] = np.concatenate(lv, 1)
    tok = np.arange(T)
    start = np.where(tok < TPR, tok % CH == 0, tok % TS == 0)
    c["restart"] = np.repeat((~start)[None, :], P, 0)
    c["seq"] = ((p % CH)[:, None] // TS == np.arange(NB)[None, :])
    q = np.arange(4)[None, :, None] * P + p[:, None, None]
    c["cmpneg_p"] = np.where(np.arange(NKC_P)[None, None, :] * 16 + 31 <= q, 0.0, NEG).reshape(P, -1)
    c["cmp_p"] = (np.arange(NKC_P)[None, None, :] * 16 + 31 <= q).reshape(P, -1)
    b4, g, m, st = p // 32, p // 16 % 2, p // 4 % 4, p % 4
    nb = np.arange(TSM)
    new = [(nb[None, :] // TS == (4 * h + b4)[:, None]) & (nb[None, :] % TS <= st[:, None]) for h in range(2)]
    c["new_s"] = np.concatenate([np.where(x, 0.0, NEG) for x in new], 1)
    c["win_old"] = np.where(np.arange(TS)[None, :] > st[:, None], 0.0, NEG)
    c["sumheads"] = (b4[:, None] == b4[None, :]) & (g[:, None] == g[None, :]) & (st[:, None] == st[None, :])
    n = np.arange(P)[:, None] * 16
    j = np.arange(NSB)[None, :]
    c["overlap"] = (n < (j + 1) * HD) & (n + 32 > j * HD) & (p[:, None] < NKC_S)
    c["grp"] = np.stack([g == 0, g == 1], 1)
    c["rowtok"] = np.concatenate([(p[:, None] < TSM) & (p[:, None] // TS == 4 * h + b4[None, :]) & (p[:, None] % TS == st[None, :]) for h in range(2)], 1)
    c["rowhead"] = np.tile(np.arange(8)[None, :] == (g * 4 + m)[:, None], (1, 3))
    c["before"] = p[:, None] < p[None, :]
    c["iota_e"] = np.repeat(np.arange(NE)[None, :], P, 0)
    c["egroup"] = np.repeat((np.arange(NE) // 8)[None, :], P, 0)
    c["iota_o"] = np.repeat(np.arange(NOV)[None, :], P, 0)
    c["slotval"] = np.concatenate([(2 * (i * P + p) + k)[:, None] for i in range(5) for k in range(2)], 1)
    out, at, cols = {}, 0, []
    for k, v in c.items():
        v = np.asarray(v, np.float32)
        out[k] = (at, v.shape[1])
        cols.append(v)
        at += v.shape[1]
    return out, np.concatenate(cols, 1)


CONST_AT, CONSTS = shape_constants()
PAR_AT = {}
_at = 0
for _n, _w in (("mu", 14), ("w0", 4), ("a0", 4), ("k_k", 4), ("k_a", 4), ("r_k", 4), ("ln_w", 4), ("ln_b", 4),
               ("norm1", KC), ("b1k", 1), ("b1v", 1), ("norm2", KC)):
    PAR_AT[_n] = (_at, _w)
    _at += _w
NPAR = _at


class Chain:

    def __init__(self, eng, sem):
        self.eng, self.sem, self.n = eng, sem, 0

    def __call__(self, ins):
        self.n += 1
        ins.then_inc(self.sem, 1)
        self.eng.wait_ge(self.sem, self.n)


def in_halves(ps):
    return ps.rearrange("p (b n) -> p b n", b=2)[:, :, 0:TH]


def two(ap):
    return ap.rearrange("p (b n) -> p b n", b=2)


def project_inputs(nc, io, PS, sem, cst, z):
    with ExitStack() as ctx:
        def t(name, shape, dt=F32):
            return ctx.enter_context(nc.sbuf_tensor(name, shape, dt))

        par = io["par_sb"]
        xT = t("p1_xT", [P, KC, T])
        sq = t("p1_sq", [P, KC, T])
        rstd = t("p1_rstd", [P, T])
        hT = t("p1_hT", [P, KC, T])
        NW = 3
        w = t("p1_w", [P, NW, KC, 512])
        NEV = 3
        ev = t("p1_ev", [P, NEV, 512])
        sqh = t("p1_sqh", [P, 512])
        ssh = t("p1_ssh", [P, 8])
        gains = t("p1_gains", [P, 3, HD])
        gate = t("p1_gate", [P, NEV, 24])

        slabs = [("T", 512), ("T", 512), ("T", 512), ("T", 160), ("q", 512), ("kvcs", 512), ("kvwg", 280)]
        units = []
        for s, (kind, width) in enumerate(slabs):
            if kind == "T" and width == 512:
                units += [(s, "T", 128 * j, 128, 4 * s + j) for j in range(4)]
            elif kind == "T":
                units += [(s, "T", 0, 64, 12), (s, "T", 64, 96, 13)]
            else:
                units += [(s, kind, i, min(P, T - i * P), width) for i in range(5)]
        tok_units = [u for u in units if u[1] != "T"]
        nT = len(units) - len(tok_units)
        last_of_slab = [max(i for i, u in enumerate(units) if u[0] == s) for s in range(len(slabs))]

        const_in, x_in = sem("p1_const_in"), sem("p1_x_in")
        w_ready = [sem(f"p1_w_ready{i}") for i in range(NW)]
        squared, sumsq, h_ready = sem("p1_squared"), sem("p1_sumsq"), sem("p1_h_ready")
        mm_done, evac_act, evac_dve = sem("p1_mm_done"), sem("p1_evac_act"), sem("p1_evac_dve")
        normed, stored = sem("p1_normed"), [sem(f"p1_stored{i}") for i in range(NEV)]
        h_stored = sem("p1_h_stored")
        root_in, root_out = sem("p1_root_in"), sem("p1_root_out")
        dchain, zeroed, gated = sem("p1_dchain"), sem("p1_zeroed"), sem("p1_gated")

        def unit_psum(i):
            u = units[i]
            if u[1] == "T":
                return in_halves(PS[0:u[3], (i % 2) * 1024:(i % 2) * 1024 + 1024])
            k = i - nT
            return PS[0:u[3], 2048 + (k % 2) * 512:2048 + (k % 2) * 512 + u[4]]

        with nc.Block() as block:
            @block.sync
            def _(sp):
                sp.dma_start(xT[:], io["xT"]).then_inc(x_in, 16)
                sp.dma_start(cst[:], io["consts"]).then_inc(const_in, 16)
                sp.dma_start(par[:], io["par"]).then_inc(const_in, 16)
                sp.dma_start(gains[:], io["gains"]).then_inc(const_in, 16)
                for s in range(len(slabs)):
                    if s == 3:
                        sp.wait_ge(h_ready, KC)
                        sp.dma_start(io["h_dram"], hT[:]).then_inc(h_stored, 16)
                    if s >= NW:
                        sp.wait_ge(mm_done, last_of_slab[s - NW] + 1)
                    wd = slabs[s][1]
                    sp.dma_start(w[:, s % NW, :, 0:wd], io["w_in"][s]).then_inc(w_ready[s % NW], 16)
                sp.wait_ge(h_stored, 16)

            @block.gpsimd
            def _(pool):
                nc.gpsimd.memset(z[:, 12:14, :], 0.0).then_inc(zeroed, 1)
                n_st = [0] * NEV
                for k, (s, kind, i, rows, width) in enumerate(tok_units):
                    e = k % NEV
                    pool.wait_ge(normed, k + 1)
                    r = slice(i * P, i * P + rows)
                    if kind == "q":
                        pool.dma_start(io["q_dram"][r, :], ev[0:rows, e, :]).then_inc(stored[e], 16)
                    elif kind == "kvcs":
                        pool.dma_start(io["kvc"][r, :], ev[0:rows, e, 0:256]).then_inc(stored[e], 16)
                        pool.dma_start(io["kvs"][r, :], ev[0:rows, e, 256:512]).then_inc(stored[e], 16)
                    else:
                        pool.dma_start(io["kvw"][r, :], ev[0:rows, e, 0:256]).then_inc(stored[e], 16)
                        pool.wait_ge(gated, i + 1)
                        pool.dma_start(io["gate_dram"][r, :], gate[0:rows, e, :]).then_inc(stored[e], 16)
                    n_st[e] += 16 if kind == "q" else 32
                for e in range(NEV):
                    pool.wait_ge(stored[e], n_st[e])

            def stores_before(k):
                return sum(16 if tok_units[j][1] == "q" else 32 for j in range(k % NEV, k, NEV))

            @block.tensor
            def _(pe):
                pe.wait_ge(const_in, 48)
                for c in range(KC):
                    pe.wait_ge(squared, c + 1)
                    o = slice(c * 128, c * 128 + 128)
                    nc.tensor.matmul(PS[:, 3072:3584], cst["ones"], sq[:, c, 0:512], start=(c == 0), stop=(c == KC - 1))
                    last = nc.tensor.matmul(PS[:, 3584:3584 + TSM], cst["ones"], sq[:, c, 512:T],
                                            start=(c == 0), stop=(c == KC - 1))
                last.then_inc(sumsq, 1)
                for i, (s, kind, a, m, b) in enumerate(units):
                    if i == 0 or units[i - 1][0] != s:
                        pe.wait_ge(w_ready[s % NW], 16 * (s // NW + 1))
                    out = unit_psum(i)
                    if kind == "T":
                        if i >= 2:
                            pe.wait_ge(evac_act if i % 2 == 0 else evac_dve, i // 2)
                        for n in range(2):
                            for c in range(KC):
                                if i == 0 and n == 0:
                                    pe.wait_ge(h_ready, c + 1)
                                last = nc.tensor.matmul(out[:, n], w[:, s % NW, c, a:a + m], hT[:, c, n * TH:n * TH + TH],
                                                        start=(c == 0), stop=(c == KC - 1))
                    else:
                        k = i - nT
                        if k >= 2:
                            pe.wait_ge(evac_act, nT // 2 + k - 1)
                        for c in range(KC):
                            last = nc.tensor.matmul(out, hT[:, c, a * P:a * P + m], w[:, s % NW, c, 0:b],
                                                    start=(c == 0), stop=(c == KC - 1))
                    last.then_inc(mm_done, 1)

            @block.scalar
            def _(act):
                act.wait_ge(x_in, 16)
                for c in range(KC):
                    nc.scalar.activation(sq[:, c, :], xT[:, c, :], ACT.Square).then_inc(squared, 1)
                act.wait_ge(root_in, 1)
                nc.scalar.activation(rstd[:], rstd[:], ACT.Sqrt).then_inc(root_out, 1)

                def root(k):
                    m, nh = tok_units[k][3], 8 if tok_units[k][1] == "q" else 2
                    act.wait_ge(root_in, k + 2)
                    nc.scalar.activation(ssh[0:m, 0:nh], ssh[0:m, 0:nh], ACT.Sqrt).then_inc(root_out, 1)

                act.wait_ge(zeroed, 1)
                for i, (s, kind, a, m, b) in enumerate(units):
                    if kind == "T":
                        if i % 2 == 0:
                            act.wait_ge(mm_done, i + 1)
                            nc.scalar.activation(two(z[0:m, b, 0:T]), unit_psum(i), ACT.Copy).then_inc(evac_act, 1)
                        continue
                    k = i - nT
                    act.wait_ge(mm_done, i + 1)
                    if k >= NEV:
                        act.wait_ge(stored[k % NEV], stores_before(k))
                    if kind == "kvwg":
                        nc.scalar.activation(gate[0:m, k % NEV, :], unit_psum(i)[:, 256:280], ACT.Sigmoid).then_inc(gated, 1)
                        nc.scalar.activation(ev[0:m, k % NEV, 0:256], unit_psum(i)[:, 0:256], ACT.Copy).then_inc(evac_act, 1)
                    else:
                        nc.scalar.activation(ev[0:m, k % NEV, :], unit_psum(i), ACT.Copy).then_inc(evac_act, 1)
                    if k:
                        root(k - 1)
                root(len(tok_units) - 1)

            @block.vector
            def _(dve):
                link = Chain(dve, dchain)
                dve.wait_ge(sumsq, 1)
                link(nc.vector.tensor_scalar(rstd[:], PS[:, 3072:3072 + T], 1.0 / D, RMS_EPS, ALU.mult, ALU.add))
                dve.sem_inc(root_in, 1)
                dve.wait_ge(root_out, 1)
                link(nc.vector.reciprocal(rstd[:], rstd[:]))
                dve.wait_ge(x_in, 16)
                dve.wait_ge(const_in, 48)
                for c in range(KC):
                    nc.vector.scalar_tensor_tensor(out=hT[:, c, :], in0=xT[:, c, :], scalar=io["P"]("norm1", c),
                                                   in1=rstd[:], op0=ALU.mult, op1=ALU.mult).then_inc(h_ready, 1)
                dve.wait_ge(zeroed, 1)
                for i, (s, kind, a, m, b) in enumerate(units):
                    if kind == "T" and i % 2 == 1:
                        dve.wait_ge(mm_done, i + 1)
                        nc.vector.tensor_copy(two(z[0:m, b, 0:T]), unit_psum(i)).then_inc(evac_dve, 1)
                for k, (s, kind, i, m, width) in enumerate(tok_units):
                    nh, lo, g = {"q": (8, 0, 0), "kvcs": (2, 256, 1), "kvwg": (2, 0, 2)}[kind]
                    dve.wait_ge(evac_act, nT // 2 + k + 1)
                    v = ev[0:m, k % NEV, lo:lo + nh * HD].rearrange("p (h d) -> p h d", d=HD)
                    s_ = sqh[0:m, 0:nh * HD].rearrange("p (h d) -> p h d", d=HD)
                    link(nc.vector.tensor_tensor(s_, v, v, ALU.mult))
                    link(nc.vector.reduce_sum(ssh[0:m, 0:nh], s_, AX_X))
                    link(nc.vector.tensor_scalar(ssh[0:m, 0:nh], ssh[0:m, 0:nh], 1.0 / HD, RMS_EPS, ALU.mult, ALU.add))
                    dve.sem_inc(root_in, 1)
                    dve.wait_ge(root_out, k + 2)
                    link(nc.vector.reciprocal(ssh[0:m, 0:nh], ssh[0:m, 0:nh]))
                    link(nc.vector.tensor_tensor(v, v, ssh[0:m, 0:nh].unsqueeze(2).to_broadcast([m, nh, HD]), ALU.mult))
                    nc.vector.tensor_tensor(v, v, gains[0:m, g, :].unsqueeze(1).to_broadcast([m, nh, HD]),
                                            ALU.mult).then_inc(normed, 1)


def rwkv(nc, io, PS, sem, cst, z):
    Pm = io["P"]
    with ExitStack() as ctx:
        def t(name, shape, dt=F32):
            return ctx.enter_context(nc.sbuf_tensor(name, shape, dt))

        zm = t("r_zm", [P, 14, TP])
        r_, k_, v_ = zm[:, 0:4, :], zm[:, 4:8, :], zm[:, 8:12, :]
        sp2 = t("r_sp2", [P, 4, TP])
        lw, a_, L, kk = z[:, 0:4, :], z[:, 4:8, :], z[:, 8:12, :], sp2[:, :, :]
        g_ = t("r_g", [P, 4, TP])
        kka = t("r_kka", [P, 4, TP])
        AR = t("r_AR", [P, 4, 2, TP])
        BK = t("r_BK", [P, 4, 2, TP])
        BD = t("r_BD", [P, 4, TP])
        KD = t("r_KD", [P, 4, TP])
        E3 = t("r_E3", [P, 4, TP])
        tw, sg = E3[0:32, 0, 0:T], E3[0:96, 1, 0:T]
        wup = t("r_wup", [64, 512])
        wgu = t("r_wgu", [96, 512])
        shift = t("r_shift", [P, 14, NB])
        wc = t("r_wc", [P, 4, NCH - 1 + NB])
        spare = z[:, 0:4, :].rearrange("p a s -> p (a s)")
        tok = [t("r_tok", [P, 3, 4, CH])[:],
               spare[:, 0:768].rearrange("p (k a s) -> p k a s", k=3, a=4)]
        G = [t("r_G", [P, 2, 4, 2, CH])[:], spare[:, 768:1792].rearrange("p (k a b s) -> p k a b s", k=2, a=4, b=2)]
        TB = [t("r_TB", [P, 4, 2, CH])[:],
              spare[:, 1792:2304].rearrange("p (a b s) -> p a b s", a=4, b=2)]
        NT = t("r_NT", [P, 4, LV, CH])
        X = sp2
        U0 = t("r_U0", [P, 4, CH])
        U = t("r_U", [P, 4, CH])
        S = t("r_S", [P, 4, HD])
        Yt = io["Yt"] = t("r_Y", [P, NCH, 4, HD])
        S0 = E3[:, :, 0:512].rearrange("p a (b i) -> p a b i", b=NB)
        SAT = t("r_SAT", [P, 4, 2, CH])
        expd = [t("r_exp", [P, 2, NB, HD])[:],
                sp2[:].rearrange("p a s -> p (a s)")[:, 0:1024].rearrange("p (k b i) -> p k b i", k=2, b=NB)]
        ysq = t("r_ysq", [P, 4, HD])
        st1, st2 = t("r_st1", [P, NCH * 4]), t("r_st2", [P, NCH * 4])

        par_in, lora_w, s0_in = sem("r_par_in"), sem("r_lora_w"), sem("r_s0_in")
        mixed, lora_in, lora_mm = sem("r_mixed"), sem("r_lora_in"), sem("r_lora_mm")
        lora_out, kk2_ready, kk_mm, kk_used = sem("r_lora_out"), sem("r_kk2"), sem("r_kkmm"), sem("r_kkused")
        L_ready, exps, ops_ready, e3_free = sem("r_L"), sem("r_exps"), sem("r_ops"), sem("r_e3free")
        bonus_in, bonus_mm, bonus_out = sem("r_bonus_in"), sem("r_bonus_mm"), sem("r_bonus_out")
        gram, gram_out, tok_out = sem("r_gram"), sem("r_gram_out"), sem("r_tok_out")
        x_mm, x_out, t_mm, t_out = sem("r_x_mm"), sem("r_x_out"), sem("r_t_mm"), sem("r_t_out")
        u0_mm, u0_out, u_mm, u_out = sem("r_u0_mm"), sem("r_u0_out"), sem("r_u_mm"), sem("r_u_out")
        y_mm, y_out, s_mm, s_out = sem("r_y_mm"), sem("r_y_out"), sem("r_s_mm"), sem("r_s_out")
        sat_mm, sat_out, exp_out, sf_mm, sf_out = (sem("r_sat_mm"), sem("r_sat_out"), sem("r_exp_out"), sem("r_sf_mm"),
                                                   sem("r_sf_out"))
        gn_ready, back_mm, back_out, oa_ready, out_dma = (sem("r_gn"), sem("r_back_mm"), sem("r_back_out"),
                                                          sem("r_oa"), sem("r_out_dma"))
        shift_dma = sem("r_shift_dma")
        root_in, root_out = sem("r_root_in"), sem("r_root_out")
        lastz = t("r_lastz", [P, 14, 1 + NB])
        last_rows = sem("r_last_rows")
        tok_mm = sem("r_tok_mm")
        x_zeroed, g1_out = sem("r_x_zeroed"), sem("r_g1_out")
        scanned = sem("r_scanned")
        pchain, v_mixed, mix_done = sem("r_pchain"), sem("r_v_mixed"), sem("r_mix_done")
        dchain, achain, s_init = sem("r_dchain"), sem("r_achain"), sem("r_s_init")

        def wide(k):
            return PS[:, (k % 4) * 1024:(k % 4) * 1024 + T]

        def mmT(k, m, lhsT, rhs):
            nc.tensor.matmul(wide(k)[0:m, 0:512], lhsT, rhs[:, 0:512], start=True, stop=True)
            return nc.tensor.matmul(wide(k)[0:m, 512:T], lhsT, rhs[:, 512:T], start=True, stop=True)

        halves = (slice(0, 64), slice(64, 128))
        psG = PS[:, 0:1024].rearrange("p (k a b s) -> p k a b s", k=2, a=4, b=2)
        psN = PS[:, 1024:1280].rearrange("p (a s) -> p a s", a=4)
        psX = PS[:, 1280:1408].rearrange("p (a s) -> p a s", a=4)
        psTok = PS[:, 1536:2304].rearrange("p (k a s) -> p k a s", k=3, a=4)
        psS = PS[:, 2304:2560].rearrange("p (a s) -> p a s", a=4)
        psT = PS[:, 2560:2816].rearrange("p (a b s) -> p a b s", a=4, b=2)
        psU0 = PS[:, 3072:3328].rearrange("p (a s) -> p a s", a=4)
        psU = PS[:, 3328:3584].rearrange("p (a s) -> p a s", a=4)
        psY = PS[:, 3584:3840].rearrange("p (a s) -> p a s", a=4)
        psSAT = PS[:, 0:512].rearrange("p (a b s) -> p a b s", a=4, b=2)

        def levels(c):
            return LV if c < NCH - 1 else 1

        def parity(ap, l, odd):
            b = 2 ** (l + 1)
            if len(ap.shape) == 2:
                return ap.rearrange("p (n two b) -> p n two b", two=2, b=b)[:, :, odd, :]
            return ap.rearrange("p a (n two b) -> p a n two b", two=2, b=b)[:, :, :, odd, :]

        def packed(ap, l):
            b = 2 ** (l + 1)
            return ap.rearrange("p (n b) -> p n b", b=b) if len(ap.shape) == 2 else ap.rearrange("p a (n b) -> p a n b", b=b)

        def xl(l):
            return slice(l * CH, (l + 1) * CH)

        with nc.Block() as block:
            @block.sync
            def _(sp):
                sp.dma_start(wup[:], io["w_lora_up"]).then_inc(lora_w, 16)
                sp.dma_start(wgu[:], io["w_gate_up"]).then_inc(lora_w, 16)
                sp.dma_start(shift[:], io["shift_in"]).then_inc(par_in, 16)
                sp.wait_ge(last_rows, 1)
                sp.dma_start(io["shift_out"], lastz[:]).then_inc(shift_dma, 16)
                sp.wait_ge(e3_free, 1)
                sp.dma_start(S0, io["wkv_in"]).then_inc(s0_in, 16)
                sp.wait_ge(s_out, NCH - 1)
                sp.dma_start(io["wkv_p"], S[:]).then_inc(out_dma, 16)
                sp.wait_ge(sf_out, 4)
                sp.dma_start(io["wkv_s"], S0).then_inc(out_dma, 16)
                sp.wait_ge(oa_ready, 4)
                sp.dma_start(io["oa_dram"], BD[:, :, 0:T]).then_inc(out_dma, 16)
                sp.wait_ge(shift_dma, 16)
                sp.wait_ge(out_dma, 48)

            def shift_rows(eng, link, cs):
                n = cs.stop - cs.start
                link(eng.tensor_tensor(zm[:, cs, 1:TPR], z[:, cs, 0:TPR - 1], z[:, cs, 1:TPR], ALU.subtract))
                link(eng.tensor_scalar(zm[:, cs, 0:1], z[:, cs, 0:1], -1.0, None, ALU.mult))
                zs = z[:, cs, TPR:T].rearrange("p c (b t) -> p c b t", t=TS)
                zms = zm[:, cs, TPR:T].rearrange("p c (b t) -> p c b t", t=TS)
                for c in range(n):
                    link(eng.tensor_tensor(zms[:, c, :, 1:TS], zs[:, c, :, 0:TS - 1], zs[:, c, :, 1:TS], ALU.subtract))
                link(eng.tensor_tensor(zms[:, :, :, 0], shift[:, cs], zs[:, :, :, 0], ALU.subtract))

            @block.gpsimd
            def _(pool):
                link = Chain(pool, pchain)
                G_ = nc.gpsimd
                pool.wait_ge(par_in, 16)
                cs = slice(8, 12)
                shift_rows(G_, link, cs)
                mu = Pm("mu", 8, 4).unsqueeze(2).to_broadcast([P, 4, T])
                link(G_.tensor_tensor(zm[:, cs, 0:T], zm[:, cs, 0:T], mu, ALU.mult))
                link(G_.tensor_tensor(zm[:, cs, 0:T], zm[:, cs, 0:T], z[:, cs, 0:T], ALU.add))
                pool.sem_inc(v_mixed, 1)
                link(G_.memset(zm[:, :, T:TP], 0.0))
                for tile in (BK, AR):
                    link(G_.memset(tile[:, :, :, T:TP], 0.0))
                for tile in (BD, KD):
                    link(G_.memset(tile[:, :, T:TP], 0.0))
                link(G_.memset(SAT[:], 0.0))
                link(G_.memset(S[:], 0.0))
                pool.sem_inc(s_init, 1)
                pool.wait_ge(scanned, 1)
                link(G_.tensor_tensor(KD[:, :, 0:T], L[:, :, 0:T], lw[:, :, 0:T], ALU.subtract))
                pool.sem_inc(L_ready, 1)
                for at, end, n in ((0, TPR, CH), (TPR, T, TS)):
                    for c in range(4):
                        l3 = L[:, c, at:end].rearrange("p (c s) -> p c s", s=n)
                        link(G_.tensor_tensor(lw[:, c, at:end].rearrange("p (c s) -> p c s", s=n),
                                              l3[:, :, n - 1:n].to_broadcast([P, (end - at) // n, n]), l3, ALU.subtract))
                pool.sem_inc(L_ready, 1)

            @block.vector
            def _(dve):
                link = Chain(dve, dchain)
                V = nc.vector

                def bc(ap, shape):
                    return ap.to_broadcast(shape)

                link(V.tensor_copy(lastz[:, :, 0:1], z[:, :, TPR - 1:TPR]))
                link(V.tensor_copy(lastz[:, :, 1:1 + NB], z[:, :, TPR + TS - 1:T:TS]))
                dve.sem_inc(last_rows, 1)
                dve.wait_ge(par_in, 16)
                for cs in (slice(12, 14), slice(4, 8), slice(0, 4)):
                    shift_rows(V, link, cs)
                    for c in range(cs.start, cs.stop):
                        V.scalar_tensor_tensor(out=zm[:, c, 0:T], in0=zm[:, c, 0:T], scalar=Pm("mu", c), in1=z[:, c, 0:T],
                                               op0=ALU.mult, op1=ALU.add).then_inc(mix_done, 1)
                    dve.wait_ge(mix_done, {12: 2, 4: 6, 0: 10}[cs.start])
                    if cs.start != 4:
                        dve.sem_inc(mixed, 1)
                for c in range(4):
                    link(V.tensor_scalar(kk[:, c, 0:T], k_[:, c, 0:T], Pm("k_k", c), None, ALU.mult))
                    link(V.tensor_tensor(kka[:, c, 0:T], kk[:, c, 0:T], kk[:, c, 0:T], ALU.mult))
                    dve.sem_inc(kk2_ready, 1)
                dve.wait_ge(v_mixed, 1)
                dve.wait_ge(lora_out, 12)
                link(V.tensor_scalar(lw[:, :, 0:T], lw[:, :, 0:T], DECAY, None, ALU.mult))
                for c in range(4):
                    link(V.tensor_tensor_scan(L[:, c, 0:T], cst["restart"], lw[:, c, 0:T], 0.0, ALU.mult, ALU.add))
                dve.sem_inc(scanned, 1)
                for c in range(4):
                    dve.wait_ge(kk_mm, c + 1)
                    link(V.tensor_scalar(kka[:, c, 0:T], wide(c), 1e-24, None, ALU.max))
                    dve.sem_inc(root_in, 1)
                dve.sem_inc(kk_used, 1)
                for c in range(4):
                    dve.wait_ge(root_out, c + 1)
                    link(V.reciprocal(kka[:, c, 0:T], kka[:, c, 0:T]))
                    link(V.tensor_tensor(kk[:, c, 0:T], kk[:, c, 0:T], kka[:, c, 0:T], ALU.mult))
                link(V.tensor_tensor(kka[:, :, 0:T], kk[:, :, 0:T], a_[:, :, 0:T], ALU.mult))
                for c in range(4):
                    link(V.tensor_scalar(a_[:, c, 0:T], a_[:, c, 0:T], 1.0, Pm("k_a", c), ALU.subtract, ALU.mult))
                    link(V.scalar_tensor_tensor(out=k_[:, c, 0:T], in0=a_[:, c, 0:T], scalar=1.0, in1=k_[:, c, 0:T],
                                                op0=ALU.add, op1=ALU.mult))
                dve.wait_ge(exps, 1)
                link(V.scalar_tensor_tensor(out=AR[:, :, 0, 0:T], in0=kk[:, :, 0:T], scalar=-1.0, in1=KD[:, :, 0:T],
                                            op0=ALU.mult, op1=ALU.mult))
                dve.wait_ge(exps, 2)
                link(V.tensor_tensor(AR[:, :, 1, 0:T], r_[:, :, 0:T], BD[:, :, 0:T], ALU.mult))
                dve.wait_ge(exps, 3)
                link(V.tensor_tensor(BK[:, :, 0, 0:T], kka[:, :, 0:T], E3[:, :, 0:T], ALU.mult))
                link(V.tensor_tensor(BK[:, :, 1, 0:T], k_[:, :, 0:T], E3[:, :, 0:T], ALU.mult))
                dve.sem_inc(e3_free, 1)
                dve.wait_ge(exps, 5)
                link(V.tensor_tensor(BD[:, :, 0:T], kka[:, :, 0:T], lw[:, :, 0:T], ALU.mult))
                link(V.tensor_tensor(KD[:, :, 0:T], k_[:, :, 0:T], lw[:, :, 0:T], ALU.mult))
                for c in range(4):
                    link(V.scalar_tensor_tensor(out=kka[:, c, 0:T], in0=r_[:, c, 0:T], scalar=Pm("r_k", c),
                                                in1=k_[:, c, 0:T], op0=ALU.mult, op1=ALU.mult))
                dve.sem_inc(ops_ready, 1)
                for c in range(4):
                    dve.wait_ge(bonus_mm, c + 1)
                    link(V.tensor_tensor(a_[:, c, 0:T], wide(c), v_[:, c, 0:T], ALU.mult))
                dve.sem_inc(bonus_out, 1)
                link(V.memset(X[:, :, 0:LV * CH], 0.0))
                dve.sem_inc(x_zeroed, 1)

                def masks(c):
                    kind = "s" if c == NCH - 1 else "p"
                    g, tb = G[c % 2], TB[c % 2]
                    dve.wait_ge(gram, c + 1)
                    mG = bc(cst["gram_" + kind].rearrange("p (b s) -> p b s", b=2).unsqueeze(1), [P, 4, 2, CH])
                    m0 = cst["lvl0_" + kind].rearrange("p (b s) -> p b s", b=2)
                    link(V.tensor_tensor(g[:, 0], psG[:, 0], mG, ALU.mult))
                    mL = cst["levels"].rearrange("p (l s) -> p l s", l=LV)
                    n = levels(c)
                    V.tensor_tensor(NT[:, :, 0:n], bc(g[:, 0, :, 0, :].unsqueeze(2), [P, 4, n, CH]),
                                    bc(mL[:, 0:n].unsqueeze(1), [P, 4, n, CH]), ALU.mult)
                    V.tensor_tensor(tb[:, :, 0, :], psN, bc(m0[:, 0:1, :], [P, 4, CH]), ALU.mult)
                    link(V.tensor_tensor(tb[:, :, 1, :], g[:, 0, :, 0, :], bc(m0[:, 1:2, :], [P, 4, CH]), ALU.mult))
                    tb8 = tb.rearrange("p a b s -> p (a b) s")
                    link(V.tensor_tensor(tb8, tb8, bc(cst["eye2"].unsqueeze(1), [P, 8, CH]), ALU.add))
                    dve.sem_inc(gram_out, 1)
                    V.tensor_tensor(g[:, 1], psG[:, 1], mG, ALU.mult).then_inc(g1_out, 1)

                def level(c, l):
                    tb = TB[c % 2]
                    dve.wait_ge(t_mm, c * LV + l + 1)
                    if l < LV - 1:
                        o = parity(tb[:, :, 0], l, 0)
                        V.tensor_tensor(o, o, packed(psT[:, :, 0], l), ALU.add)
                    o = parity(tb[:, :, 1], l, 1)
                    V.tensor_tensor(o, o, packed(psT[:, :, 1], l), ALU.add).then_inc(t_out, 1)
                    dve.wait_ge(t_out, c * LV + l + 1)

                def center(c):
                    dve.wait_ge(y_out, c + 1)
                    m = st1[:, 4 * c:4 * c + 4]
                    link(V.reduce_sum(m, Yt[:, c], AX_X))
                    link(V.tensor_scalar(m, m, 1.0 / HD, None, ALU.mult))
                    link(V.tensor_tensor(Yt[:, c], Yt[:, c], bc(m.unsqueeze(2), [P, 4, HD]), ALU.subtract))
                    link(V.tensor_tensor(ysq[:], Yt[:, c], Yt[:, c], ALU.mult))
                    link(V.reduce_sum(st2[:, 4 * c:4 * c + 4], ysq[:], AX_X))

                for c in range(-1, NCH - 1):
                    masks(c + 1)
                    if c >= 0:
                        dve.wait_ge(y_mm, c + 1)
                        link(V.tensor_tensor(S[:], S[:], bc(wc[:, :, c:c + 1], [P, 4, HD]), ALU.mult))
                    level(c + 1, 0)
                    if c >= 0:
                        dve.wait_ge(s_mm, c + 1)
                        V.tensor_tensor(S[:], S[:], psS, ALU.add).then_inc(s_out, 1)
                        dve.wait_ge(s_out, c + 1)
                    for l in range(1, levels(c + 1)):
                        level(c + 1, l)
                        if l == 1 and c >= 0:
                            center(c)
                center(NCH - 2)
                dve.wait_ge(u_out, NCH)
                seq = bc(cst["seq"].unsqueeze(2), [P, NB, HD])

                def spread(pr):
                    e = expd[pr % 2]
                    if pr >= 2:
                        dve.wait_ge(sf_mm, pr - 1)
                    V.tensor_tensor(e[:, 0], bc(U[:, pr, :].unsqueeze(1), [P, NB, HD]), seq, ALU.mult)
                    link(V.tensor_tensor(e[:, 1], bc(tok[(NCH - 1) % 2][:, 0, pr, :].unsqueeze(1), [P, NB, HD]), seq, ALU.mult))
                    dve.sem_inc(exp_out, 1)

                spread(0)
                link(V.tensor_tensor(S0, S0, bc(wc[:, :, 8:16].unsqueeze(3), [P, 4, NB, HD]), ALU.mult))
                for pr in range(4):
                    if pr < 3:
                        spread(pr + 1)
                    dve.wait_ge(sf_mm, pr + 1)
                    V.tensor_tensor(S0[:, pr], S0[:, pr], PS[:, 512 * (pr % 2):512 * (pr % 2) + 512].rearrange(
                        "p (b i) -> p b i", b=NB), ALU.add).then_inc(sf_out, 1)
                center(NCH - 1)
                Yf = Yt[:].rearrange("p c a i -> p (c a) i")
                link(V.tensor_scalar(st2[:], st2[:], 1.0 / HD, GN_EPS, ALU.mult, ALU.add))
                dve.sem_inc(root_in, 1)
                dve.wait_ge(root_out, 5)
                link(V.reciprocal(st2[:], st2[:]))
                link(V.tensor_tensor(Yf, Yf, bc(st2[:].unsqueeze(2), [P, NCH * 4, HD]), ALU.mult))
                dve.sem_inc(gn_ready, 1)
                for pr in range(4):
                    dve.wait_ge(back_mm, pr + 1)
                    link(V.tensor_scalar(BD[:, pr, 0:T], PS[:, pr * 1024:pr * 1024 + T], Pm("ln_w", pr), Pm("ln_b", pr),
                                         ALU.mult, ALU.add))
                    link(V.tensor_tensor(BD[:, pr, 0:T], BD[:, pr, 0:T], a_[:, pr, 0:T], ALU.add))
                    V.tensor_tensor(BD[:, pr, 0:T], BD[:, pr, 0:T], g_[:, pr, 0:T], ALU.mult).then_inc(oa_ready, 1)

            @block.scalar
            def _(act):
                link = Chain(act, achain)
                A = nc.scalar.activation
                act.wait_ge(mixed, 1)
                link(A(tw, zm[0:32, 12, 0:T], ACT.Tanh))
                link(A(sg, zm[0:96, 13, 0:T], ACT.Sigmoid))
                act.sem_inc(lora_in, 1)
                act.wait_ge(mixed, 2)
                act.wait_ge(v_mixed, 1)
                for c in range(4):
                    act.wait_ge(lora_mm, 3 * c + 1)
                    A(lw[:, c, 0:T], wide(3 * c), ACT.Sigmoid, bias=Pm("w0", c)).then_inc(lora_out, 1)
                    act.wait_ge(lora_mm, 3 * c + 2)
                    A(a_[:, c, 0:T], wide(3 * c + 1), ACT.Sigmoid, bias=Pm("a0", c)).then_inc(lora_out, 1)
                    act.wait_ge(lora_mm, 3 * c + 3)
                    A(g_[:, c, 0:T], wide(3 * c + 2), ACT.Copy).then_inc(lora_out, 1)
                for c in range(4):
                    act.wait_ge(root_in, c + 1)
                    A(kka[:, c, 0:T], kka[:, c, 0:T], ACT.Sqrt).then_inc(root_out, 1)
                act.wait_ge(L_ready, 1)
                A(KD[:, :, 0:T], KD[:, :, 0:T], ACT.Exp).then_inc(exps, 1)
                A(BD[:, :, 0:T], L[:, :, 0:T], ACT.Exp).then_inc(exps, 1)
                A(E3[:, :, 0:T], L[:, :, 0:T], ACT.Exp, scale=-1.0).then_inc(exps, 1)
                act.wait_ge(L_ready, 2)
                A(lw[:, :, 0:T], lw[:, :, 0:T], ACT.Exp).then_inc(exps, 1)
                A(wc[:, :, 0:8], L[:, :, CH - 1:TPR:CH], ACT.Exp)
                A(wc[:, :, 8:16], L[:, :, TPR + TS - 1:T:TS], ACT.Exp).then_inc(exps, 1)
                act.wait_ge(ops_ready, 1)
                act.wait_ge(x_zeroed, 1)

                def level(c, l):
                    act.wait_ge(x_mm, c * LV + l + 1)
                    A(parity(X[:, :, xl(l)], l, 0), packed(psX, l), ACT.Copy).then_inc(x_out, 1)

                for c in range(-1, NCH):
                    if c < NCH - 1:
                        if c + 1 == NCH - 1:
                            act.wait_ge(s_init, 1)
                            act.wait_ge(sat_mm, 1)
                            A(SAT[:, :, :, 0:TSM], psSAT[:, :, :, 0:TSM], ACT.Copy).then_inc(sat_out, 1)
                    if c >= 0:
                        act.wait_ge(u0_mm, c + 1)
                        A(U0[:], psU0, ACT.Copy).then_inc(u0_out, 1)
                        act.wait_ge(u_mm, c + 1)
                        if c:
                            act.wait_ge(s_mm, c)
                        A(U[:], psU, ACT.Copy).then_inc(u_out, 1)
                    if c < NCH - 1:
                        level(c + 1, 0)
                    if c >= 0:
                        act.wait_ge(y_mm, c + 1)
                        A(Yt[:, c], psY, ACT.Copy).then_inc(y_out, 1)
                    if c < NCH - 1:
                        for l in range(1, levels(c + 1)):
                            level(c + 1, l)
                        act.wait_ge(tok_mm, 3 * (c + 2))
                        A(tok[(c + 1) % 2], psTok, ACT.Copy).then_inc(tok_out, 1)
                act.wait_ge(root_in, 5)
                A(st2[:], st2[:], ACT.Sqrt).then_inc(root_out, 1)

            @block.tensor
            def _(pe):
                M = nc.tensor.matmul
                pe.wait_ge(lora_w, 32)
                pe.wait_ge(lora_in, 1)
                for c in range(4):
                    cs = slice(c * P, (c + 1) * P)
                    for j, (lhsT, rhs) in enumerate(((wup[0:32, cs], tw), (wup[32:64, cs], zm[32:64, 12, 0:T]),
                                                     (wgu[:, cs], sg))):
                        u = 3 * c + j
                        if u >= 4:
                            pe.wait_ge(lora_out, u - 3)
                        mmT(u, P, lhsT, rhs).then_inc(lora_mm, 1)
                for c in range(4):
                    pe.wait_ge(kk2_ready, c + 1)
                    pe.wait_ge(lora_out, 9 + c)
                    mmT(c, P, cst["blockones"], kka[:, c, 0:T]).then_inc(kk_mm, 1)
                pe.wait_ge(kk_used, 1)
                pe.wait_ge(ops_ready, 1)
                for c in range(4):
                    mmT(c, P, cst["blockones"], kka[:, c, 0:T]).then_inc(bonus_mm, 1)
                pe.wait_ge(bonus_out, 1)
                pe.wait_ge(s_init, 1)

                def grams(c):
                    ts = slice(c * CH, (c + 1) * CH)
                    if c == NCH - 1:
                        pe.wait_ge(s0_in, 16)
                        pe.wait_ge(g1_out, c)
                        for pr in range(4):
                            for b in range(NB):
                                for h in halves:
                                    s4 = slice(TPR + TS * b, TPR + TS * b + TS)
                                    last = M(psSAT[h, pr, :, TS * b:TS * b + TS], S0[h, pr, b, :], AR[h, pr, :, s4],
                                             start=True, stop=True)
                        last.then_inc(sat_mm, 1)
                        pe.wait_ge(sat_out, 1)
                    if c:
                        pe.wait_ge(g1_out, c)
                    for pr in range(4):
                        for h in halves:
                            for k2 in range(2):
                                M(psG[h, k2, pr], BK[h, pr, k2, ts], AR[h, pr, :, ts], start=True, stop=True)
                            last = M(psN[h, pr], AR[h, pr, 0, ts], BK[h, pr, 0, ts], start=True, stop=True)
                    last.then_inc(gram, 1)

                def token_major(c, k3):
                    if c:
                        pe.wait_ge(tok_out, c)
                    if k3 == 2 and c >= 1:
                        pe.wait_ge(s_out, c)
                    for pr in range(4):
                        for h in halves:
                            last = M(psTok[h, k3, pr], (v_, BD, KD)[k3][h, pr, c * CH:(c + 1) * CH],
                                     cst["eye2"][h, :], start=True, stop=True)
                    last.then_inc(tok_mm, 1)

                def level_x(c, l):
                    pe.wait_ge(gram_out, c + 1)
                    if l:
                        pe.wait_ge(t_out, c * LV + l)
                    for pr in range(4):
                        for h in halves:
                            last = M(packed(psX[h, pr], l), NT[h, pr, l], parity(TB[c % 2][h, pr, 0], l, 0),
                                     start=True, stop=True)
                    last.then_inc(x_mm, 1)

                def level_t(c, l):
                    pe.wait_ge(x_out, c * LV + l + 1)
                    for pr in range(4):
                        for h in halves:
                            if l < LV - 1:
                                M(packed(psT[h, pr, 0], l), TB[c % 2][h, pr, 1], parity(X[h, pr, xl(l)], l, 0),
                                  start=True, stop=True)
                            last = M(packed(psT[h, pr, 1], l), X[h, pr, xl(l)], parity(TB[c % 2][h, pr, 1], l, 1),
                                     start=True, stop=True)
                    last.then_inc(t_mm, 1)

                def solve(c):
                    g, tk, ts = G[c % 2], tok[c % 2], slice(c * CH, (c + 1) * CH)
                    pe.wait_ge(t_out, c * LV + levels(c))
                    pe.wait_ge(tok_out, c + 1)
                    pe.wait_ge(g1_out, c + 1)
                    if c:
                        pe.wait_ge(s_out, min(c, NCH - 1))
                    for pr in range(4):
                        for h in halves:
                            if c < NCH - 1:
                                M(psU0[h, pr], AR[h, pr, 0, ts], S[h, pr], start=True, stop=False)
                            else:
                                M(psU0[h, pr], SAT[h, pr, 0], cst["eye2"][h, :], start=True, stop=False)
                            last = M(psU0[h, pr], g[h, 1, pr, 0], tk[h, 0, pr], start=False, stop=True)
                    last.then_inc(u0_mm, 1)
                    if c < NCH - 1:
                        token_major(c + 1, 0)
                    pe.wait_ge(u0_out, c + 1)
                    for pr in range(4):
                        for h in halves:
                            last = M(psU[h, pr], TB[c % 2][h, pr, 1], U0[h, pr], start=True, stop=True)
                    last.then_inc(u_mm, 1)

                def outputs(c):
                    g, tk, ts = G[c % 2], tok[c % 2], slice(c * CH, (c + 1) * CH)
                    pe.wait_ge(u_out, c + 1)
                    if c:
                        pe.wait_ge(y_out, c)
                    for pr in range(4):
                        for h in halves:
                            if c < NCH - 1:
                                M(psY[h, pr], AR[h, pr, 1, ts], S[h, pr], start=True, stop=False)
                            else:
                                M(psY[h, pr], SAT[h, pr, 1], cst["eye2"][h, :], start=True, stop=False)
                            M(psY[h, pr], g[h, 1, pr, 1], tk[h, 0, pr], start=False, stop=False)
                            last = M(psY[h, pr], g[h, 0, pr, 1], U[h, pr], start=False, stop=True)
                    last.then_inc(y_mm, 1)

                def state(c):
                    tk = tok[c % 2]
                    for pr in range(4):
                        for h in halves:
                            M(psS[h, pr], tk[h, 1, pr], U[h, pr], start=True, stop=False)
                            last = M(psS[h, pr], tk[h, 2, pr], tk[h, 0, pr], start=False, stop=True)
                    last.then_inc(s_mm, 1)

                for c in range(-1, NCH):
                    if c < NCH - 1:
                        grams(c + 1)
                    if c >= 0:
                        solve(c)
                    if c < NCH - 1:
                        level_x(c + 1, 0)
                    if c >= 0:
                        outputs(c)
                    if c < NCH - 1:
                        level_t(c + 1, 0)
                        if c >= 0:
                            state(c)
                        n = levels(c + 1)
                        for l in range(1, n):
                            level_x(c + 1, l)
                            level_t(c + 1, l)
                            if l < 3:
                                token_major(c + 1, l)
                            elif l == 3 and c < 0:
                                token_major(c + 1, 0)
                        for k3 in range(n, 3):
                            token_major(c + 1, k3)
                tk = tok[(NCH - 1) % 2]
                for pr in range(4):
                    pe.wait_ge(exp_out, pr + 1)
                    if pr >= 2:
                        pe.wait_ge(sf_out, pr - 1)
                    for h in halves:
                        o = 512 * (pr % 2)
                        M(PS[h, o:o + 512], tk[h, 1, pr], expd[pr % 2][h, 0], start=True, stop=False)
                        last = M(PS[h, o:o + 512], tk[h, 2, pr], expd[pr % 2][h, 1], start=False, stop=True)
                    last.then_inc(sf_mm, 1)
                pe.wait_ge(gn_ready, 1)
                pe.wait_ge(sf_out, 4)
                for pr in range(4):
                    for c in range(NCH):
                        for h in halves:
                            o = pr * 1024 + c * CH
                            last = M(PS[h, o:o + CH], Yt[h, c, pr], cst["eye2"][h, :], start=True, stop=True)
                    last.then_inc(back_mm, 1)


def load_pages(eng, table, dst, pool, half, arrived, seqs=range(4)):
    for b in seqs:
        with eng.Fori(0, NPAGES // 4) as i:
            pages = [eng.value_load(table[0:1, bass.ds(4 * i + ((4 * half + b) * NPAGES + j), 1)], min_val=0,
                                    max_val=pool.shape[0] - 1) for j in range(4)]
            for j, page in enumerate(pages):
                src = pool[bass.ds(page, 1)].rearrange("a p k t -> p (a k) t")
                eng.dma_start(dst(b, 4 * i + j), src).then_inc(arrived, 16)


def compress(nc, io, PS, sem, cst, table, kcT_p, vc_p, kcT_s, vc_s):
    with ExitStack() as ctx:
        def t(name, shape, dt=F32):
            return ctx.enter_context(nc.sbuf_tensor(name, shape, dt))

        w1 = t("c_w1", [P, 2, 32, P])
        w2 = t("c_w2", [P, 2, P])
        pe2 = t("c_pe", [P, 2, 32])
        gain = t("c_gain", [P, HD])
        rows = t("c_rows", [P, 4, 256])
        cols = t("c_cols", [P, 2, 32, NKC_P + 1])
        cT = [t(f"c_cT{h}", [P, 4, 2, PAST]) for h in range(2)]
        bias = t("c_bias", [P, 2])
        hid = t("c_hid", [P, 2, 512])
        kraw = t("c_kraw", [P, 4, 2, P])
        ksq = t("c_ksq", [P, 4, P])
        ss = t("c_ss", [P, 8])
        kdup = t("c_kdup", [P, 2, 2, HD])

        w_in, rows_in, pages = sem("c_w_in"), sem("c_rows_in"), [sem("c_pages0"), sem("c_pages1")]
        table_in, pages_pool = sem("c_table_in"), [sem("c_pages_pool0"), sem("c_pages_pool1")]
        tr_mm, tr_out = sem("c_tr_mm"), sem("c_tr_out")
        bias_out, hid_mm, hid_out = sem("c_bias_out"), sem("c_hid_mm"), sem("c_hid_out")
        kc_mm, kc_out, root_in, root_out = sem("c_kc_mm"), sem("c_kc_out"), sem("c_root_in"), sem("c_root_out")
        normed, kT_mm, kT_out, dchain = sem("c_normed"), sem("c_kT_mm"), sem("c_kT_out"), sem("c_dchain")
        ins = [(NKC_P, 1), (4 * NKC_S, 4), (4 * NKC_S, 4)]

        with nc.Block() as block:
            @block.sync
            def _(sp):
                sp.dma_start(table[:], io["page_table"]).then_inc(table_in, 16)
                sp.dma_start(rows[:], io["kvc"][0:TPR, :].rearrange("(i p) n -> p i n", p=P)).then_inc(rows_in, 16)
                sp.wait_ge(table_in, 16)
                for hf in range(2):
                    load_pages(sp, table, lambda b, i: cT[hf][:, b, :, bass.ds(i * PAGE, PAGE)], io["cmp_pool"], hf,
                               pages[hf], (0, 1))

            @block.gpsimd
            def _(pool):
                pool.wait_ge(table_in, 16)
                for hf in range(2):
                    load_pages(pool, table, lambda b, i: cT[hf][:, b, :, bass.ds(i * PAGE, PAGE)], io["cmp_pool"], hf,
                               pages_pool[hf], (2, 3))

            @block.tensor
            def _(pe):
                M = nc.tensor.matmul
                pe.wait_ge(rows_in, 16)
                for kv in range(2):
                    for i in range(4):
                        last = nc.tensor.transpose(PS[:, kv * 512 + i * P:kv * 512 + i * P + P],
                                                   rows[:, i, kv * P:kv * P + P], cst["ident"])
                last.then_inc(tr_mm, 1)
                pe.wait_ge(w_in, 64)
                pe.wait_ge(tr_out, 2)
                for r, (n, nb) in enumerate(ins):
                    if r:
                        pe.wait_ge(pages[r - 1], 16 * 2 * NPAGES)
                        pe.wait_ge(pages_pool[r - 1], 16 * 2 * NPAGES)
                    for kv in range(2):
                        if r:
                            pe.wait_ge(hid_out, 2 * r - 1 + kv)
                        for l in range(32):
                            if r == 0:
                                rhs = cols[:, kv, l, :]
                            else:
                                rhs = cT[r - 1][:, :, kv, l:l + 16 * (NKC_S - 1) + 1:16]
                            last = M(PS[:, 2048 + 512 * kv:2048 + 512 * kv + n + (r == 0)], w1[:, kv, l, :], rhs,
                                     start=(l == 0), stop=(l == 31))
                        last.then_inc(hid_mm, 1)
                    pe.wait_ge(hid_out, 2 * r + 2)
                    if r:
                        pe.wait_ge(kc_out, r)
                    nk = n // nb
                    for b in range(nb):
                        for kv in range(2):
                            o = 3072 + (b * 2 + kv) * P
                            last = M(PS[0:nk, o:o + P], hid[:, kv, b * nk:b * nk + nk], w2[:, kv, :],
                                     start=True, stop=True)
                    last.then_inc(kc_mm, 1)
                    pe.wait_ge(normed, r + 1)
                    if r == 0:
                        for g in range(2):
                            last = nc.tensor.transpose(PS[:, 1536 + g * 32:1536 + g * 32 + nk],
                                                       kdup[0:nk, g].rearrange("p a d -> p (a d)"), cst["ident"][0:nk, 0:nk])
                    else:
                        pe.wait_ge(kT_out, r)
                        for b in range(nb):
                            last = nc.tensor.transpose(PS[:, 1536 + b * P:1536 + b * P + nk], kraw[0:nk, b, 0, :],
                                                       cst["ident"][0:nk, 0:nk])
                    last.then_inc(kT_mm, 1)

            @block.scalar
            def _(act):
                A = nc.scalar.activation
                act.dma_start(w1[:], io["cmp_w1"]).then_inc(w_in, 16)
                act.dma_start(pe2[:], io["cmp_pe"]).then_inc(w_in, 16)
                act.dma_start(w2[:], io["cmp_w2"]).then_inc(w_in, 16)
                act.dma_start(gain[:], io["kc_gain"]).then_inc(w_in, 16)
                act.wait_ge(tr_mm, 1)
                for kv in range(2):
                    for a in range(2):
                        src = PS[:, 512 * kv + 16 * a:512 * kv + 16 * (a + NKC_P)].rearrange("p (n l) -> p l n", l=16)
                        last = A(cols[:, kv, 16 * a:16 * a + 16, 0:NKC_P], src, ACT.Copy)
                last.then_inc(tr_out, 1)
                act.wait_ge(bias_out, 1)
                for r, (n, nb) in enumerate(ins):
                    nk = n // nb
                    for kv in range(2):
                        act.wait_ge(hid_mm, 2 * r + kv + 1)
                        if r:
                            act.wait_ge(kc_mm, r)
                        A(hid[:, kv, 0:n], PS[:, 2048 + 512 * kv:2048 + 512 * kv + n], ACT.Silu,
                          bias=bias[:, kv:kv + 1]).then_inc(hid_out, 1)
                    act.wait_ge(root_in, r + 1)
                    A(ss[0:nk, 0:2 * nb], ss[0:nk, 0:2 * nb], ACT.Sqrt).then_inc(root_out, 1)

            @block.vector
            def _(dve):
                link = Chain(dve, dchain)
                V = nc.vector
                dve.wait_ge(w_in, 64)
                V.tensor_copy(cols[:, :, :, NKC_P], pe2[:]).then_inc(tr_out, 1)
                dve.wait_ge(hid_mm, 2)
                par = io["P"]
                for kv, name in enumerate(("b1k", "b1v")):
                    o = 2048 + 512 * kv + NKC_P
                    link(V.tensor_tensor(bias[:, kv:kv + 1], PS[:, o:o + 1], par(name), ALU.add))
                dve.sem_inc(bias_out, 1)
                for r, (n, nb) in enumerate(ins):
                    nk = n // nb
                    dve.wait_ge(kc_mm, r + 1)
                    if r:
                        dve.wait_ge(kT_mm, r)
                    ps = PS[0:nk, 3072:3072 + nb * 256].rearrange("p (b k n) -> p b k n", b=nb, k=2)
                    link(V.tensor_copy(kraw[0:nk, 0:nb], ps))
                    dve.sem_inc(kc_out, 1)
                    k = kraw[0:nk, 0:nb, 0, :].rearrange("p b (g d) -> p b g d", g=2)
                    q = ksq[0:nk, 0:nb].rearrange("p b (g d) -> p b g d", g=2)
                    s = ss[0:nk, 0:2 * nb]
                    s3 = s.rearrange("p (b g) -> p b g", g=2)
                    link(V.tensor_tensor(q, k, k, ALU.mult))
                    link(V.reduce_sum(s3, q, AX_X))
                    link(V.tensor_scalar(s, s, 1.0 / HD, RMS_EPS, ALU.mult, ALU.add))
                    dve.sem_inc(root_in, 1)
                    dve.wait_ge(root_out, r + 1)
                    link(V.reciprocal(s, s))
                    link(V.tensor_tensor(k, k, s3.unsqueeze(3).to_broadcast([nk, nb, 2, HD]), ALU.mult))
                    gb = gain[0:nk].unsqueeze(1).unsqueeze(1).to_broadcast([nk, nb, 2, HD])
                    link(V.tensor_tensor(k, k, gb, ALU.mult))
                    if r == 0:
                        for a in range(2):
                            link(V.tensor_copy(kdup[0:nk, :, a, :], k[:, 0]))
                        link(V.tensor_copy(vc_p[0:nk, :], kraw[0:nk, 0, 1, :]))
                        dve.sem_inc(normed, 1)
                        dve.wait_ge(kT_mm, 1)
                        link(V.tensor_copy(kcT_p[:], PS[:, 1536:1600].rearrange("p (g n) -> p g n", g=2)[:, :, 0:nk]))
                    else:
                        b0 = 4 * (r - 1)
                        link(V.tensor_copy(vc_s[0:nk, b0:b0 + 4, :], kraw[0:nk, :, 1, :]))
                        dve.sem_inc(normed, 1)
                        dve.wait_ge(kT_mm, r + 1)
                        link(V.tensor_copy(kcT_s[:, b0:b0 + 4, :],
                                           PS[:, 1536:2048].rearrange("p (b n) -> p b n", b=4)[:, :, 0:nk]))
                    dve.sem_inc(kT_out, 1)


def prompt_attention(nc, io, PS, sem, cst, kcT_p, vc_p, table, kv, wkv):
    with ExitStack() as ctx:
        def t(name, shape, dt=F32):
            return ctx.enter_context(nc.sbuf_tensor(name, shape, dt))

        qrow = t("a_qrow", [P, 4, 512])
        krow = t("a_krow", [P, 2, 4, 2, 2, HD])
        vrow = t("a_vrow", [P, 2, 4, P])
        gate = t("a_gate", [P, 4, 3, 8])
        qT = t("a_qT", [P, 4, TPR])
        qs = t("a_qs", [P, 8, TPR], F32R)
        k_hi, k_lo = t("a_k_hi", [P, 2, 2, TPR], F32R), t("a_k_lo", [P, 2, 2, TPR], F32R)
        E = t("a_E", [P, 2, 2, TPR])
        kT = E
        Ec = t("a_Ec", [P, 2, 16, NKC_P])
        pT = t("a_pT", [P, 2, 2, TPR])
        pcT = t("a_pcT", [32, 4, 8, P])
        cm, cs = t("a_cm", [P, 2, 16]), t("a_cs", [P, 2, 16])
        mx = t("a_mx", [P, 2, 2])
        sm = t("a_sm", [P, 2, 2])
        co = t("a_co", [P, 3, 2])
        ob = t("a_ob", [P, 4, 512])
        obT = qrow

        halves = (slice(0, 64), slice(64, 128))
        split_hi, split_lo = sem("a_split_hi"), sem("a_split_lo")
        units = [(i, hh) for i in range(4) for hh in range(8)]
        N = len(units)
        rows_in, tr_mm, tr_out = sem("a_rows_in"), sem("a_tr_mm"), sem("a_tr_out")
        score_mm, masked, exped = sem("a_score_mm"), sem("a_masked"), sem("a_exped")
        c_mm, c_in, c_exp, c_ready = sem("a_c_mm"), sem("a_c_in"), sem("a_c_exp"), sem("a_c_ready")
        cT_mm, cT_out, co_mm, co_out = sem("a_cT_mm"), sem("a_cT_out"), sem("a_co_mm"), sem("a_co_out")
        pT_mm, pT_act, pT_dve = sem("a_pT_mm"), sem("a_pT_act"), sem("a_pT_dve")
        o_mm, o_out, ob_mm, ob_out = sem("a_o_mm"), sem("a_o_out"), sem("a_ob_mm"), sem("a_ob_out")
        dchain, stored, ahead = sem("a_dchain"), sem("a_stored"), sem("a_ahead")

        def psS(u, br):
            return PS[:, 1024 * (u % 2) + 512 * br:1024 * (u % 2) + 512 * br + 512]

        def psP(br):
            return PS[:, 2048 + 512 * br:2560 + 512 * br]

        def psO(u):
            return PS[:, 3072 + 512 * (u % 2):3072 + 512 * (u % 2) + 128].rearrange("p (b d) -> p b d", b=2)

        with nc.Block() as block:
            @block.sync
            def _(sp):
                sp.dma_start(qrow[:], io["q_dram"][0:TPR, :].rearrange("(i p) n -> p i n", p=P)).then_inc(rows_in, 16)
                for br, src in enumerate((io["kvs"], io["kvw"])):
                    rr = src[0:TPR, :].rearrange("(i p) n -> p i n", p=P)
                    for i in range(4):
                        for a in range(2):
                            sp.dma_start(krow[:, br, i, :, a, :], rr[:, i, 0:P].rearrange("p (g d) -> p g d", g=2)
                                         ).then_inc(rows_in, 16)
                    sp.dma_start(vrow[:, br], rr[:, :, P:256]).then_inc(rows_in, 16)
                sp.dma_start(gate[:], io["gate_dram"][0:TPR, :].rearrange("(i p) (b h) -> p i b h", p=P, b=3)).then_inc(rows_in, 16)
                for b in range(4):
                    sp.dma_start(wkv[:, b], io["win_kv"][b]).then_inc(ahead, 16)
                load_pages(sp, table, lambda b, i: kv[:, b, bass.ds(i, 1)].rearrange("p a k t -> p (a k) t"),
                           io["slc_pool"], 0, ahead)
                sp.dma_start(io["win_s"][:, 0:508], io["win_cache"][:, TS:512]).then_inc(stored, 16)
                sp.dma_start(io["win_s"][:, 508:512], io["kvw"][TPR:T, :].rearrange("(b t) n -> b t n", b=NB)
                             ).then_inc(stored, 16)
                sp.wait_ge(ob_out, 4)
                sp.dma_start(io["ob_dram"][:, :, 0:TPR], obT[:]).then_inc(stored, 16)
                sp.wait_ge(stored, 48)
                sp.wait_ge(ahead, 16 * (4 + 4 * NPAGES))

            n_in = 16 * 20

            @block.tensor
            def _(pe):
                M, X = nc.tensor.matmul, nc.tensor.transpose
                pe.wait_ge(rows_in, n_in)
                for j in range(8):
                    o = 512 * j
                    for i in range(4):
                        src = qrow[:, i, j * P:j * P + P] if j < 4 else \
                            krow[:, (j - 4) // 2, i, (j - 4) % 2].rearrange("p a d -> p (a d)")
                        last = X(PS[:, o + i * P:o + i * P + P], src, cst["ident"])
                    last.then_inc(tr_mm, 1)
                pe.wait_ge(tr_out, 8)
                for i, hh in units:
                    h = slice(64 * (hh % 2), 64 * (hh % 2) + 64)
                    o = 512 * (hh % 2) + NKC_P * (4 * i + hh // 2)
                    last = M(PS[:, o:o + NKC_P], qT[h, hh // 2, i * P:i * P + P], kcT_p[h, hh // 4, :],
                             start=True, stop=True)
                    if hh % 2:
                        last.then_inc(c_mm, 1)
                pe.wait_ge(c_ready, 1)
                for i in range(4):
                    for hh in range(8):
                        o = 1024 * i + P * hh
                        last = X(PS[0:NKC_P, o:o + P], Ec[:, hh % 2, 4 * i + hh // 2, :], cst["ident"])
                    last.then_inc(cT_mm, 1)
                pe.wait_ge(cT_out, 4)
                for u, (i, hh) in enumerate(units):
                    last = M(PS[:, HD * u:HD * u + HD], pcT[0:NKC_P, i, hh, :], vc_p[0:NKC_P, 64 * (hh // 4):64 * (hh // 4) + 64],
                             start=True, stop=True)
                last.then_inc(co_mm, 1)
                pe.wait_ge(co_out, 1)
                pe.wait_ge(split_lo, 12)

                def scores(u):
                    i, hh = units[u]
                    q = qs[:, hh, i * P:i * P + P]
                    if u >= 2:
                        pe.wait_ge(exped, u - 1)
                    n = P * (i + 1)
                    for br in range(2):
                        M(psS(u, br)[:, 0:n], q, k_hi[:, br, hh // 4, 0:n], start=True, stop=False)
                        last = M(psS(u, br)[:, 0:n], q, k_lo[:, br, hh // 4, 0:n], start=False, stop=True)
                    last.then_inc(score_mm, 1)

                def turn(u):
                    i, hh = units[u]
                    pe.wait_ge(exped, u + 1)
                    if u:
                        pe.wait_ge(pT_act, u)
                        pe.wait_ge(pT_dve, u)
                    for br in range(2):
                        for j in range(i + 1):
                            last = X(psP(br)[:, j * P:j * P + P], E[:, u % 2, br, j * P:j * P + P], cst["ident"])
                    last.then_inc(pT_mm, 1)

                def values(u):
                    i, hh = units[u]
                    g = slice(64 * (hh // 4), 64 * (hh // 4) + 64)
                    pe.wait_ge(pT_act, u + 1)
                    pe.wait_ge(pT_dve, u + 1)
                    if u >= 2:
                        pe.wait_ge(o_out, u - 1)
                    for br in range(2):
                        for j in range(i + 1):
                            last = M(psO(u)[:, br], pT[:, u % 2, br, j * P:j * P + P], vrow[:, br, j, g],
                                     start=(j == 0), stop=(j == i))
                    last.then_inc(o_mm, 1)
                    if hh == 7:
                        pe.wait_ge(o_out, u + 1)
                        pe.wait_ge(pT_act, u + 1)
                        if i < 3:
                            pe.wait_ge(pT_act, u + 2)
                            pe.wait_ge(pT_dve, u + 2)
                        for c in range(4):
                            last = X(psP(0)[:, c * P:c * P + P], ob[:, i, c * P:c * P + P], cst["ident"])
                        last.then_inc(ob_mm, 1)
                        pe.wait_ge(ob_out, i + 1)

                for k in range(N + 2):
                    if k < N:
                        scores(k)
                    if 1 <= k <= N:
                        turn(k - 1)
                    if k >= 2:
                        values(k - 2)

            @block.vector
            def _(dve):
                link = Chain(dve, dchain)
                V = nc.vector
                for j in range(1, 8, 2):
                    dve.wait_ge(tr_mm, j + 1)
                    dst = qT[:, j, :] if j < 4 else kT[:, (j - 4) // 2, (j - 4) % 2, :]
                    link(V.tensor_copy(dst, PS[:, 512 * j:512 * j + 512]))
                    dve.sem_inc(tr_out, 1)
                dve.wait_ge(tr_out, 8)
                for hh in range(8):
                    h, o = halves[hh % 2], halves[1 - hh % 2]
                    dve.wait_ge(split_hi, hh + 1)
                    V.tensor_tensor(qs[o, hh], qT[h, hh // 2, :], qs[h, hh].bitcast(F32), ALU.subtract).then_inc(split_lo, 1)
                for j in range(4):
                    dve.wait_ge(split_hi, 9 + j)
                    V.tensor_tensor(k_lo[:, j // 2, j % 2], kT[:, j // 2, j % 2], k_hi[:, j // 2, j % 2].bitcast(F32),
                                    ALU.subtract).then_inc(split_lo, 1)

                def tiles(ap):
                    return ap.rearrange("p (i h) n -> p i h n", i=4)

                neg, keep = (cst[n].rearrange("p (i n) -> p i n", i=4).unsqueeze(2).to_broadcast([P, 4, 4, NKC_P])
                             for n in ("cmpneg_p", "cmp_p"))
                dve.wait_ge(c_mm, 16)
                for par in range(2):
                    src = PS[:, 512 * par:512 * par + 16 * NKC_P].rearrange("p (u n) -> p u n", n=NKC_P)
                    link(V.tensor_tensor(tiles(Ec[:, par]), tiles(src), neg, ALU.add))
                link(V.reduce_max(cm[:], Ec[:], AX_X))
                link(V.tensor_tensor(Ec[:], Ec[:], cm[:].unsqueeze(3).to_broadcast([P, 2, 16, NKC_P]), ALU.subtract))
                dve.sem_inc(c_in, 1)
                dve.wait_ge(c_exp, 1)
                for par in range(2):
                    link(V.tensor_tensor(tiles(Ec[:, par]), tiles(Ec[:, par]), keep, ALU.mult))
                link(V.reduce_sum(cs[:], Ec[:], AX_X))
                link(V.tensor_scalar(cs[:], cs[:], 1e-30, None, ALU.max))
                link(V.reciprocal(cs[:], cs[:]))
                for par in range(2):
                    c3 = cs[:, par].rearrange("p (i h) -> p i h", i=4)
                    link(V.tensor_tensor(c3, c3, gate[:, :, 0, par:8:2], ALU.mult))
                link(V.tensor_tensor(Ec[:], Ec[:], cs[:].unsqueeze(3).to_broadcast([P, 2, 16, NKC_P]), ALU.mult))
                dve.sem_inc(c_ready, 1)
                for i in (1, 3):
                    dve.wait_ge(cT_mm, i + 1)
                    V.tensor_copy(pcT[0:NKC_P, i], PS[0:NKC_P, 1024 * i:1024 * i + 1024].rearrange("p (h t) -> p h t", h=8)
                                  ).then_inc(cT_out, 1)
                dve.wait_ge(co_mm, 1)
                link(V.tensor_copy(ob[:], PS[:, 0:2048].rearrange("p (i n) -> p i n", i=4)))
                dve.sem_inc(co_out, 1)

                def mask(u):
                    i, hh = units[u]
                    dve.wait_ge(score_mm, u + 1)
                    n = P * (i + 1)
                    for br in range(2):
                        s = psS(u, br)
                        link(V.tensor_tensor(s[:, n - P:n], s[:, n - P:n], cst["tri"], ALU.add))
                        link(V.reduce_max(mx[:, u % 2, br:br + 1], s[:, 0:n], AX_X))
                    V.tensor_scalar(mx[:, u % 2, :], mx[:, u % 2, :], -0.125, None, ALU.mult).then_inc(masked, 1)

                def weigh(u):
                    i, hh = units[u]
                    dve.wait_ge(exped, u + 1)
                    c = co[:, u % 3, :]
                    link(V.reciprocal(c, sm[:, u % 2, :]))
                    link(V.tensor_tensor(c, c, gate[:, i, 1:3, hh], ALU.mult))
                    dve.wait_ge(pT_mm, u + 1)
                    if u >= 2:
                        dve.wait_ge(o_mm, u - 1)
                    n = P * (i + 1)
                    V.tensor_copy(pT[:, u % 2, 1, 0:n], psP(1)[:, 0:n]).then_inc(pT_dve, 1)

                def gather(u):
                    i, hh = units[u]
                    dve.wait_ge(o_mm, u + 1)
                    c, o = co[:, u % 3, :], ob[:, i, hh * HD:hh * HD + HD]
                    link(V.scalar_tensor_tensor(out=o, in0=psO(u)[:, 0], scalar=c[:, 0:1], in1=o,
                                                op0=ALU.mult, op1=ALU.add))
                    V.scalar_tensor_tensor(out=o, in0=psO(u)[:, 1], scalar=c[:, 1:2], in1=o,
                                           op0=ALU.mult, op1=ALU.add).then_inc(o_out, 1)
                    dve.wait_ge(o_out, u + 1)

                for k in range(N + 2):
                    if k < N:
                        mask(k)
                    if 1 <= k <= N:
                        weigh(k - 1)
                    if k >= 2:
                        gather(k - 2)

            @block.scalar
            def _(act):
                A = nc.scalar.activation

                def ob_copy(i):
                    act.wait_ge(ob_mm, i + 1)
                    nc.scalar.activation(obT[:, :, i * P:i * P + P], psP(0).rearrange("p (c t) -> p c t", c=4),
                                         ACT.Copy).then_inc(ob_out, 1)

                for j in range(0, 8, 2):
                    act.wait_ge(tr_mm, j + 1)
                    dst = qT[:, j, :] if j < 4 else kT[:, (j - 4) // 2, (j - 4) % 2, :]
                    A(dst, PS[:, 512 * j:512 * j + 512], ACT.Copy).then_inc(tr_out, 1)
                act.wait_ge(tr_out, 8)
                for hh in range(8):
                    h = halves[hh % 2]
                    A(qs[h, hh], qT[h, hh // 2, :], ACT.Copy).then_inc(split_hi, 1)
                for j in range(4):
                    A(k_hi[:, j // 2, j % 2], kT[:, j // 2, j % 2], ACT.Copy).then_inc(split_hi, 1)
                act.wait_ge(c_in, 1)
                A(Ec[:], Ec[:], ACT.Exp, scale=0.125).then_inc(c_exp, 1)
                for i in (0, 2):
                    act.wait_ge(cT_mm, i + 1)
                    A(pcT[0:NKC_P, i], PS[0:NKC_P, 1024 * i:1024 * i + 1024].rearrange("p (h t) -> p h t", h=8), ACT.Copy
                      ).then_inc(cT_out, 1)
                for k in range(N + 1):
                    if k < N:
                        i, hh = units[k]
                        n = P * (i + 1)
                        act.wait_ge(masked, k + 1)
                        if k >= 2:
                            act.wait_ge(pT_mm, k - 1)
                            act.wait_ge(pT_dve, k - 1)
                        for br in range(2):
                            last = A(E[:, k % 2, br, 0:n], psS(k, br)[:, 0:n], ACT.Exp, bias=mx[:, k % 2, br:br + 1],
                                     scale=0.125, accum_out=sm[:, k % 2, br:br + 1])
                        last.then_inc(exped, 1)
                    if k >= 1:
                        u = k - 1
                        i, hh = units[u]
                        act.wait_ge(pT_mm, u + 1)
                        if u >= 2:
                            act.wait_ge(o_mm, u - 1)
                        A(pT[:, u % 2, 0, 0:P * (i + 1)], psP(0)[:, 0:P * (i + 1)], ACT.Copy).then_inc(pT_act, 1)
                        if u >= 1 and units[u - 1][1] == 7:
                            ob_copy(units[u - 1][0])
                ob_copy(3)


def sample_attention(nc, io, PS, sem, cst, kcT_s, vc_s, table, kv_first, wkv):
    with ExitStack() as ctx:
        def t(name, shape, dt=F32):
            return ctx.enter_context(nc.sbuf_tensor(name, shape, dt))

        kvs = (kv_first, t("s_kv", [P, 4, NPAGES, 2, PAGE]))
        qrow = t("s_qrow", [TSM, 512])
        nrow = t("s_nrow", [TSM, 2, 256])
        gate = t("s_gate", [TSM, 24])
        Q = t("s_Q", [P, NB, 32])
        nT = t("s_nT", [P, 2, TSM])
        gr = t("s_gr", [P, 24])
        g3 = t("s_g3", [P, 3])
        Es = t("s_Es", [P, PAST + TSM])
        Ew = t("s_Ew", [P, 512 + TSM])
        Ec = t("s_Ec", [P, 128])
        mx, sm = t("s_mx", [P, 3]), t("s_sm", [P, 3])
        pT = t("s_pT", [P, 20, P])
        nTp = t("s_nTp", [TSM, 2, P])
        pcT = t("s_pcT", [P, P])
        imp0, imp, top = t("s_imp0", [P, NSB]), t("s_imp", [P, NSB]), t("s_top", [P, 8])
        ot, o64 = t("s_ot", [P, P]), t("s_o64", [P, HD])
        obT = t("s_obT", [P, 4, TSM])

        rows_in, pages, win_in = sem("s_rows_in"), sem("s_pages"), sem("s_win_in")
        pages_pool = sem("s_pages_pool")
        zeroed, prep_mm, prep_out = sem("s_zeroed"), sem("s_prep_mm"), sem("s_prep_out")
        small_mm, small_used, sel_mm, sel_read = sem("s_small_mm"), sem("s_small_used"), sem("s_sel_mm"), sem("s_sel_read")
        cexp_in, cexp_out, pc_ready = sem("s_cexp_in"), sem("s_cexp_out"), sem("s_pc_ready")
        pc_mm, pc_out, imp_mm, imp_out = sem("s_pc_mm"), sem("s_pc_out"), sem("s_imp_mm"), sem("s_imp_out")
        e_in, e_out, turn_mm, turn_out = sem("s_e_in"), sem("s_e_out"), sem("s_turn_mm"), sem("s_turn_out")
        o_mm, o_out, back_mm, back_out = sem("s_o_mm"), sem("s_o_out"), sem("s_back_mm"), sem("s_back_out")
        dchain, stored = sem("s_dchain"), sem("s_stored")
        NEWC, WNEWC, CMPC = 2048, 2048 + 64, 2048 + 128
        WINB, MISC, OB = 2560, 3072, 3584
        turns = [5, 5, 5, 5, 2]

        with nc.Block() as block:
            @block.sync
            def _(sp):
                sp.dma_start(qrow[:], io["q_dram"][TPR:T, :]).then_inc(rows_in, 16)
                sp.dma_start(nrow[:, 0], io["kvs"][TPR:T, :]).then_inc(rows_in, 16)
                sp.dma_start(nrow[:, 1], io["kvw"][TPR:T, :]).then_inc(rows_in, 16)
                sp.dma_start(gate[:], io["gate_dram"][TPR:T, :]).then_inc(rows_in, 16)
                load_pages(sp, table, lambda b, i: kvs[1][:, b, bass.ds(i, 1)].rearrange("p a k t -> p (a k) t"),
                           io["slc_pool"], 1, pages, (0, 1))
                sp.wait_ge(o_mm, 1)
                for b in range(4):
                    sp.dma_start(wkv[:, b], io["win_kv"][4 + b]).then_inc(win_in, 16)
                sp.wait_ge(back_out, 2)
                sp.dma_start(io["ob_dram"][:, :, TPR:T], obT[:]).then_inc(stored, 16)
                sp.wait_ge(stored, 16)

            @block.gpsimd
            def _(pool):
                load_pages(pool, table, lambda b, i: kvs[1][:, b, bass.ds(i, 1)].rearrange("p a k t -> p (a k) t"),
                           io["slc_pool"], 1, pages_pool, (2, 3))

            @block.tensor
            def _(pe):
                M, X = nc.tensor.matmul, nc.tensor.transpose
                id32 = cst["ident"][0:TSM, 0:TSM]
                pe.wait_ge(rows_in, 64)
                for c in range(4):
                    X(PS[:, 32 * c:32 * c + 32], qrow[:, c * P:c * P + P], id32)
                for br in range(2):
                    last = X(PS[:, 128 + 32 * br:160 + 32 * br], nrow[:, br, 0:P], id32)
                last.then_inc(prep_mm, 1)
                pe.wait_ge(prep_out, 1)
                for hf in range(2):
                    if hf:
                        pe.wait_ge(small_used, 1)
                        pe.wait_ge(o_out, 1)
                        pe.wait_ge(back_out, 1)
                    M(PS[:, MISC:MISC + 24], cst["rowtok"][0:TSM, hf * P:hf * P + P], gate[:], start=True, stop=True)
                    kv = kvs[hf]
                    if hf:
                        pe.wait_ge(win_in, 64)
                    for b in range(4):
                        r, q = slice(32 * b, 32 * b + 32), Q[:, 4 * hf + b, :]
                        M(PS[r, CMPC:CMPC + NKC_S], q, kcT_s[:, 4 * hf + b, :], start=True, stop=True)
                        M(PS[r, NEWC:NEWC + 32], q, nT[:, 0, :], start=True, stop=True)
                        M(PS[r, WNEWC:WNEWC + 32], q, nT[:, 1, :], start=True, stop=True)
                        last = M(PS[r, WINB:WINB + 512], q, wkv[:, b, :, 0, :], start=True, stop=True)
                    last.then_inc(small_mm, 1)
                    if hf:
                        pe.wait_ge(pages, 16 * 2 * NPAGES)
                        pe.wait_ge(pages_pool, 16 * 2 * NPAGES)
                    for b in range(4):
                        r, q = slice(32 * b, 32 * b + 32), Q[:, 4 * hf + b, :]
                        for c in range(4):
                            last = M(PS[r, 512 * c:512 * c + 512], q, kv[:, b, 4 * c:4 * c + 4, 0, :],
                                     start=True, stop=True)
                    last.then_inc(sel_mm, 1)
                    pe.wait_ge(pc_ready, hf + 1)
                    X(PS[0:NKC_S, MISC:MISC + P], Ec[:, 0:NKC_S], cst["ident"]).then_inc(pc_mm, 1)
                    pe.wait_ge(pc_out, hf + 1)
                    M(PS[:, MISC + 128:MISC + 128 + NSB], pcT[0:NKC_S, :], cst["overlap"][0:NKC_S, :],
                      start=True, stop=True).then_inc(imp_mm, 1)
                    pe.wait_ge(imp_out, 2 * hf + 1)
                    M(PS[:, MISC + 192:MISC + 192 + NSB], cst["sumheads"], imp0[:], start=True, stop=True).then_inc(imp_mm, 1)
                    pe.wait_ge(e_out, hf + 1)
                    k = 0
                    for rnd, n in enumerate(turns):
                        at = hf * 5 + rnd
                        o = 1024 * (rnd % 2)
                        if rnd >= 2:
                            pe.wait_ge(turn_out, at - 1)
                        for j in range(n):
                            if rnd == 4:
                                src, w = ((Es, PAST), (Ew, 512))[j]
                                last = X(PS[0:TSM, o + j * P:o + j * P + P], src[:, w:w + TSM], cst["ident"])
                            else:
                                src = Es[:, k * P:k * P + P] if k < 16 else Ew[:, (k - 16) * P:(k - 15) * P]
                                last = X(PS[:, o + j * P:o + j * P + P], src, cst["ident"])
                                k += 1
                        last.then_inc(turn_mm, 1)
                    pe.wait_ge(turn_out, 5 * hf + 5)
                    for b in range(4):
                        r = slice(32 * b, 32 * b + 32)
                        o = OB
                        for c in range(16):
                            M(PS[r, o:o + P], pT[:, c, r], kv[:, b, c, 1, :], start=(c == 0), stop=False)
                        M(PS[r, o:o + P], nTp[:, 0, r], nrow[:, 0, P:256], start=False, stop=True)
                        o = OB + P
                        for c in range(4):
                            M(PS[r, o:o + P], pT[:, 16 + c, r], wkv[:, b, c, 1, :], start=(c == 0), stop=False)
                        M(PS[r, o:o + P], nTp[:, 1, r], nrow[:, 1, P:256], start=False, stop=True)
                        o = OB + 2 * P
                        last = M(PS[r, o:o + P], pcT[0:NKC_S, r], vc_s[0:NKC_S, 4 * hf + b, :], start=True, stop=True)
                    last.then_inc(o_mm, 1)
                    pe.wait_ge(o_out, hf + 1)
                    X(PS[0:HD, MISC + 256:MISC + 384], o64[:], cst["ident"]).then_inc(back_mm, 1)

            @block.scalar
            def _(act):
                A = nc.scalar.activation
                for hf in range(2):
                    act.wait_ge(cexp_in, hf + 1)
                    A(Ec[:, 0:NKC_S], Ec[:, 0:NKC_S], ACT.Exp, bias=mx[:, 0:1], scale=0.125,
                      accum_out=sm[:, 0:1]).then_inc(cexp_out, 1)
                    act.wait_ge(e_in, hf + 1)
                    A(Es[:], Es[:], ACT.Exp, bias=mx[:, 1:2], scale=0.125, accum_out=sm[:, 1:2])
                    A(Ew[:], Ew[:], ACT.Exp, bias=mx[:, 2:3], scale=0.125, accum_out=sm[:, 2:3]).then_inc(e_out, 1)

            @block.vector
            def _(dve):
                link = Chain(dve, dchain)
                V = nc.vector
                link(V.memset(Q[:], 0.0))
                dve.wait_ge(prep_mm, 1)
                for hh in range(8):
                    g, par = hh // 4, hh % 2
                    src = PS[64 * par:64 * par + 64, 32 * (hh // 2):32 * (hh // 2) + 32]
                    link(V.tensor_copy(Q[64 * g:64 * g + 64, :, g * 16 + hh % 4 * 4:g * 16 + hh % 4 * 4 + 4],
                                       src.rearrange("p (b t) -> p b t", t=TS)))
                link(V.tensor_copy(nT[:], PS[:, 128:192].rearrange("p (k t) -> p k t", k=2)))
                dve.sem_inc(prep_out, 1)
                for hf in range(2):
                    new = cst["new_s"][:, hf * TSM:hf * TSM + TSM]
                    dve.wait_ge(small_mm, hf + 1)
                    link(V.tensor_tensor(gr[:], PS[:, MISC:MISC + 24], cst["rowhead"], ALU.mult))
                    link(V.reduce_sum(g3[:], gr[:].rearrange("p (b h) -> p b h", b=3), AX_X))
                    link(V.tensor_copy(Ec[:, 0:NKC_S], PS[:, CMPC:CMPC + NKC_S]))
                    link(V.reduce_max(mx[:, 0:1], Ec[:, 0:NKC_S], AX_X))
                    link(V.tensor_scalar(mx[:, 0:1], mx[:, 0:1], -0.125, None, ALU.mult))
                    dve.sem_inc(cexp_in, 1)
                    link(V.tensor_tensor(Ew[:, 0:TS], PS[:, WINB:WINB + TS], cst["win_old"], ALU.add))
                    link(V.tensor_copy(Ew[:, TS:512], PS[:, WINB + TS:WINB + 512]))
                    link(V.tensor_tensor(Ew[:, 512:512 + TSM], PS[:, WNEWC:WNEWC + TSM], new, ALU.add))
                    link(V.reduce_max(mx[:, 2:3], Ew[:], AX_X))
                    dve.wait_ge(cexp_out, hf + 1)
                    link(V.reciprocal(sm[:, 0:1], sm[:, 0:1]))
                    link(V.tensor_scalar(Ec[:, 0:NKC_S], Ec[:, 0:NKC_S], sm[:, 0:1], None, ALU.mult))
                    dve.sem_inc(pc_ready, 1)
                    dve.wait_ge(pc_mm, hf + 1)
                    link(V.tensor_copy(pcT[0:NKC_S, :], PS[0:NKC_S, MISC:MISC + P]))
                    dve.sem_inc(pc_out, 1)
                    dve.wait_ge(imp_mm, 2 * hf + 1)
                    link(V.tensor_copy(imp0[:], PS[:, MISC + 128:MISC + 128 + NSB]))
                    dve.sem_inc(imp_out, 1)
                    dve.wait_ge(imp_mm, 2 * hf + 2)
                    link(V.tensor_copy(imp[:], PS[:, MISC + 192:MISC + 192 + NSB]))
                    dve.sem_inc(imp_out, 1)
                    link(V.memset(imp[:, 0:1], 1e6))
                    link(V.memset(imp[:, NSB - 2:NSB], 1e6))
                    for _ in range(2):
                        link(V.max(top[:], imp[:]))
                        link(V.match_replace(imp[:], top[:], imp[:], -1.0))
                    link(V.tensor_scalar(imp[:], imp[:], -1.0, NEG, ALU.not_equal, ALU.mult))
                    dve.wait_ge(sel_mm, hf + 1)
                    link(V.tensor_tensor(Es[:, 0:PAST].rearrange("p (j t) -> p j t", t=HD),
                                         PS[:, 0:PAST].rearrange("p (j t) -> p j t", t=HD),
                                         imp[:, 0:NSB - 1].unsqueeze(2).to_broadcast([P, NSB - 1, HD]), ALU.add))
                    link(V.tensor_tensor(Es[:, PAST:PAST + TSM], PS[:, NEWC:NEWC + TSM], new, ALU.add))
                    dve.sem_inc(small_used, 1)
                    link(V.reduce_max(mx[:, 1:2], Es[:], AX_X))
                    link(V.tensor_scalar(mx[:, 1:3], mx[:, 1:3], -0.125, None, ALU.mult))
                    dve.sem_inc(e_in, 1)
                    k = 0
                    for rnd, n in enumerate(turns):
                        dve.wait_ge(turn_mm, hf * 5 + rnd + 1)
                        o = 1024 * (rnd % 2)
                        if rnd == 4:
                            link(V.tensor_copy(nTp[:], PS[0:TSM, o:o + 2 * P].rearrange("p (k r) -> p k r", k=2)))
                        else:
                            link(V.tensor_copy(pT[:, k:k + n, :], PS[:, o:o + n * P].rearrange("p (k r) -> p k r", k=n)))
                            k += n
                        dve.sem_inc(turn_out, 1)
                    link(V.reciprocal(sm[:, 1:3], sm[:, 1:3]))
                    link(V.tensor_tensor(g3[:, 1:3], g3[:, 1:3], sm[:, 1:3], ALU.mult))
                    dve.wait_ge(o_mm, hf + 1)
                    link(V.tensor_scalar(ot[:], PS[:, OB + 2 * P:OB + 3 * P], g3[:, 0:1], None, ALU.mult))
                    for j in range(2):
                        link(V.scalar_tensor_tensor(out=ot[:], in0=PS[:, OB + j * P:OB + j * P + P],
                                                    scalar=g3[:, 1 + j:2 + j], in1=ot[:], op0=ALU.mult, op1=ALU.add))
                    link(V.tensor_scalar(o64[:], ot[:, 0:HD], cst["grp"][:, 0:1], None, ALU.mult))
                    link(V.scalar_tensor_tensor(out=o64[:], in0=ot[:, HD:P], scalar=cst["grp"][:, 1:2], in1=o64[:],
                                                op0=ALU.mult, op1=ALU.add))
                    dve.sem_inc(o_out, 1)
                    dve.wait_ge(back_mm, hf + 1)
                    src = PS[0:HD, MISC + 256:MISC + 384].rearrange("p (b c a t) -> p a c b t", b=4, c=4, a=2)
                    for par in range(2):
                        for c in range(4):
                            dst = obT[64 * par:64 * par + 64, c, 16 * hf:16 * hf + 16].rearrange("p (b t) -> p b t", t=TS)
                            link(V.tensor_copy(dst, src[:, par, c]))
                    dve.sem_inc(back_out, 1)


def merge_and_route(nc, io, PS, sem, cst, wk, raw):
    with ExitStack() as ctx:
        def t(name, shape, dt=F32, c=ctx):
            return c.enter_context(nc.sbuf_tensor(name, shape, dt))

        x1 = t("m_x1", [P, 5, D])
        hT = t("m_hT", [P, KC, T])
        oT = t("m_oT", [P, 2, 4, T])
        wg = t("m_wg", [P, 2, 2, KC, P])
        wb = t("m_wb", [P, 2, 2, 4, P])
        mT = t("m_mT", [P, KC, T])
        sg = t("m_sg", [P, 2, 2, TH])
        wo = t("m_wo", [P, 2, KC, D // 2])
        ss = t("m_ss", [P, 5])
        n2 = t("m_n2", [P, D])
        h2 = oT[:].rearrange("p a b n -> p (a b n)")[:, 0:4 * D].rearrange("p (i n) -> p i n", i=4)
        wr = t("m_wr", [P, KC, 36])
        br = t("m_br", [P, 36])
        lg = t("m_lg", [P, 5, 36])
        h2T = hT
        gl, g8, gi = t("m_gl", [P, 5, 8]), t("m_g8", [P, 5, 8]), t("m_gi", [P, 5, 8], U32)
        gf, em = t("m_gf", [P, 5, 1]), t("m_em", [P, 5, NE])
        e8, ei, ef = t("m_e8", [P, 5, 8]), t("m_ei", [P, 5, 8], U32), t("m_ef", [P, 5, 2])
        ge, gs, dd = t("m_ge", [P, 5, 4]), t("m_gs", [P, 5]), t("m_dd", [P, 5, 1])
        oh, ohs = t("m_oh", [P, 2, 5, NE]), t("m_ohs", [P, 5, NE])
        rk, kk, ad, tm = t("m_rk", [P, 5, NE]), t("m_kk", [P, 5, NE]), t("m_ad", [P, 5, NE]), t("m_tm", [P, 5, NE])
        cnt, nov, inc, exc = t("m_cnt", [P, NE]), t("m_nov", [P, NE]), t("m_inc", [P, NE]), t("m_exc", [P, NE])
        addr, addri = t("m_addr", [P, 5, 2]), t("m_addri", [P, 5, 2], I32)
        ov, ovs, ids = t("m_ov", [P, NOV, NE]), t("m_ovs", [P, NOV]), t("m_ids", [P, NBLK + 1], I32)
        slotv = t("m_slotv", [P, 10], I32)
        big = t("m_big", [CAP, NBLK], I32)

        h_in, o_in, small_in = sem("m_h_in"), sem("m_o_in"), sem("m_small_in")
        wg_in, wo_in = [sem("m_wg_in0"), sem("m_wg_in1")], sem("m_wo_in")
        gates_mm, sig_out, merged = sem("m_gates_mm"), sem("m_sig_out"), sem("m_merged")
        out_mm, x1_ready = sem("m_out_mm"), sem("m_x1_ready")
        sq_out, root_in, root_out = sem("m_sq_out"), sem("m_root_in"), sem("m_root_out")
        h2_ready, h2T_mm, h2T_out, h2_stored = sem("m_h2_ready"), sem("m_h2T_mm"), sem("m_h2T_out"), sem("m_h2_stored")
        lg_mm, lg_out = sem("m_lg_mm"), sem("m_lg_out")
        exp_in, exp_out = sem("m_exp_in"), sem("m_exp_out")
        oh_ready, rank_mm, addr_ready, big_ready = sem("m_oh_ready"), sem("m_rank_mm"), sem("m_addr_ready"), sem("m_big_ready")
        raw_in, first_stored = sem("m_raw_in"), sem("m_first_stored")
        filled, scattered, ids_out, dchain = sem("m_filled"), sem("m_scattered"), sem("m_ids_out"), sem("m_dchain")
        rows = [min(P, T - i * P) for i in range(5)]

        def gate_ps(k, n):
            return PS[:, 2048 * n + 512 * k:2048 * n + 512 * k + TH]

        with nc.Block() as block:
            @block.sync
            def _(sp):
                sp.dma_start(hT[:], io["h_dram"]).then_inc(h_in, 16)
                for j in range(KC):
                    if j >= 2:
                        sp.wait_ge(gates_mm, 2 * j - 2)
                    for k in range(2):
                        sp.dma_start(wg[:, j % 2, k], io["w_gates"][k, j]).then_inc(wg_in[j % 2], 16)
                        sp.dma_start(wb[:, j % 2, k], io["w_branch"][k, j]).then_inc(wg_in[j % 2], 16)
                    if j == 0:
                        sp.dma_start(oT[:, 0], io["oa_dram"]).then_inc(o_in, 16)
                        sp.dma_start(oT[:, 1], io["ob_dram"]).then_inc(o_in, 16)
                for hf in range(2):
                    sp.dma_start(wo[:, hf], io["w_out"][hf]).then_inc(wo_in, 16)
                for k in range(6):
                    sp.dma_start(raw[k][:], expert_half(io, k, 0)).then_inc(raw_in, 16)
                for i in range(5):
                    sp.wait_ge(h2_ready, i + 1)
                    sp.dma_start(io["h2_dram"][i * P:i * P + rows[i], :], h2[0:rows[i], i % 4]
                                 ).then_inc(h2_stored if i else first_stored, 16)
                for i in range(5):
                    sp.dma_start(io["x1_dram"][0:rows[i], i, :], x1[0:rows[i], i, :]).then_inc(h2_stored, 16)
                sp.wait_ge(ids_out, 1)
                sp.dma_start(io["ids_dram"], ids[0:1, :]).then_inc(h2_stored, 16)
                sp.wait_ge(first_stored, 16)
                sp.wait_ge(h2_stored, 16 * 10)
                sp.wait_ge(raw_in, 16 * 6)

            @block.gpsimd
            def _(pool):
                pool.dma_start(n2[:], io["norm2_rows"]).then_inc(small_in, 16)
                pool.dma_start(wr[:], io["w_route"]).then_inc(small_in, 16)
                pool.dma_start(br[:], io["b_route"]).then_inc(small_in, 16)
                for i in range(5):
                    pool.dma_start(x1[0:rows[i], i, :], io["x"][i * P:i * P + rows[i], :]).then_inc(small_in, 16)
                nc.gpsimd.memset(big[:], 1 << 20).then_inc(big_ready, 1)
                pool.wait_ge(big_ready, 1)
                pool.dma_start(io["slots_dram"].rearrange("(p n) a -> p (n a)", n=NBLK), big[:]).then_inc(filled, 16)
                pool.wait_ge(filled, 16)
                pool.wait_ge(addr_ready, 1)
                for i in range(5):
                    for k in range(2):
                        pool.indirect_dma_start(io["slots_dram"],
                                                bass.IndirectOffsetOnAxis(ap=addri[0:rows[i], i, k:k + 1], axis=0),
                                                slotv[0:rows[i], 2 * i + k:2 * i + k + 1], None).then_inc(scattered, 16)
                pool.wait_ge(scattered, 160)

            @block.tensor
            def _(pe):
                M = nc.tensor.matmul
                pe.wait_ge(h_in, 16)
                for j in range(KC):
                    pe.wait_ge(wg_in[j % 2], 64 * (j // 2 + 1))
                    for n in range(2):
                        if j:
                            pe.wait_ge(merged, 2 * j + n - 1)
                        ns = slice(n * TH, n * TH + TH)
                        for k in range(2):
                            for c in range(KC):
                                M(gate_ps(k, n), wg[:, j % 2, k, c, :], hT[:, c, ns], start=(c == 0), stop=(c == KC - 1))
                            if j == 0:
                                pe.wait_ge(o_in, 32)
                            for c in range(4):
                                last = M(gate_ps(2 + k, n), wb[:, j % 2, k, c, :], oT[:, k, c, ns],
                                         start=(c == 0), stop=(c == 3))
                        last.then_inc(gates_mm, 1)
                pe.wait_ge(merged, 2 * KC)
                pe.wait_ge(wo_in, 32)
                pe.wait_ge(small_in, 16 * 8)

                def project(i):
                    for hf in range(2):
                        n = 2 * i + hf
                        if n >= 4:
                            pe.wait_ge(x1_ready, n - 3)
                        for c in range(KC):
                            last = M(PS[0:rows[i], 512 * (n % 4):512 * (n % 4) + 512], mT[:, c, i * P:i * P + rows[i]],
                                     wo[:, hf, c, :], start=(c == 0), stop=(c == KC - 1))
                        last.then_inc(out_mm, 1)

                def turn(i):
                    pe.wait_ge(h2_ready, i + 1)
                    if i:
                        pe.wait_ge(h2T_out, i)
                    for c in range(KC):
                        last = nc.tensor.transpose(PS[:, 2048 + c * P:2048 + c * P + rows[i]],
                                                   h2[0:rows[i], i % 4, c * P:c * P + P], cst["ident"][0:rows[i], 0:rows[i]])
                    last.then_inc(h2T_mm, 1)

                def logits(i):
                    pe.wait_ge(h2T_out, i + 1)
                    for c in range(KC):
                        last = M(PS[0:rows[i], 3072 + 64 * i:3072 + 64 * i + 36], h2T[:, c, i * P:i * P + rows[i]],
                                 wr[:, c, :], start=(c == 0), stop=(c == KC - 1))
                    last.then_inc(lg_mm, 1)

                for i in range(7):
                    if i < 5:
                        project(i)
                    if 1 <= i <= 5:
                        turn(i - 1)
                    if i >= 2:
                        logits(i - 2)
                pe.wait_ge(oh_ready, 1)
                for i in range(5):
                    for i2 in range(i + 1):
                        M(PS[0:rows[i], 3584 + 32 * i:3616 + 32 * i],
                          cst["ones"][0:rows[i2], 0:rows[i]] if i2 < i else cst["before"][0:rows[i2], 0:rows[i]],
                          ohs[0:rows[i2], i2, :], start=(i2 == 0), stop=(i2 == i))
                for i in range(5):
                    last = M(PS[:, 3584 + 192:3584 + 224], cst["ones"][0:rows[i], :], ohs[0:rows[i], i, :],
                             start=(i == 0), stop=(i == 4))
                last.then_inc(rank_mm, 1)

            @block.scalar
            def _(act):
                A = nc.scalar.activation
                for u in range(2 * KC):
                    n = u % 2
                    act.wait_ge(gates_mm, u + 1)
                    if u >= 2:
                        act.wait_ge(merged, u - 1)
                    A(sg[:, n], PS[:, 2048 * n:2048 * n + 1024].rearrange("p (k t) -> p k t", k=2)[:, :, 0:TH],
                      ACT.Sigmoid).then_inc(sig_out, 1)
                for i in range(6):
                    if i < 5:
                        r = rows[i]
                        act.wait_ge(x1_ready, 2 * i + 2)
                        if i == 4:
                            act.wait_ge(first_stored, 16)
                            act.wait_ge(h2T_mm, 1)
                        A(h2[0:r, i % 4], x1[0:r, i, :], ACT.Square, accum_out=ss[0:r, i:i + 1]).then_inc(sq_out, 1)
                        act.wait_ge(root_in, i + 1)
                        A(ss[:, i:i + 1], ss[:, i:i + 1], ACT.Sqrt).then_inc(root_out, 1)
                    if i:
                        j = i - 1
                        act.wait_ge(h2T_mm, j + 1)
                        A(h2T[:, :, j * P:j * P + rows[j]],
                          PS[:, 2048:3072].rearrange("p (c t) -> p c t", c=KC)[:, :, 0:rows[j]], ACT.Copy).then_inc(h2T_out, 1)
                act.wait_ge(exp_in, 1)
                A(ge[:], ge[:], ACT.Exp)
                A(dd[:], dd[:], ACT.Exp).then_inc(exp_out, 1)

            @block.vector
            def _(dve):
                link = Chain(dve, dchain)
                V = nc.vector
                link(V.memset(ss[:], 1.0))
                link(V.memset(gl[:], NEG))
                link(V.memset(lg[:], 0.0))
                for u in range(2 * KC):
                    j, n = u // 2, u % 2
                    dve.wait_ge(sig_out, u + 1)
                    ps = PS[:, 2048 * n + 1024:2048 * n + 2048].rearrange("p (k t) -> p k t", k=2)[:, :, 0:TH]
                    link(V.tensor_tensor(sg[:, n], sg[:, n], ps, ALU.mult))
                    V.tensor_tensor(mT[:, j, n * TH:n * TH + TH], sg[:, n, 0], sg[:, n, 1], ALU.add).then_inc(merged, 1)
                dve.wait_ge(small_in, 16 * 8)
                for i in range(5):
                    for hf in range(2):
                        n = 2 * i + hf
                        dve.wait_ge(out_mm, n + 1)
                        xs = x1[0:rows[i], i, 512 * hf:512 * hf + 512]
                        V.tensor_tensor(xs, xs, PS[0:rows[i], 512 * (n % 4):512 * (n % 4) + 512], ALU.add).then_inc(x1_ready, 1)
                    dve.wait_ge(sq_out, i + 1)
                    link(V.tensor_scalar(ss[:, i:i + 1], ss[:, i:i + 1], 1.0 / D, RMS_EPS, ALU.mult, ALU.add))
                    dve.sem_inc(root_in, 1)
                    dve.wait_ge(root_out, i + 1)
                    link(V.reciprocal(ss[:, i:i + 1], ss[:, i:i + 1]))
                    V.scalar_tensor_tensor(out=h2[0:rows[i], i % 4], in0=x1[0:rows[i], i, :], scalar=ss[0:rows[i], i:i + 1],
                                           in1=n2[0:rows[i], :], op0=ALU.mult, op1=ALU.mult).then_inc(h2_ready, 1)
                dve.wait_ge(lg_mm, 5)
                for i in range(5):
                    link(V.tensor_tensor(lg[0:rows[i], i, :], PS[0:rows[i], 3072 + 64 * i:3072 + 64 * i + 36],
                                         br[0:rows[i], :], ALU.add))
                link(V.tensor_copy(gl[:, :, 0:4], lg[:, :, 0:4]))
                for i in range(5):
                    link(V.max(g8[:, i, :], gl[:, i, :]))
                    link(V.max_index(gi[:, i, :], g8[:, i, :], gl[:, i, :]))
                link(V.tensor_copy(gf[:], gi[:, :, 0:1]))
                link(V.tensor_tensor(ge[:], gl[:, :, 0:4], g8[:, :, 0:1].to_broadcast([P, 5, 4]), ALU.subtract))
                eg = cst["egroup"].unsqueeze(1).to_broadcast([P, 5, NE])
                link(V.tensor_tensor(em[:], eg, gf[:].to_broadcast([P, 5, NE]), ALU.not_equal))
                link(V.scalar_tensor_tensor(out=em[:], in0=em[:], scalar=NEG, in1=lg[:, :, 4:36], op0=ALU.mult, op1=ALU.add))
                for i in range(5):
                    link(V.max(e8[:, i, :], em[:, i, :]))
                    link(V.max_index(ei[:, i, :], e8[:, i, :], em[:, i, :]))
                link(V.tensor_copy(ef[:], ei[:, :, 0:2]))
                link(V.tensor_tensor(dd[:], e8[:, :, 1:2], e8[:, :, 0:1], ALU.subtract))
                dve.sem_inc(exp_in, 1)
                ie = cst["iota_e"].unsqueeze(1).to_broadcast([P, 5, NE])
                for k in range(2):
                    link(V.tensor_tensor(oh[:, k], ie, ef[:, :, k:k + 1].to_broadcast([P, 5, NE]), ALU.is_equal))
                link(V.tensor_tensor(ohs[:], oh[:, 0], oh[:, 1], ALU.add))
                dve.sem_inc(oh_ready, 1)
                dve.wait_ge(exp_out, 1)
                link(V.reduce_sum(gs[:], ge[:], AX_X))
                link(V.reciprocal(gs[:], gs[:]))
                link(V.tensor_scalar(wk[:, :, 0:1], dd[:], 1.0, None, ALU.add))
                link(V.reciprocal(wk[:, :, 0:1], wk[:, :, 0:1]))
                link(V.tensor_tensor(wk[:, :, 0:1], wk[:, :, 0:1], gs[:].unsqueeze(2), ALU.mult))
                link(V.tensor_tensor(wk[:, :, 1:2], wk[:, :, 0:1], dd[:], ALU.mult))
                dve.wait_ge(rank_mm, 1)
                link(V.memset(rk[:], 0.0))
                for i in range(5):
                    link(V.tensor_copy(rk[0:rows[i], i, :], PS[0:rows[i], 3584 + 32 * i:3616 + 32 * i]))
                link(V.tensor_copy(cnt[:], PS[:, 3584 + 192:3584 + 224]))
                steps = -(-T // CAP) - 1
                link(V.tensor_scalar(nov[:], cnt[:], float(CAP), None, ALU.is_gt))
                link(V.tensor_scalar(kk[:], rk[:], float(CAP), None, ALU.is_ge))
                for j in range(2, steps + 1):
                    link(V.scalar_tensor_tensor(out=nov[:], in0=cnt[:], scalar=float(CAP * j), in1=nov[:],
                                                op0=ALU.is_gt, op1=ALU.add))
                    link(V.scalar_tensor_tensor(out=kk[:], in0=rk[:], scalar=float(CAP * j), in1=kk[:],
                                                op0=ALU.is_ge, op1=ALU.add))
                link(V.tensor_tensor_scan(inc[:], cst["ones"][:, 0:NE], nov[:], 0.0, ALU.mult, ALU.add))
                link(V.tensor_tensor(exc[:], inc[:], nov[:], ALU.subtract))
                link(V.scalar_tensor_tensor(out=rk[:], in0=kk[:], scalar=-float(CAP), in1=rk[:], op0=ALU.mult, op1=ALU.add))
                link(V.scalar_tensor_tensor(out=tm[:], in0=kk[:], scalar=float(NE - 1),
                                            in1=exc[:].unsqueeze(1).to_broadcast([P, 5, NE]), op0=ALU.add, op1=ALU.add))
                link(V.tensor_tensor(tm[:], tm[:], ie, ALU.subtract))
                link(V.scalar_tensor_tensor(out=tm[:], in0=kk[:], scalar=0.5, in1=tm[:], op0=ALU.is_gt, op1=ALU.mult))
                link(V.tensor_tensor(tm[:], tm[:], ie, ALU.add))
                link(V.scalar_tensor_tensor(out=ad[:], in0=rk[:], scalar=float(NBLK), in1=tm[:], op0=ALU.mult, op1=ALU.add))
                for k in range(2):
                    link(V.tensor_tensor(tm[:], oh[:, k], ad[:], ALU.mult))
                    link(V.reduce_sum(addr[:, :, k:k + 1].rearrange("p a b -> p (a b)"), tm[:], AX_X))
                link(V.tensor_copy(addri[:], addr[:]))
                link(V.tensor_copy(slotv[:], cst["slotval"]))
                dve.sem_inc(addr_ready, 1)
                link(V.tensor_tensor(ov[:], inc[:].unsqueeze(1).to_broadcast([P, NOV, NE]),
                                     cst["iota_o"].unsqueeze(2).to_broadcast([P, NOV, NE]), ALU.is_le))
                link(V.reduce_sum(ovs[:], ov[:], AX_X))
                link(V.tensor_scalar(ovs[:], ovs[:], float(NE - 1), None, ALU.min))
                link(V.tensor_copy(ids[:, NE:NBLK], ovs[:]))
                link(V.tensor_copy(ids[:, 0:NE], cst["iota_e"]))
                link(V.tensor_copy(ids[:, NBLK:NBLK + 1], inc[:, NE - 1:NE]))
                dve.sem_inc(ids_out, 1)


def expert_half(io, k, e):
    src = io[("w_exp_gate", "w_exp_up", "w_exp_down")[k // 2]]
    src = src[bass.ds(e, 1)].rearrange("a (p c) n -> p (a c n)", p=P)
    return src[:, (k % 2) * HW:(k % 2) * HW + HW]


def experts(nc, io, PS, sem, cst, raw):
    with ExitStack() as ctx:
        def t(name, shape, dt=F32):
            return ctx.enter_context(nc.sbuf_tensor(name, shape, dt))

        DE = D // 2
        FC = DE // P
        hi = [t(f"e_hi{m}", [P, 2 * HW], F32R) for m in range(3)]
        lo = [t(f"e_lo{m}", [P, 2 * HW], F32R) for m in range(3)]
        xe = t("e_xe", [CAP, 2, D])
        xs = t("e_xs", [P, 2, KC, 2 * CAP], F32R)
        hs = t("e_hs", [P, FC, 2 * CAP], F32R)
        g_lo, u_lo, y_lo = t("e_g_lo", [CAP, DE]), t("e_u_lo", [CAP, DE]), t("e_y_lo", [CAP, D])
        g, u = t("e_g", [CAP, DE]), t("e_u", [CAP, DE])
        ye = t("e_ye", [CAP, 2, D])
        slots, toks = t("e_slots", [CAP, NBLK], I32), t("e_toks", [CAP, NBLK], I32)
        ids = t("e_ids", [1, NBLK + 1], I32)
        gi, si = t("e_gi", [CAP, 2], I32), t("e_si", [CAP, 2], I32)

        tables_in, toks_ready, zeroed = sem("e_tables_in"), sem("e_toks_ready"), sem("e_zeroed")
        w_in = [sem(f"e_w_in{k}") for k in range(6)]
        hi_done, lo_done = sem("e_hi_done"), sem("e_lo_done")
        idx_ready, paced, pe_paced = sem("e_idx_ready"), sem("e_paced"), sem("e_pe_paced")
        x_in, y_stored = [sem("e_x_in0"), sem("e_x_in1")], [sem("e_y_st0"), sem("e_y_st1")]
        x_mm, xh_done, xl_done = sem("e_x_mm"), sem("e_xh_done"), sem("e_xl_done")
        gate_mm, up_mm, y_mm = sem("e_gate_mm"), sem("e_up_mm"), sem("e_y_mm")
        g_lo_out, g_out, u_lo_out, u_out = sem("e_g_lo_out"), sem("e_g_out"), sem("e_u_lo_out"), sem("e_u_out")
        silu_out, h_out, h_mm, hh_done, hl_done = (sem("e_silu"), sem("e_h_out"), sem("e_h_mm"), sem("e_hh_done"),
                                                   sem("e_hl_done"))
        y_lo_out, y_out = sem("e_y_lo_out"), sem("e_y_out")

        psX = PS[:, 0:512].rearrange("p (c t) -> p c t", c=KC)
        psG, psU = PS[:, 512:1024], PS[:, 1024:1536]
        psH = PS[:, 1536:1536 + FC * CAP].rearrange("p (c t) -> p c t", c=FC)
        psY = PS[:, 2048:3072]
        top, low = slice(0, CAP), slice(CAP, 2 * CAP)

        def each_overflow(eng, body):
            over = eng.value_load(ids[0:1, NBLK:NBLK + 1], min_val=0, max_val=NOV)
            with eng.Fori(0, NOV) as j:
                with eng.If(j < over):
                    body(j)

        with nc.Block() as block:
            @block.sync
            def _(sp):
                sp.dma_start(ids[:], io["ids_dram"]).then_inc(tables_in, 16)
                sp.dma_start(slots[:], io["slots_dram"].rearrange("(p n) a -> p (n a)", n=NBLK)).then_inc(tables_in, 16)

                def load(e, n):
                    for k in range(6):
                        sp.wait_ge(lo_done, 6 * n + (k - 5))
                        sp.dma_start(raw[k][:], expert_half(io, k, e)).then_inc(w_in[k], 16)

                for k in range(6):
                    sp.sem_inc(w_in[k], 16)
                with sp.Fori(1, NE) as n:
                    load(n, n)
                sp.wait_ge(tables_in, 32)
                each_overflow(sp, lambda j: load(sp.value_load(ids[0:1, bass.ds(j + NE, 1)], min_val=0, max_val=NE - 1),
                                                 j + NE))

            @block.gpsimd
            def _(pool):
                nc.gpsimd.memset(xe[:], 0.0).then_inc(zeroed, 1)
                pool.wait_ge(tables_in, 32)
                pool.wait_ge(toks_ready, 1)
                pool.wait_ge(zeroed, 1)

                def wait(on, value):
                    pool.wait_ge(on, value)
                    pool.sem_inc(paced, 1)

                def gather(n, b, count):
                    nc.gpsimd.tensor_copy(gi[:, b:b + 1], toks[:, bass.ds(n, 1)]).then_inc(idx_ready, 1)
                    wait(idx_ready, count)
                    pool.indirect_dma_start(xe[:, b, :], None, io["h2_dram"],
                                            bass.IndirectOffsetOnAxis(ap=gi[:, b:b + 1], axis=0),
                                            bounds_check=T - 1, oob_is_err=False).then_inc(x_in[b], 16)

                def scatter(n, b, count):
                    nc.gpsimd.tensor_copy(si[:, b:b + 1], slots[:, bass.ds(n, 1)]).then_inc(idx_ready, 1)
                    wait(idx_ready, count)
                    pool.indirect_dma_start(io["y2_dram"], bass.IndirectOffsetOnAxis(ap=si[:, b:b + 1], axis=0),
                                            ye[:, b, :], None,
                                            bounds_check=2 * T - 1, oob_is_err=False).then_inc(y_stored[b], 16)

                gather(0, 0, 1)
                gather(1, 1, 2)
                with pool.Fori(0, (NE - 2) // 2) as i:
                    for b in range(2):
                        wait(x_mm, 2 * i + (b + 1))
                        gather(2 * i + (b + 2), b, 4 * i + (2 * b + 3))
                        wait(y_out, 2 * i + (b + 1))
                        scatter(2 * i + b, b, 4 * i + (2 * b + 4))
                for b in range(2):
                    pool.wait_ge(y_out, NE - 2 + b + 1)
                    scatter(NE - 2 + b, b, 2 * NE - 1 + b)
                for b in range(2):
                    pool.wait_ge(y_stored[b], 8 * NE)

                def overflow(j):
                    gather(j + NE, 0, 2 * j + (2 * NE + 1))
                    wait(y_out, j + (NE + 1))
                    scatter(j + NE, 0, 2 * j + (2 * NE + 2))
                    wait(y_stored[0], 16 * j + (8 * NE + 16))

                each_overflow(pool, overflow)

            @block.tensor
            def _(pe):
                M, X = nc.tensor.matmul, nc.tensor.transpose

                def rows_in(n, b, arrivals, first=False):
                    pe.wait_ge(x_in[b], arrivals)
                    if not first:
                        pe.wait_ge(xl_done, n)
                    pe.sem_inc(pe_paced, 1)
                    for c in range(KC):
                        last = X(psX[:, c, :], xe[:, b, c:D:KC], cst["ident"][0:CAP, 0:CAP])
                    last.then_inc(x_mm, 1)

                def product(ps, rows, m, chunks, width, off=0):
                    for c in range(chunks):
                        for w in (hi[m], lo[m]):
                            last = M(ps, rows[:, c, :], w[:, c * width + off:c * width + off + 512],
                                     start=(c == 0 and w is hi[m]), stop=(c == chunks - 1 and w is lo[m]))
                    return last

                def gate(n, b, first=False):
                    pe.wait_ge(xl_done, n + 1)
                    pe.wait_ge(lo_done, 6 * n + 2)
                    if not first:
                        pe.wait_ge(g_out, n)
                    product(psG, xs[:, b], 0, KC, DE).then_inc(gate_mm, 1)

                def up(n, b, first=False):
                    pe.wait_ge(lo_done, 6 * n + 4)
                    if not first:
                        pe.wait_ge(u_out, n)
                    product(psU, xs[:, b], 1, KC, DE).then_inc(up_mm, 1)

                def hidden(n, first=False):
                    pe.wait_ge(h_out, n + 1)
                    if not first:
                        pe.wait_ge(hl_done, n)
                    pe.sem_inc(pe_paced, 1)
                    for c in range(FC):
                        last = X(psH[:, c, :], g[:, c:DE:FC], cst["ident"][0:CAP, 0:CAP])
                    last.then_inc(h_mm, 1)

                def down(n, first=False):
                    pe.wait_ge(hl_done, n + 1)
                    pe.wait_ge(lo_done, 6 * n + 6)
                    if not first:
                        pe.wait_ge(y_out, n)
                    for hf in range(2):
                        last = product(psY[:, 512 * hf:512 * hf + 512], hs, 2, FC, D, 512 * hf)
                    last.then_inc(y_mm, 1)

                rows_in(0, 0, 16, True)
                gate(0, 0, True)
                rows_in(1, 1, 16)
                up(0, 0, True)
                hidden(0, True)
                down(0, True)
                gate(1, 1)
                rows_in(2, 0, 32)
                up(1, 1)
                with pe.Fori(1, NE // 2 - 1) as i:
                    for b in range(2):
                        hidden(2 * i + (b - 1))
                        down(2 * i + (b - 1))
                        gate(2 * i + b, b)
                        rows_in(2 * i + (b + 1), 1 - b, 16 * i + 16 * (b + 1))
                        up(2 * i + b, b)
                n = NE - 2
                hidden(n - 1)
                down(n - 1)
                gate(n, 0)
                rows_in(n + 1, 1, 8 * NE)
                up(n, 0)
                hidden(n)
                down(n)
                gate(n + 1, 1)
                up(n + 1, 1)
                hidden(n + 1)
                down(n + 1)

                def overflow(j):
                    rows_in(j + NE, 0, 16 * j + (8 * NE + 16))
                    gate(j + NE, 0)
                    up(j + NE, 0)
                    hidden(j + NE)
                    down(j + NE)

                pe.wait_ge(tables_in, 32)
                each_overflow(pe, overflow)

            freed = (gate_mm, up_mm, y_mm)

            @block.scalar
            def _(act):
                A = nc.scalar.activation

                def split(n, k, first=False):
                    act.wait_ge(w_in[k], 16 * n + 16)
                    if not first:
                        act.wait_ge(freed[k // 2], n)
                    o = (k % 2) * HW
                    A(hi[k // 2][:, o:o + HW], raw[k][:], ACT.Copy).then_inc(hi_done, 1)

                def rows_hi(n, b, first=False):
                    act.wait_ge(x_mm, n + 1)
                    if not first:
                        act.wait_ge(up_mm, n + (-1))
                    A(xs[:, b, :, top], psX, ACT.Copy).then_inc(xh_done, 1)

                def halves_out(n, first=False):
                    act.wait_ge(gate_mm, n + 1)
                    if not first:
                        act.wait_ge(g_out, n)
                    A(g_lo[:], psG[low], ACT.Copy).then_inc(g_lo_out, 1)
                    act.wait_ge(up_mm, n + 1)
                    if not first:
                        act.wait_ge(u_out, n)
                    A(u_lo[:], psU[low], ACT.Copy).then_inc(u_lo_out, 1)
                    act.wait_ge(g_out, n + 1)
                    A(g[:], g[:], ACT.Silu).then_inc(silu_out, 1)

                def hidden_hi(n, first=False):
                    act.wait_ge(h_mm, n + 1)
                    if not first:
                        act.wait_ge(y_mm, n)
                    A(hs[:, :, top], psH, ACT.Copy).then_inc(hh_done, 1)

                def y_low(n, first=False):
                    act.wait_ge(y_mm, n + 1)
                    if not first:
                        act.wait_ge(y_out, n)
                    A(y_lo[:], psY[low], ACT.Copy).then_inc(y_lo_out, 1)

                def block_of(n, b, first=False, second=False, last=False):
                    split(n, 0, first)
                    if not first:
                        hidden_hi(n + (-1), second)
                    split(n, 1, first)
                    split(n, 2, first)
                    split(n, 3, first)
                    if not first:
                        y_low(n + (-1), second)
                    split(n, 4, first)
                    if not last:
                        rows_hi(n + 1, 1 - b, first)
                    split(n, 5, first)
                    halves_out(n, first)

                rows_hi(0, 0, True)
                block_of(0, 0, first=True)
                block_of(1, 1, second=True)
                with act.Fori(1, NE // 2 - 1) as i:
                    block_of(2 * i, 0)
                    block_of(2 * i + 1, 1)
                block_of(NE - 2, 0)
                block_of(NE - 1, 1, last=True)
                hidden_hi(NE - 1)
                y_low(NE - 1)

                def overflow(j):
                    n = j + NE
                    rows_hi(n, 0)
                    for k in range(6):
                        split(n, k)
                    halves_out(n)
                    hidden_hi(n)
                    y_low(n)

                act.wait_ge(tables_in, 32)
                each_overflow(act, overflow)

            @block.vector
            def _(dve):
                V = nc.vector

                def rest(n, k):
                    dve.wait_ge(hi_done, 6 * n + (k + 1))
                    o = (k % 2) * HW
                    V.tensor_tensor(lo[k // 2][:, o:o + HW], raw[k][:], hi[k // 2][:, o:o + HW].bitcast(F32),
                                    ALU.subtract).then_inc(lo_done, 1)

                def rows_lo(n, b):
                    dve.wait_ge(xh_done, n + 1)
                    V.tensor_tensor(xs[:, b, :, low], psX, xs[:, b, :, top].bitcast(F32), ALU.subtract).then_inc(xl_done, 1)

                def sums(n, first=False):
                    dve.wait_ge(g_lo_out, n + 1)
                    if not first:
                        dve.wait_ge(h_mm, n)
                    V.tensor_tensor(g[:], psG[top], g_lo[:], ALU.add).then_inc(g_out, 1)
                    dve.wait_ge(u_lo_out, n + 1)
                    V.tensor_tensor(u[:], psU[top], u_lo[:], ALU.add).then_inc(u_out, 1)

                def hidden(n):
                    dve.wait_ge(silu_out, n + 1)
                    dve.wait_ge(u_out, n + 1)
                    V.tensor_tensor(g[:], g[:], u[:], ALU.mult).then_inc(h_out, 1)

                def hidden_lo(n):
                    dve.wait_ge(hh_done, n + 1)
                    V.tensor_tensor(hs[:, :, low], psH, hs[:, :, top].bitcast(F32), ALU.subtract).then_inc(hl_done, 1)

                def y_sum(n, b, stored):
                    dve.wait_ge(y_lo_out, n + 1)
                    if stored is not None:
                        dve.wait_ge(y_stored[b], stored)
                    V.tensor_tensor(ye[:, b, :], psY[top], y_lo[:], ALU.add).then_inc(y_out, 1)

                def block_of(n, b, first=False, stored=None, last=False):
                    rest(n, 0)
                    if not first:
                        hidden_lo(n + (-1))
                    rest(n, 1)
                    rest(n, 2)
                    rest(n, 3)
                    if not first:
                        y_sum(n + (-1), 1 - b, stored)
                    rest(n, 4)
                    if not last:
                        rows_lo(n + 1, 1 - b)
                    rest(n, 5)
                    sums(n, first)
                    hidden(n)

                dve.wait_ge(tables_in, 32)
                V.tensor_scalar(toks[:], slots[:], 1, None, ALU.arith_shift_right).then_inc(toks_ready, 1)
                rows_lo(0, 0)
                block_of(0, 0, first=True)
                block_of(1, 1)
                block_of(2, 0)
                block_of(3, 1, stored=16)
                with dve.Fori(2, NE // 2 - 1) as i:
                    block_of(2 * i, 0, stored=16 * i + (-16))
                    block_of(2 * i + 1, 1, stored=16 * i)
                block_of(NE - 2, 0, stored=8 * NE - 32)
                block_of(NE - 1, 1, stored=8 * NE - 16, last=True)
                hidden_lo(NE - 1)
                y_sum(NE - 1, 1, 8 * NE - 16)

                def overflow(j):
                    n = j + NE
                    rows_lo(n, 0)
                    for k in range(6):
                        rest(n, k)
                    sums(n)
                    hidden(n)
                    hidden_lo(n)
                    y_sum(n, 0, 16 * j + 8 * NE)

                each_overflow(dve, overflow)


def combine(nc, io, PS, sem, wk):
    with ExitStack() as ctx:
        y2 = ctx.enter_context(nc.sbuf_tensor("f_y2", [P, 5, 2, D], F32))
        x1 = ctx.enter_context(nc.sbuf_tensor("f_x1", [P, 5, D], F32))
        y_in, done, stored = [sem(f"f_y_in{i}") for i in range(5)], sem("f_done"), sem("f_stored")
        rows = [min(P, T - i * P) for i in range(5)]
        with nc.Block() as block:
            @block.sync
            def _(sp):
                for i in range(5):
                    sp.dma_start(x1[0:rows[i], i], io["x1_dram"][0:rows[i], i]).then_inc(y_in[i], 16)
                    sp.dma_start(y2[0:rows[i], i], io["y2_dram"][2 * i * P:2 * (i * P + rows[i]), :].rearrange(
                        "(p k) n -> p k n", k=2)).then_inc(y_in[i], 16)
                for i in range(5):
                    sp.wait_ge(done, 2 * i + 2)
                    sp.dma_start(io["y"][i * P:i * P + rows[i], :], x1[0:rows[i], i, :]).then_inc(stored, 16)
                sp.wait_ge(stored, 80)

            @block.vector
            def _(dve):
                for i in range(5):
                    r = rows[i]
                    dve.wait_ge(y_in[i], 32)
                    for k in range(2):
                        nc.vector.scalar_tensor_tensor(out=x1[0:r, i, :], in0=y2[0:r, i, k, :], scalar=wk[0:r, i, k:k + 1],
                                                       in1=x1[0:r, i, :], op0=ALU.mult, op1=ALU.add).then_inc(done, 1)
                        dve.wait_ge(done, 2 * i + k + 1)


def build(nc, io):
    with ExitStack() as ctx:
        def stage(run, *args):
            own = []

            def sem(name):
                own.append(nc.alloc_semaphore(name))
                return own[-1]

            run(nc, io, PS, sem, *args)
            nc.clear_and_free_semaphores(own)
            nc.all_engine_barrier()

        PS = ctx.enter_context(nc.psum_tensor("PS", [P, 4096], F32))
        cst_t = ctx.enter_context(nc.sbuf_tensor("cst", [P, CONSTS.shape[1]], F32))
        par = ctx.enter_context(nc.sbuf_tensor("par", [P, NPAR], F32))

        class Consts(dict):
            def __missing__(self, name):
                at, width = CONST_AT[name]
                return cst_t[:, at:at + width]

            def __getitem__(self, name):
                return cst_t[:] if isinstance(name, slice) else self.__missing__(name)

        cst = Consts()
        io["par_sb"] = par
        io["P"] = lambda name, c=0, n=1: par[:, PAR_AT[name][0] + c:PAR_AT[name][0] + c + n]
        with nc.sbuf_tensor("z", [P, 14, TP], F32) as z:
            stage(project_inputs, cst, z)
            stage(rwkv, cst, z)
        with ExitStack() as c2:
            kcT_p = c2.enter_context(nc.sbuf_tensor("kcT_p", [P, 2, NKC_P], F32))
            vc_p = c2.enter_context(nc.sbuf_tensor("vc_p", [32, P], F32))
            kcT_s = c2.enter_context(nc.sbuf_tensor("kcT_s", [P, NB, NKC_S], F32))
            vc_s = c2.enter_context(nc.sbuf_tensor("vc_s", [P, NB, P], F32))
            table = c2.enter_context(nc.sbuf_tensor("table", [1, NB * NPAGES], I32))
            stage(compress, cst, table, kcT_p, vc_p, kcT_s, vc_s)
            kv = c2.enter_context(nc.sbuf_tensor("kv", [P, 4, NPAGES, 2, PAGE], F32))
            wkv = c2.enter_context(nc.sbuf_tensor("wkv", [P, 4, 4, 2, P], F32))
            stage(prompt_attention, cst, kcT_p, vc_p, table, kv, wkv)
            stage(sample_attention, cst, kcT_s, vc_s, table, kv, wkv)
        wk = ctx.enter_context(nc.sbuf_tensor("wk", [P, 5, 2], F32))
        with ExitStack() as c3:
            raw = [c3.enter_context(nc.sbuf_tensor(f"raw{k}", [P, HW], F32)) for k in range(6)]
            stage(merge_and_route, cst, wk, raw)
            stage(experts, cst, raw)
        stage(combine, wk)




def chan(v, cols):
    return np.ascontiguousarray(v.reshape(cols, P).T)


def low_rank(v):
    lead = v.shape[:-1]
    o = np.zeros(lead + (14, P), v.dtype)
    o[..., 0:12, :] = v[..., 0:1536].reshape(lead + (12, P))
    o[..., 12, 0:64] = v[..., 1536:1600]
    o[..., 13, 0:96] = v[..., 1600:1696]
    return o


def per_group(w):
    o = np.zeros((2, HD) + w.shape[1:-1] + (2, HD), w.dtype)
    for g in range(2):
        o[g, ..., g, :] = w
    return o.reshape((P,) + w.shape[1:-1] + (P,))


def slab(w):
    return np.ascontiguousarray(w.reshape(KC, P, -1).transpose(1, 0, 2))


def kernel(**inputs):
    import concourse.bacc as _bacc
    from concourse.bass_utils import run_bass_kernel_spmd as _run

    x = {k: np.asarray(v) for k, v in inputs.items()}
    w = {k: (v if k in ("x_prompt", "x_sample", "page_table") else v[0]) for k, v in x.items()}
    nc = _bacc.Bacc("TRN2", target_bir_lowering=False, num_devices=1)
    arrays, io = {}, {}

    def give(name, a):
        a = np.ascontiguousarray(a)
        arrays["in_" + name] = a
        io[name] = nc.dram_tensor("in_" + name, a.shape, mybir.dt.from_np(a.dtype), kind="ExternalInput").ap()

    def take(name, shape):
        io[name] = nc.dram_tensor("out_" + name, shape, F32, kind="ExternalOutput").ap()

    def scratch(name, shape, dt=F32):
        io[name] = nc.dram_tensor("scratch_" + name, shape, dt, kind="Internal").ap()

    tokens = np.concatenate([w["x_prompt"].reshape(TPR, D), w["x_sample"].reshape(TSM, D)], 0)
    give("x", tokens)
    give("xT", slab(tokens.T))
    give("consts", CONSTS)
    par = [low_rank(w["mu_shift"]).T] + [chan(w[k], 4) for k in ("w0", "a0", "k_k", "k_a")]
    par += [chan(w["r_k"].reshape(-1), 4), chan(w["ln_x_w"], 4), chan(w["ln_x_b"], 4), chan(w["norm1"], KC)]
    par += [np.concatenate([w[k]] * 2)[:, None] for k in ("cmp_b1_k", "cmp_b1_v")] + [chan(w["norm2"], KC)]
    give("par", np.concatenate(par, 1))
    give("gains", np.broadcast_to(np.stack([w[k] for k in ("q_norm", "ks_norm", "kw_norm")])[None], (P, 3, HD)))
    wi, cuts = w["w_in"], [(0, 512), (512, 1024), (1024, 1536), (1536, 1696), (1696, 2208), (2208, 2720), (2720, 3000)]
    for i, (a, b) in enumerate(cuts):
        give(f"w_in{i}", slab(wi[:, a:b]))
    io["w_in"] = [io[f"w_in{i}"] for i in range(len(cuts))]
    give("w_lora_up", np.concatenate([w["w_decay_up"], w["w_iclr_up"]], 0))
    give("w_gate_up", w["w_gate_up"])
    give("shift_in", low_rank(w["state_shift"]).transpose(2, 1, 0))
    give("wkv_in", w["state_wkv"].reshape(NB, 4, 2, HD, HD).transpose(2, 4, 1, 0, 3).reshape(P, 4, NB, HD))
    take("kvc", (T, 256))
    take("kvs", (T, 256))
    take("kvw", (T, 256))
    take("shift_out", (P, 14, 1 + NB))
    take("wkv_p", (P, 4, HD))
    take("wkv_s", (P, 4, NB, HD))
    take("y", (T, D))
    take("win_s", (NB, 512, 256))
    give("win_cache", w["cache_win_kv"].reshape(NB, 512, 256))
    scratch("q_dram", (T, 512))
    scratch("gate_dram", (T, 24))
    scratch("oa_dram", (P, 4, T))
    scratch("h_dram", (P, KC, T))
    scratch("ob_dram", (P, 4, T))
    scratch("h2_dram", (T, D))
    scratch("y2_dram", (2 * T, D))
    scratch("slots_dram", (CAP * NBLK, 1), I32)
    scratch("ids_dram", (1, NBLK + 1), I32)
    scratch("x1_dram", (P, 5, D))
    give("page_table", w["page_table"].reshape(1, -1).astype(np.int32))
    pool_c = w["cache_cmp_kv"].reshape(-1, PAGE, 2, P)
    give("cmp_pool", pool_c.transpose(0, 3, 2, 1))
    pool_s = w["cache_slc_kv"].reshape(-1, PAGE, 2, P)
    give("slc_pool", np.stack([pool_s[:, :, 0].transpose(0, 2, 1), pool_s[:, :, 1]], 2))
    win = w["cache_win_kv"].reshape(NB, 4, P, 2, P)
    give("win_kv", np.stack([win[:, :, :, 0].transpose(0, 3, 1, 2), win[:, :, :, 1].transpose(0, 2, 1, 3)], 3))
    give("cmp_w1", per_group(np.stack([w["cmp_w1_k"], w["cmp_w1_v"]]).transpose(2, 0, 1, 3)))
    give("cmp_w2", per_group(np.stack([w["cmp_w2_k"], w["cmp_w2_v"]]).transpose(1, 0, 2)))
    give("cmp_pe", np.concatenate([np.stack([w["cmp_pe_k"], w["cmp_pe_v"]]).transpose(2, 0, 1)] * 2))
    give("kc_gain", np.broadcast_to(w["kc_norm"][None], (P, HD)))
    give("w_gates", wi[:, 3000:5048].reshape(KC, P, 2, KC, P).transpose(2, 3, 1, 0, 4))
    give("w_branch", np.stack([w["w_branch_a"], w["w_branch_b"]]).reshape(2, 4, P, KC, P).transpose(0, 3, 2, 1, 4))
    give("w_out", w["w_out"].reshape(KC, P, 2, D // 2).transpose(2, 1, 0, 3))
    give("norm2_rows", np.broadcast_to(w["norm2"][None], (P, D)))
    give("w_route", slab(np.concatenate([w["w_route_group"], w["w_route_expert"]], 1)))
    give("b_route", np.broadcast_to(np.concatenate([w["b_route_group"], w["b_route_expert"]])[None], (P, 36)))
    for k in ("w_exp_gate", "w_exp_up", "w_exp_down"):
        give(k, w[k])
    build(nc, io)
    got = _run(nc, [arrays], core_ids=[0]).results[0]
    o = {k[4:]: np.asarray(got[k]) for k in got if k.startswith("out_")}

    def rows(a):
        return a[0:TPR].reshape(1, 1, TPR, 2, 2, HD), a[TPR:].reshape(1, NB, TS, 2, 2, HD)

    (cp, cs), (sp, ss), (wp, ws) = rows(o["kvc"]), rows(o["kvs"]), rows(o["kvw"])
    sh = o["shift_out"].transpose(2, 1, 0)
    sh = np.concatenate([sh[:, 0:12].reshape(9, 1536), sh[:, 12, 0:64], sh[:, 13, 0:96]], 1)
    wkv_p = o["wkv_p"].reshape(2, HD, 4, HD).transpose(2, 0, 3, 1).reshape(1, 1, 8, HD, HD)
    wkv_s = o["wkv_s"].reshape(2, HD, 4, NB, HD).transpose(3, 2, 0, 4, 1).reshape(1, NB, 8, HD, HD)
    return (o["y"][0:TPR].reshape(1, TPR, D), o["y"][TPR:].reshape(NB, TS, D), cp, sp, wp, wkv_p, sh[None, 0:1],
            cs, ss, o["win_s"].reshape(1, NB, 512, 2, 2, HD), wkv_s, sh[None, 1:])
```
